# Optimizing a Trainium2 kernel written in Bass

```python
import math
import jax, jax.numpy as jnp
from jax import lax
import numpy as np

D_MODEL = 1024
BATCH = 1
SEQ = 256
DEPTH = 2
DEC_BATCH = 8
DEC_SEQ = 1
PAST_LEN = 2048
PAGE_SIZE = 128

N_A_LAYERS = DEPTH // 2
N_B_LAYERS = DEPTH - N_A_LAYERS
HGRN_HEADS = 8
HGRN_DK = D_MODEL // HGRN_HEADS
HGRN_DV = D_MODEL // HGRN_HEADS
HGRN_CHUNK = 64
MLA_HEADS = 16
QK_NOPE = 64
QK_ROPE = 32
V_DIM = 64
KV_LORA = 256
Q_LORA = 384
ROPE_THETA = 10000.0
MLA_SCALE = (QK_NOPE + QK_ROPE) ** -0.5
Q_BLOCK = 128
PAGES_PER_STEP = 16
PEER_HEADS = 8
PEER_KEY_DIM = 256
N_KEYS = 128
N_EXPERTS = N_KEYS * N_KEYS
PEER_TOPK = 16
PEER_TOKEN_BLOCK = 128
DEEPNORM_ALPHA = (2.0 * DEPTH) ** 0.25
DEEPNORM_BETA = (8.0 * DEPTH) ** -0.25
LN_EPS = 1e-5
RMS_EPS = 1e-6

kernel_name = 'yoco_hgrn2_mla_peer_step'

def _layernorm(x, g, b):
    xf = x.astype(jnp.float32)
    mu = xf.mean(-1, keepdims=True)
    var = jnp.square(xf - mu).mean(-1, keepdims=True)
    return ((xf - mu) * lax.rsqrt(var + LN_EPS) * g + b).astype(x.dtype)

def _rmsnorm(x, g):
    xf = x.astype(jnp.float32)
    return (xf * lax.rsqrt(jnp.mean(xf * xf, -1, keepdims=True) + RMS_EPS) * g).astype(x.dtype)

def _rope(x, pos):
    half = QK_ROPE // 2
    inv = ROPE_THETA ** (-jnp.arange(half, dtype=jnp.float32) / half)
    ang = pos.astype(jnp.float32)[:, None] * inv[None, :]
    shape = (1, ang.shape[0]) + (1,) * (x.ndim - 3) + (half,)
    cos = jnp.cos(ang).reshape(shape)
    sin = jnp.sin(ang).reshape(shape)
    xf = x.astype(jnp.float32)
    x1, x2 = xf[..., :half], xf[..., half:]
    return jnp.concatenate([x1 * cos - x2 * sin, x2 * cos + x1 * sin], axis=-1).astype(x.dtype)

def _gla_chunked(q, k, v, logf, S0):
    B, T, H, _ = q.shape
    DV = v.shape[-1]
    C = min(HGRN_CHUNK, T)
    n = -(-T // C)
    pad = n * C - T

    def prep(a):
        a = jnp.pad(a.astype(jnp.float32), ((0, 0), (0, pad), (0, 0), (0, 0)))
        return a.reshape(B, n, C, H, a.shape[-1]).transpose(1, 0, 3, 2, 4)

    xs = (prep(q), prep(k), prep(v), prep(logf))
    tri = jnp.tril(jnp.ones((C, C), dtype=bool))[None, None, :, :, None]

    def step(S, inp):
        qc, kc, vc, gc = inp
        b = jnp.cumsum(gc, axis=2)
        o_inter = jnp.einsum('bhtd,bhde->bhte', qc * jnp.exp(b), S)
        diff = jnp.where(tri, b[:, :, :, None, :] - b[:, :, None, :, :], -jnp.inf)
        att = jnp.einsum('bhtd,bhsd,bhtsd->bhts', qc, kc, jnp.exp(diff))
        o = o_inter + jnp.einsum('bhts,bhse->bhte', att, vc)
        b_last = b[:, :, -1:, :]
        S_new = jnp.exp(b_last[:, :, 0, :])[..., None] * S + jnp.einsum(
            'bhsd,bhse->bhde', kc * jnp.exp(b_last - b), vc)
        return S_new, o

    S_fin, o = lax.scan(step, S0.astype(jnp.float32), xs)
    o = o.transpose(1, 0, 3, 2, 4).reshape(B, n * C, H, DV)[:, :T]
    return o, S_fin

def _hgrn2_mixer(x, S0, w_in, lb, norm_g, w_out):
    B, T, _ = x.shape
    q, fz, i, g = jnp.split(x @ w_in, 4, axis=-1)
    lbh = lb.reshape(HGRN_HEADS, HGRN_DK)
    fz = fz.reshape(B, T, HGRN_HEADS, HGRN_DK).astype(jnp.float32)
    logf = jnp.log(lbh + (1.0 - lbh) * jax.nn.sigmoid(fz))
    k = (1.0 - lbh) * jax.nn.sigmoid(-fz)
    o, S = _gla_chunked(q.reshape(B, T, HGRN_HEADS, HGRN_DK), k, i.reshape(B, T, HGRN_HEADS, HGRN_DV), logf, S0)
    o = _rmsnorm(o, norm_g).astype(x.dtype) * jax.nn.silu(g.reshape(B, T, HGRN_HEADS, HGRN_DV))
    return o.reshape(B, T, HGRN_HEADS * HGRN_DV) @ w_out, S

def _peer(x, w_q, k1, k2, u, v):
    B, T, D = x.shape
    n = B * T
    blk = min(PEER_TOKEN_BLOCK, n)
    nb = -(-n // blk)
    xp = jnp.pad(x.reshape(n, D), ((0, nb * blk - n), (0, 0))).reshape(nb, blk, D)
    half = PEER_KEY_DIM // 2

    def block(xb):
        q = (xb @ w_q).reshape(blk, PEER_HEADS, PEER_KEY_DIM)
        s1 = jnp.einsum('thd,hnd->thn', q[..., :half], k1).astype(jnp.float32)
        s2 = jnp.einsum('thd,hnd->thn', q[..., half:], k2).astype(jnp.float32)
        v1, i1 = lax.top_k(s1, PEER_TOPK)
        v2, i2 = lax.top_k(s2, PEER_TOPK)
        cand = (v1[..., :, None] + v2[..., None, :]).reshape(blk, PEER_HEADS, PEER_TOPK * PEER_TOPK)
        cidx = (i1[..., :, None] * N_KEYS + i2[..., None, :]).reshape(blk, PEER_HEADS, PEER_TOPK * PEER_TOPK)
        sv, si = lax.top_k(cand, PEER_TOPK)
        e = jnp.take_along_axis(cidx, si, axis=-1)
        gate = jax.nn.softmax(sv, axis=-1)
        act = jax.nn.gelu(jnp.einsum('thkd,td->thk', u[e], xb).astype(jnp.float32), approximate=False)
        return jnp.einsum('thk,thkd->td', (gate * act).astype(x.dtype), v[e])

    y = lax.map(block, xp).reshape(nb * blk, D)[:n]
    return y.reshape(B, T, D)

def _mla_kv(x, pos, w_dkv, kv_norm_g):
    kv = x @ w_dkv
    return _rmsnorm(kv[..., :KV_LORA], kv_norm_g), _rope(kv[..., KV_LORA:], pos)

def _mla_q(x, pos, w_dq, q_norm_g, w_uq, w_uk):
    B, T, _ = x.shape
    q = (_rmsnorm(x @ w_dq, q_norm_g) @ w_uq).reshape(B, T, MLA_HEADS, QK_NOPE + QK_ROPE)
    q_pe = _rope(q[..., QK_NOPE:], pos)
    q_lat = jnp.einsum('bthn,lhn->bthl', q[..., :QK_NOPE], w_uk)
    return q_lat, q_pe

def _mla_scores(q_lat, q_pe, ckv, kpe):
    s = jnp.einsum('bthl,bkl->bhtk', q_lat, ckv, preferred_element_type=jnp.float32)
    s = s + jnp.einsum('bthr,bkr->bhtk', q_pe, kpe, preferred_element_type=jnp.float32)
    return s * MLA_SCALE

def _mla_attend_prompt(q_lat, q_pe, ckv, kpe):
    B, S, H, L = q_lat.shape
    qb = min(Q_BLOCK, S)
    nb = S // qb
    kpos = jnp.arange(S)
    ckv32 = ckv.astype(jnp.float32)
    ql = q_lat.reshape(B, nb, qb, H, L).transpose(1, 0, 2, 3, 4)
    qp = q_pe.reshape(B, nb, qb, H, QK_ROPE).transpose(1, 0, 2, 3, 4)

    def block(inp):
        qlb, qpb, i = inp
        qpos = i * qb + jnp.arange(qb)
        s = jnp.where(kpos[None, :] <= qpos[:, None], _mla_scores(qlb, qpb, ckv, kpe), -jnp.inf)
        p = jax.nn.softmax(s, axis=-1)
        return jnp.einsum('bhtk,bkl->bthl', p, ckv32)

    o = lax.map(block, (ql, qp, jnp.arange(nb)))
    return o.transpose(1, 0, 2, 3, 4).reshape(B, S, H, L).astype(q_lat.dtype)

def _online_update(carry, s, vals):
    m, l, acc = carry
    m_new = jnp.maximum(m, s.max(-1))
    corr = jnp.exp(m - m_new)
    p = jnp.exp(s - m_new[..., None])
    l = l * corr + p.sum(-1)
    acc = acc * corr[..., None] + jnp.einsum('bhtk,bkl->bhtl', p, vals.astype(jnp.float32))
    return m_new, l, acc

def _pages_per_step(n_pages):
    return max(d for d in range(1, PAGES_PER_STEP + 1) if n_pages % d == 0)

def _mla_attend_sample(q_lat, q_pe, ckv_new, kpe_new, cache_ckv, cache_kpe, page_table):
    Bd, T, H, L = q_lat.shape
    n_pages = page_table.shape[1]
    g = _pages_per_step(n_pages)
    pages = page_table.reshape(Bd, n_pages // g, g).transpose(1, 0, 2)
    init = (jnp.full((Bd, H, T), -1e30, jnp.float32),
            jnp.zeros((Bd, H, T), jnp.float32),
            jnp.zeros((Bd, H, T, L), jnp.float32))

    def step(carry, pg):
        ck = cache_ckv[pg].reshape(Bd, g * cache_ckv.shape[1], L)
        kp = cache_kpe[pg].reshape(Bd, g * cache_kpe.shape[1], QK_ROPE)
        return _online_update(carry, _mla_scores(q_lat, q_pe, ck, kp), ck), None

    carry, _ = lax.scan(step, init, pages)
    causal = jnp.tril(jnp.ones((T, T), dtype=bool))
    s_new = jnp.where(causal, _mla_scores(q_lat, q_pe, ckv_new, kpe_new), -jnp.inf)
    m, l, acc = _online_update(carry, s_new, ckv_new)
    return (acc / l[..., None]).transpose(0, 2, 1, 3).astype(q_lat.dtype)

def _mla_out(o_lat, w_uv, w_o):
    B, T, _, _ = o_lat.shape
    o = jnp.einsum('bthl,lhv->bthv', o_lat, w_uv)
    return o.reshape(B, T, MLA_HEADS * V_DIM) @ w_o

def setup_inputs(seed: int = 0) -> dict:
    key = jax.random.key(seed)
    ks = jax.random.split(key, 26)
    f32 = jnp.float32

    def nrm(k, shape, scale=1.0):
        return jax.random.normal(k, shape, f32) * scale

    n_pages = PAST_LEN // PAGE_SIZE
    n_used = DEC_BATCH * n_pages
    n_pool = n_used + -(-n_used // 4)
    page_table = jax.random.permutation(ks[0], n_pool)[:n_used].reshape(DEC_BATCH, n_pages).astype(jnp.int32)

    hd = HGRN_HEADS * HGRN_DK
    col_scale = jnp.concatenate([jnp.ones((2 * hd,), f32), jnp.full((hd,), DEEPNORM_BETA, f32), jnp.ones((hd,), f32)])
    hgrn_w_in = nrm(ks[1], (N_A_LAYERS, D_MODEL, 4 * hd), D_MODEL ** -0.5) * col_scale
    ukv_scale = jnp.concatenate([jnp.ones((QK_NOPE,), f32), jnp.full((V_DIM,), DEEPNORM_BETA, f32)])
    mla_w_ukv = nrm(ks[2], (KV_LORA, MLA_HEADS, QK_NOPE + V_DIM), KV_LORA ** -0.5) * ukv_scale

    return {
        'x_prompt': nrm(ks[3], (BATCH, SEQ, D_MODEL)),
        'x_sample': nrm(ks[4], (DEC_BATCH, DEC_SEQ, D_MODEL)),
        'state_hgrn': nrm(ks[5], (N_A_LAYERS, DEC_BATCH, HGRN_HEADS, HGRN_DK, HGRN_DV), 0.5),
        'cache_ckv': nrm(ks[6], (n_pool, PAGE_SIZE, KV_LORA)),
        'cache_kpe': nrm(ks[7], (n_pool, PAGE_SIZE, QK_ROPE)),
        'page_table': page_table,
        'hgrn_w_in': hgrn_w_in,
        'hgrn_lb_logits': nrm(ks[8], (N_A_LAYERS + 1, hd), 0.5),
        'hgrn_norm_g': 1.0 + nrm(ks[9], (N_A_LAYERS, HGRN_HEADS, HGRN_DV), 0.02),
        'hgrn_w_out': nrm(ks[10], (N_A_LAYERS, HGRN_HEADS * HGRN_DV, D_MODEL), (HGRN_HEADS * HGRN_DV) ** -0.5 * DEEPNORM_BETA),
        'mla_w_dkv': nrm(ks[11], (D_MODEL, KV_LORA + QK_ROPE), D_MODEL ** -0.5),
        'mla_kv_norm_g': 1.0 + nrm(ks[12], (KV_LORA,), 0.02),
        'mla_w_ukv': mla_w_ukv,
        'mla_w_dq': nrm(ks[13], (N_B_LAYERS, D_MODEL, Q_LORA), D_MODEL ** -0.5),
        'mla_q_norm_g': 1.0 + nrm(ks[14], (N_B_LAYERS, Q_LORA), 0.02),
        'mla_w_uq': nrm(ks[15], (N_B_LAYERS, Q_LORA, MLA_HEADS * (QK_NOPE + QK_ROPE)), Q_LORA ** -0.5),
        'mla_w_o': nrm(ks[16], (N_B_LAYERS, MLA_HEADS * V_DIM, D_MODEL), (MLA_HEADS * V_DIM) ** -0.5 * DEEPNORM_BETA),
        'peer_w_q': nrm(ks[17], (DEPTH, D_MODEL, PEER_HEADS * PEER_KEY_DIM), D_MODEL ** -0.5),
        'peer_k1': nrm(ks[18], (DEPTH, PEER_HEADS, N_KEYS, PEER_KEY_DIM // 2), (PEER_KEY_DIM // 2) ** -0.5),
        'peer_k2': nrm(ks[19], (DEPTH, PEER_HEADS, N_KEYS, PEER_KEY_DIM // 2), (PEER_KEY_DIM // 2) ** -0.5),
        'peer_u': nrm(ks[20], (DEPTH, N_EXPERTS, D_MODEL), D_MODEL ** -0.5 * DEEPNORM_BETA),
        'peer_v': nrm(ks[21], (DEPTH, N_EXPERTS, D_MODEL), DEEPNORM_BETA),
        'ln_g': 1.0 + nrm(ks[22], (DEPTH, 2, D_MODEL), 0.02),
        'ln_b': nrm(ks[23], (DEPTH, 2, D_MODEL), 0.02),
    }

def reference(x_prompt, x_sample, state_hgrn, cache_ckv, cache_kpe, page_table,
              hgrn_w_in, hgrn_lb_logits, hgrn_norm_g, hgrn_w_out,
              mla_w_dkv, mla_kv_norm_g, mla_w_ukv,
              mla_w_dq, mla_q_norm_g, mla_w_uq, mla_w_o,
              peer_w_q, peer_k1, peer_k2, peer_u, peer_v,
              ln_g, ln_b):
    lower_bounds = jnp.cumsum(jax.nn.softmax(hgrn_lb_logits.astype(jnp.float32), axis=0), axis=0)
    w_uk = mla_w_ukv[..., :QK_NOPE]
    w_uv = mla_w_ukv[..., QK_NOPE:]

    def trunk(x, pos, hgrn_init, attend):
        new_states = []
        ckv = None
        kpe = None
        for l in range(DEPTH):
            if l < N_A_LAYERS:
                h, S = _hgrn2_mixer(x, hgrn_init(l), hgrn_w_in[l], lower_bounds[l], hgrn_norm_g[l], hgrn_w_out[l])
                new_states.append(S)
            else:
                j = l - N_A_LAYERS
                if j == 0:
                    ckv, kpe = _mla_kv(x, pos, mla_w_dkv, mla_kv_norm_g)
                q_lat, q_pe = _mla_q(x, pos, mla_w_dq[j], mla_q_norm_g[j], mla_w_uq[j], w_uk)
                h = _mla_out(attend(q_lat, q_pe, ckv, kpe), w_uv, mla_w_o[j])
            x = _layernorm(DEEPNORM_ALPHA * x + h, ln_g[l, 0], ln_b[l, 0])
            f = _peer(x, peer_w_q[l], peer_k1[l], peer_k2[l], peer_u[l], peer_v[l])
            x = _layernorm(DEEPNORM_ALPHA * x + f, ln_g[l, 1], ln_b[l, 1])
        return x, jnp.stack(new_states), ckv, kpe

    pos_p = jnp.arange(x_prompt.shape[1])
    y_prompt, st_p, ckv_p, kpe_p = trunk(
        x_prompt, pos_p,
        lambda l: jnp.zeros((x_prompt.shape[0], HGRN_HEADS, HGRN_DK, HGRN_DV), jnp.float32),
        _mla_attend_prompt)

    pos_s = PAST_LEN + jnp.arange(x_sample.shape[1])
    y_sample, st_s, ckv_s, kpe_s = trunk(
        x_sample, pos_s,
        lambda l: state_hgrn[l],
        lambda ql, qp, ck, kp: _mla_attend_sample(ql, qp, ck, kp, cache_ckv, cache_kpe, page_table))

    return (y_prompt, y_sample, st_p, st_s, ckv_p, kpe_p, ckv_s, kpe_s)


_drawn_inputs = setup_inputs


def setup_inputs(seed=0):
    import zlib

    import numpy as np

    out = dict(_drawn_inputs(seed))
    spreads = {}
    factors = {'cache_ckv': 8.0,
     'cache_kpe': 8.0,
     'hgrn_norm_g': 5.833,
     'mla_kv_norm_g': 2.965,
     'mla_q_norm_g': 8.0}
    for name, (base, spread) in spreads.items():
        noise = np.random.default_rng([zlib.crc32(name.encode()), seed]).standard_normal(out[name].shape)
        drawn = base * np.exp(spread * noise) if base else spread * noise
        out[name] = __import__('jax').numpy.asarray(drawn.astype(out[name].dtype))
    for name, factor in factors.items():
        out[name] = (out[name] * factor).astype(out[name].dtype)
    return out
```

```python
from contextlib import ExitStack

import concourse.bass as bass
from concourse import mybir

F32 = mybir.dt.float32
I32 = mybir.dt.int32
U32 = mybir.dt.uint32
ALU = mybir.AluOpType
ACT = mybir.ActivationFunctionType
AX = mybir.AxisListType.X

P = 128
D = 1024
KO = D // P
NS = 8
NT = 2 * P + NS
TILES = ((0, P), (P, P), (2 * P, NS))
HH = 8
NLEV = 7
TOPK = 16
NKEYS = 128
NEXP = NKEYS * NKEYS
MH = 16
NOPE, ROPE, VD = 64, 32, 64
QD = NOPE + ROPE
LORA, QLORA = 256, 384
SCALE = float(QD) ** -0.5
HG = 4
NG = MH // HG
PAGES = 16
PAGE = 128
RING = 8
ALPHA = 4.0 ** 0.25
LN_EPS, RMS_EPS = 1e-5, 1e-6
NEG = -1e30
SCRATCH = 9216

C_ID, C_AID, C_CAUSAL, C_EYE8, C_BLK, C_IOTA, C_KEYM, C_BLKT, C_ROPE, C_EPS, C_ONE, C_SEL = (
    0, 128, 256, 384, 448, 456, 472, 480, 608, 704, 706, 834)
C_W = C_SEL + 16


def shape_constants(np):
    c = np.zeros((P, C_W), np.float32)
    p = np.arange(P)
    c[p, C_ID + p] = 1.0
    c[p, C_AID + p] = ALPHA
    c[:, C_CAUSAL:C_CAUSAL + P] = np.where(p[None, :] <= p[:, None], 0.0, NEG)
    c[:, C_EYE8:C_EYE8 + 64] = np.eye(NS, dtype=np.float32).reshape(1, 64)
    c[:, C_BLK:C_BLK + NS] = p[:, None] // TOPK == np.arange(NS)[None, :]
    c[:, C_IOTA:C_IOTA + TOPK] = np.arange(TOPK)[None, :]
    c[:NS, C_KEYM:C_KEYM + NS] = np.where(np.eye(NS) > 0, 0.0, NEG)
    c[:NS, C_BLKT:C_BLKT + P] = p[None, :] // TOPK == np.arange(NS)[:, None]
    inv = np.float32(10000.0) ** (-np.arange(ROPE // 2, dtype=np.float32) / np.float32(ROPE // 2))
    for t in range(3):
        pos = (p + P * t) if t < 2 else np.full(P, PAGES * PAGE)
        ang = pos.astype(np.float32)[:, None] * inv[None, :].astype(np.float32)
        c[:, C_ROPE + 32 * t:C_ROPE + 32 * t + 16] = np.cos(ang)
        c[:, C_ROPE + 32 * t + 16:C_ROPE + 32 * t + 32] = np.sin(ang)
    c[:, C_EPS] = LN_EPS
    c[:, C_EPS + 1] = RMS_EPS
    c[:, C_ONE:C_ONE + P] = 1.0
    c[:, C_SEL:C_SEL + TOPK] = p[:, None] % TOPK == np.arange(TOPK)[None, :]
    lev = np.zeros((P, NLEV, P), np.int32)
    x = p[:, None] ^ p[None, :]
    for l in range(NLEV):
        lev[:, l] = (p[:, None] < p[None, :]) & (x >= 1 << l) & (x < 2 << l)
    return c, lev.reshape(P, NLEV * P)


def bc(ap, axis, n):
    ap = ap.unsqueeze(axis)
    shape = list(ap.shape)
    shape[axis] = n
    return ap.broadcast_to(shape)


def trunk_kernel(nc, consts, level_masks, x_prompt, x_sample, state_hgrn, cache_ckv, cache_kpe, page_table,
                 hgrn_w_in, hgrn_lb_logits, hgrn_norm_g, hgrn_w_out,
                 mla_w_dkv, mla_kv_norm_g, mla_w_ukv, mla_w_dq, mla_q_norm_g, mla_w_uq, mla_w_o,
                 peer_w_q, peer_k1, peer_k2, peer_u, peer_v, ln_g, ln_b,
                 y_prompt, y_sample, st_prompt, st_sample, ckv_prompt, kpe_prompt, ckv_sample, kpe_sample):
    with ExitStack() as ctx:
        def sb(name, shape, dt=F32):
            return ctx.enter_context(nc.sbuf_tensor(name, shape, dt))

        def sem(name):
            return ctx.enter_context(nc.semaphore(name))

        cst = sb("cst", [P, C_W])
        ident = cst[:, C_ID:C_ID + P]
        aident = cst[:, C_AID:C_AID + P]
        causal = cst[:, C_CAUSAL:C_CAUSAL + P]
        eye8 = cst[:, C_EYE8:C_EYE8 + 64].rearrange("p (b c) -> p b c", b=NS)
        blk = cst[:, C_BLK:C_BLK + NS]
        iota = cst[:, C_IOTA:C_IOTA + TOPK]
        ones = cst[:, C_ONE:C_ONE + P]
        x = sb("x", [P, 3, D])
        xT = sb("xT", [P, KO, NT])
        o_all = sb("o_all", [P, 3, D])
        g_all = sb("g_all", [P, 3, D])
        wbig = sb("wbig", [P, KO, D])
        lnw = sb("lnw", [P, 2, D])
        stats = sb("stats", [P, 2, 6])
        mv = sb("mv", [P, 2])
        std = sb("std", [P, MH])
        rstd = sb("rstd", [P, MH])
        arena = sb("arena", [P, 16384])

        bank = [ctx.enter_context(nc.psum_tensor(f"bank{i}", [P, 512], F32)) for i in range(8)]

        consts_in = sem("consts_in")
        x_in = sem("x_in")
        x_ready = sem("x_ready")
        turn_ready = sem("turn_ready")
        turn_taken = sem("turn_taken")
        y_ready = sem("y_ready")
        y_free = sem("y_free")
        stat_ready = sem("stat_ready")
        std_ready = sem("std_ready")
        lnw_in = sem("lnw_in")
        wbig_in = sem("wbig_in")
        passed = {e: sem(f"{e}_passed") for e in ("pe", "act", "dve", "pool", "sp")}
        stored = sem("stored")

        def ybank(t, c, nt):
            return bank[2 * t + c][0:nt, :]

        def after(eng, name, s, value):
            eng.wait_ge(s, value)
            eng.sem_inc(passed[name], 1)

        A = arena
        def view(off, shape):
            n = 1
            for s in shape:
                n *= s
            v = A[:, off:off + n]
            if len(shape) == 2:
                v = v.rearrange("p (a b) -> p a b", a=shape[0])
            elif len(shape) == 3:
                v = v.rearrange("p (a b c) -> p a b c", a=shape[0], b=shape[1])
            return v, off + n

        off = 0
        wh, sin, snew, kk, qq, iT, gT, stf = [], [], [], [], [], [], [], []
        for j in range(2):
            v, off = view(off, [KO, 4, P]); wh.append(v)
        for j in range(2):
            v, off = view(off, [NS, P]); sin.append(v)
            v, off = view(off, [NS, P]); snew.append(v)
        for j in range(2):
            for lst in (kk, qq, iT, gT):
                v, off = view(off, [NT]); lst.append(v)
            v, off = view(off, [P]); stf.append(v)
        ksg, off = view(off, [NT])
        sgp, off = view(off, [NT])
        lf, off = view(off, [NT])
        assert off <= 16384, off
        WB = wbig[:, :, :].rearrange("p k n -> p (k n)")
        scratch = sb("scratch", [P, SCRATCH])
        soff = [0]

        def sview(n, dt=None):
            v = scratch[:, soff[0]:soff[0] + n]
            soff[0] += n
            assert soff[0] <= SCRATCH
            return v.bitcast(dt) if dt else v

        bb = sview(2 * P)
        lev = sview(NLEV * 2 * P).rearrange("p (l t) -> p l t", l=NLEV)
        lmask = sview(NLEV * P, I32).rearrange("p (l t) -> p l t", l=NLEV)
        kdec = sview(2 * P)
        kd = sview(2 * P)
        qe = [sview(P) for j in range(2)]
        eb = sview(P)
        glast = [sview(1) for j in range(2)]
        ffs = [sview(NS) for j in range(2)]
        tr = sview(4 * P).rearrange("p (a s) -> p a s", a=4)
        ts_ = sview(2 * P).rearrange("p (a s) -> p a s", a=2)[0:NS]
        vm = sview(NS * P).rearrange("p (a s) -> p a s", a=NS)[0:NS]
        qm = [sview(NS * NS).rearrange("p (a s) -> p a s", a=NS) for j in range(2)]
        att = sview(2 * P).rearrange("p (a s) -> p a s", a=2)
        st0 = sview(P)
        lbl = sb("lbl", [2 * HH, P])
        lbe = sb("lbe", [P, 2, HH])
        lbs = sb("lbs", [P, HH])
        lb = sb("lb", [P, HH])
        omlb = sb("omlb", [P, HH])

        wh_in = [sem(f"wh_in{j}") for j in range(2)]
        sin_in = [sem(f"sin_in{j}") for j in range(2)]
        lb_in = sem("lb_in")
        lbT_ready = sem("lbT_ready")
        lb_max = sem("lb_max")
        lb_exp = sem("lb_exp")
        omlb_ready = sem("omlb_ready")
        proj_ready = sem("proj_ready")
        proj_taken = sem("proj_taken")
        f_ready = sem("f_ready")
        lf_ready = sem("lf_ready")
        b_ready = sem("b_ready")
        lev_ready = sem("lev_ready")
        e_ready = sem("e_ready")
        xlev_ready = sem("xlev_ready")
        tr_ready = sem("tr_ready")
        tr_taken = sem("tr_taken")
        vm_ready = sem("vm_ready")
        att_ready = sem("att_ready")
        s0_ready = sem("s0_ready")
        st0_ready = sem("st0_ready")
        outer_ready = sem("outer_ready")
        fs_ready = sem("fs_ready")
        snew_ready = sem("snew_ready")
        o_ready = sem("o_ready")
        o_taken = sem("o_taken")
        sp_ready = sem("sp_ready")
        st_out = [sem(f"st_out{j}") for j in range(2)]
        hnorm_in = sem("hnorm_in")
        hss_ready = sem("hss_ready")
        hstd_ready = sem("hstd_ready")
        silu_ready = sem("silu_ready")

        w_in_v = hgrn_w_in[0].rearrange("(ko ki) (c h n) -> ki ko c h n", ki=P, c=4, h=HH)
        s_in_v = state_hgrn[0].rearrange("b h k v -> h k b v")
        s_out_v = st_sample[0].rearrange("b h k v -> h k b v")

        def head_pairs(body):
            def run(eng):
                with eng.Fori(0, HH // 2 - 1) as i:
                    for j in range(2):
                        body(i, j, False)
                for j in range(2):
                    body(HH // 2 - 1, j, True)
            return run

        def sp_hgrn(sp):
            sp.dma_start(cst[:, :], consts).then_inc(consts_in, 16)
            sp.dma_start(lmask[:, :, :].rearrange("p a b -> p (a b)"), level_masks).then_inc(consts_in, 16)
            sp.dma_start(x[:, 0, :], x_prompt[0, 0:P, :]).then_inc(x_in, 16)
            sp.dma_start(x[:, 1, :], x_prompt[0, P:2 * P, :]).then_inc(x_in, 16)
            sp.dma_start(x[0:NS, 2, :], x_sample.rearrange("b t d -> (b t) d")).then_inc(x_in, 16)
            sp.dma_start(lbl[:, :], hgrn_lb_logits.rearrange("r (h k) -> (r h) k", h=HH)).then_inc(lb_in, 16)

            def load_head(h, j):
                for c in range(4):
                    sp.dma_start(wh[j][:, :, c, :], w_in_v[:, :, c, h, :]).then_inc(wh_in[j], 16)
                sp.dma_start(sin[j], s_in_v[h]).then_inc(sin_in[j], 16)
            load_head(0, 0)
            load_head(1, 1)
            sp.dma_start(lnw[:, 1, :], hgrn_norm_g.rearrange("l h v -> l (h v)").broadcast_to([P, D])).then_inc(hnorm_in, 16)
            sp.dma_start(wbig[:, :, :], hgrn_w_out[0].rearrange("(k p) n -> p k n", p=P)).then_inc(wbig_in, 16)

            def body(i, j, last):
                n = 2 * i + j
                if not last:
                    after(sp, "sp", proj_ready, 4 * n + 4)
                    after(sp, "sp", fs_ready, n + 1)
                    load_head(n + 2, j)
                after(sp, "sp", snew_ready, n + 1)
                sp.dma_start(s_out_v[n], snew[j]).then_inc(st_out[j], 16)
                after(sp, "sp", sp_ready, n + 1)
                sp.dma_start(st_prompt[0, 0, n], stf[j]).then_inc(st_out[j], 16)
            head_pairs(body)(sp)

        def pe_hgrn(pe):
            pe.wait_ge(consts_in, 32)
            pe.wait_ge(lb_in, 16)
            pe.transpose(bank[2][:, 0:2 * HH], lbl[:, :], cst[0:2 * HH, C_ID:C_ID + 2 * HH]).then_inc(lbT_ready, 1)

            def project(i, j, nxt):
                n = 2 * i + j
                after(pe, "pe", wh_in[j], 64 * (i + 1))
                for g, c in enumerate((1, 0, 2, 3)):
                    if not (nxt == "first" and g < 2):
                        after(pe, "pe", proj_taken, 4 * n + g - 1)
                    for k in range(KO):
                        mm = pe.matmul(bank[g % 2][:, 0:NT], wh[j][:, k, c, :], xT[:, k, :],
                                       start=(k == 0), stop=(k == KO - 1))
                    mm.then_inc(proj_ready, 1)

            pe_turn(pe, 0)
            pe.wait_ge(turn_taken, 6)
            project(0, 0, "first")

            def body(i, j, last):
                n = 2 * i + j
                after(pe, "pe", proj_taken, 4 * n + 4)
                after(pe, "pe", xlev_ready, n + 1)
                after(pe, "pe", o_taken, n + 1)
                after(pe, "pe", sp_taken, n + 1)
                after(pe, "pe", snew_taken, n + 1)
                for t in range(2):
                    pe.transpose(bank[2][:, t * P:(t + 1) * P], iT[j][:, t * P:(t + 1) * P], ident)
                    pe.transpose(bank[2][:, (2 + t) * P:(3 + t) * P], kd[:, t * P:(t + 1) * P], ident)
                pe.transpose(bank[3][0:NS, 0:P], kk[j][:, 2 * P:NT], ident)
                pe.transpose(bank[3][0:NS, P:2 * P], iT[j][:, 2 * P:NT], ident)
                pe.transpose(bank[3][0:NS, 2 * P:3 * P], gT[j][:, 2 * P:NT], ident)
                pe.transpose(bank[3][:, 3 * P:4 * P], gT[j][:, 0:P], ident).then_inc(tr_ready, 1)
                for l in range(NLEV + 1):
                    for t in range(2):
                        cols = slice(t * P, (t + 1) * P)
                        left = kk[j][:, cols] if l == 0 else lev[:, l - 1, cols]
                        right = qq[j][:, cols] if l == 0 else lev[:, l - 1, cols]
                        mm = pe.matmul(bank[4 + l // 2][:, (l % 2) * 256 + t * P:(l % 2) * 256 + (t + 1) * P],
                                       left, right, start=True, stop=True)
                mm.then_inc(att_ready, 1)
                if j == 0:
                    project(i, 1, "")
                elif not last:
                    project(i + 1, 0, "")
                after(pe, "pe", tr_taken, n + 1)
                pe.matmul(bank[2][:, 0:P], tr[:, 2, :], tr[:, 0, :], start=True, stop=True)
                pe.matmul(bank[2][:, P:2 * P], tr[:, 3, :], tr[:, 1, :], start=True, stop=True).then_inc(s0_ready, 1)
                after(pe, "pe", vm_ready, n + 1)
                for c in range(2):
                    mm = pe.matmul(bank[4 + c][:, :], ts_[:, 0, :], vm[:, 4 * c:4 * c + 4, :],
                                   start=True, stop=True)
                mm.then_inc(outer_ready, 1)
                pe.transpose(bank[3][:, 0:P], gT[j][:, P:2 * P], ident)
                pe.matmul(bank[6][:, 0:P], att[:, 0, :], tr[:, 0, :], start=True, stop=True)
                after(pe, "pe", st0_ready, n + 1)
                pe.matmul(bank[6][:, P:2 * P], att[:, 1, :], tr[:, 1, :], start=True, stop=False)
                pe.matmul(bank[6][:, P:2 * P], qe[j], st0[:, :], start=False, stop=True)
                after(pe, "pe", snew_taken, n + 2)
                for b in range(NS):
                    mm = pe.matmul(bank[3][0:NS, P:2 * P], qm[j][:, b, :], snew[j][:, b, :],
                                   start=(b == 0), stop=(b == NS - 1))
                mm.then_inc(o_ready, 1)
            head_pairs(body)(pe)

        snew_taken = sem("snew_taken")
        sp_taken = sem("sp_taken")

        def act_hgrn(act):
            act.wait_ge(lb_max, 1)
            act.activation(lbe[:, :, :], lbe[:, :, :], ACT.Exp).then_inc(lb_exp, 1)
            act_turn(act, 0)
            act.sem_inc(o_taken, 1)

            def gates(i, j, first):
                n = 2 * i + j
                after(act, "act", proj_ready, 4 * n + 1)
                act.activation(ksg, bank[0][:, 0:NT], ACT.Sigmoid, scale=-1.0)
                act.activation(sgp, bank[0][:, 0:NT], ACT.Sigmoid).then_inc(proj_taken, 1)
                act.drain()
                act.activation(lf, sgp, ACT.Ln, scale=omlb[:, bass.ds(n, 1)], bias=lb[:, bass.ds(n, 1)]).then_inc(lf_ready, 1)
                for g, dst in ((1, qq[j]), (2, iT[j])):
                    after(act, "act", proj_ready, 4 * n + g + 1)
                    act.activation(dst, bank[g % 2][:, 0:NT], ACT.Copy).then_inc(proj_taken, 1)
                after(act, "act", b_ready, n + 1)
                act.activation(eb[:, :], bb[:, P:2 * P], ACT.Exp)
                act.activation(glast[j], bb[:, 2 * P - 1:2 * P], ACT.Exp)
                for t in range(2):
                    act.activation(kdec[:, t * P:(t + 1) * P], bb[:, t * P:(t + 1) * P], ACT.Exp,
                                   scale=-1.0, bias=bb[:, (t + 1) * P - 1:(t + 1) * P])
                after(act, "act", lev_ready, n + 1)
                act.activation(lev[:, :, :], lev[:, :, :], ACT.Exp).then_inc(e_ready, 1)
                after(act, "act", proj_ready, 4 * n + 4)
                act.activation(gT[j], bank[1][:, 0:NT], ACT.Copy).then_inc(proj_taken, 1)
            act.wait_ge(omlb_ready, 1)
            gates(0, 0, True)

            def body(i, j, last):
                n = 2 * i + j
                after(act, "act", tr_ready, n + 1)
                act.activation(tr[:, :, :].rearrange("p a b -> p (a b)"), bank[2][:, :], ACT.Copy)
                act.activation(ts_[:, :, :].rearrange("p a b -> p (a b)"), bank[3][0:NS, 0:2 * P], ACT.Copy)
                act.activation(g_all[0:NS, 2, bass.ts(n, P)], bank[3][0:NS, 2 * P:3 * P], ACT.Copy)
                act.activation(g_all[:, 0, bass.ts(n, P)], bank[3][:, 3 * P:4 * P], ACT.Copy).then_inc(tr_taken, 1)
                if j == 0:
                    gates(i, 1, False)
                elif not last:
                    gates(i + 1, 0, False)
                after(act, "act", s0_ready, n + 1)
                act.activation(st0[:, :], bank[2][:, 0:P], ACT.Copy).then_inc(st0_ready, 1)
                after(act, "act", o_ready, n + 1)
                act.activation(o_all[:, 0, bass.ts(n, P)], bank[6][:, 0:P], ACT.Copy)
                act.activation(o_all[:, 1, bass.ts(n, P)], bank[6][:, P:2 * P], ACT.Copy)
                act.activation(g_all[:, 1, bass.ts(n, P)], bank[3][:, 0:P], ACT.Copy)
                act.activation(o_all[0:NS, 2, bass.ts(n, P)], bank[3][0:NS, P:2 * P], ACT.Copy).then_inc(o_taken, 1)
            head_pairs(body)(act)
            act.drain()
            for t, (t0, nt) in enumerate(TILES):
                act.activation(g_all[0:nt, t, :], g_all[0:nt, t, :], ACT.Silu).then_inc(silu_ready, 1)
            for t, (t0, nt) in enumerate(TILES):
                act.wait_ge(hss_ready, t + 1)
                act.activation(std[0:nt, 0:HH], std[0:nt, 0:HH], ACT.Sqrt, scale=1.0 / P,
                               bias=cst[0:nt, C_EPS + 1:C_EPS + 2]).then_inc(hstd_ready, 1)

        def pool_hgrn(pool):
            def body(i, j, last):
                n = 2 * i + j
                after(pool, "pool", b_ready, n + 1)
                for l in range(1, NLEV + 1):
                    half = 1 << (l - 1)
                    b4 = bb[:, :].rearrange("p (n two s) -> p n two s", two=2, s=half)
                    d4 = lev[:, l - 1, :].rearrange("p (n two s) -> p n two s", two=2, s=half)
                    ref = b4[:, :, 0, half - 1]
                    ref = bc(ref, 2, half)
                    pool.tensor_tensor(d4[:, :, 0, :], ref, b4[:, :, 0, :], ALU.subtract)
                    ins = pool.tensor_tensor(d4[:, :, 1, :], b4[:, :, 1, :], ref, ALU.subtract)
                pool.drain()
                ins = pool.sem_inc(lev_ready, 1)
                after(pool, "pool", sin_in[j], 16 * (i + 1))
                after(pool, "pool", st_slot[j], 32 * (i + 1))
                pool.tensor_tensor(snew[j], sin[j], bc(ffs[j], 2, P), ALU.mult).then_inc(fs_ready, 1)
            head_pairs(body)(pool)

        st_slot = st_out

        def dve_hgrn(dve):
            dve.wait_ge(lbT_ready, 1)
            dve.tensor_copy(lbe[:, :, :], bank[2][:, 0:2 * HH].rearrange("p (r h) -> p r h", r=2))
            dve.drain()
            dve.tensor_tensor(lbs[:, :], lbe[:, 0, :], lbe[:, 1, :], ALU.max)
            dve.drain()
            dve.tensor_tensor(lbe[:, :, :], lbe[:, :, :], bc(lbs[:, :], 1, 2), ALU.subtract).then_inc(lb_max, 1)
            dve.wait_ge(lb_exp, 1)
            dve.tensor_tensor(lbs[:, :], lbe[:, 0, :], lbe[:, 1, :], ALU.add)
            dve.drain()
            dve.reciprocal(lbs[:, :], lbs[:, :])
            dve.drain()
            dve.tensor_tensor(lb[:, :], lbe[:, 0, :], lbs[:, :], ALU.mult)
            dve.drain()
            dve.tensor_scalar(omlb[:, :], lb[:, :], -1.0, 1.0, ALU.mult, ALU.add).then_inc(omlb_ready, 1)
            dve.drain()
            dve.sem_inc(snew_taken, 1)
            dve.sem_inc(sp_taken, 1)

            def gates(i, j):
                n = 2 * i + j
                after(dve, "dve", proj_taken, 4 * n + 1)
                dve.tensor_scalar(kk[j], ksg, omlb[:, bass.ds(n, 1)], None, ALU.mult)
                dve.tensor_scalar(ffs[j], sgp[:, 2 * P:NT], omlb[:, bass.ds(n, 1)], lb[:, bass.ds(n, 1)],
                                  ALU.mult, ALU.add).then_inc(f_ready, 1)
                after(dve, "dve", lf_ready, n + 1)
                for t in range(2):
                    ins = dve.tensor_tensor_scan(bb[:, t * P:(t + 1) * P], ones, lf[:, t * P:(t + 1) * P], 0.0,
                                                 ALU.mult, ALU.add)
                dve.drain()
                dve.sem_inc(b_ready, 1)
                after(dve, "dve", proj_taken, 4 * n + 2)
                after(dve, "dve", e_ready, n + 1)
                for l in range(1, NLEV + 1):
                    half = 1 << (l - 1)
                    e4 = lev[:, l - 1, :].rearrange("p (n two s) -> p n two s", two=2, s=half)
                    k4 = kk[j][:, 0:2 * P].rearrange("p (n two s) -> p n two s", two=2, s=half)
                    q4 = qq[j][:, 0:2 * P].rearrange("p (n two s) -> p n two s", two=2, s=half)
                    dve.tensor_tensor(e4[:, :, 0, :], e4[:, :, 0, :], k4[:, :, 0, :], ALU.mult)
                    dve.tensor_tensor(e4[:, :, 1, :], e4[:, :, 1, :], q4[:, :, 1, :], ALU.mult)
                dve.tensor_tensor(qm[j], bc(qq[j][:, 2 * P:NT], 1, NS), eye8, ALU.mult)
                dve.tensor_tensor(qe[j], qq[j][:, P:2 * P], eb[:, :], ALU.mult)
                dve.tensor_tensor(kd[:, :], kk[j][:, 0:2 * P], kdec[:, :], ALU.mult)
                dve.drain()
                dve.sem_inc(xlev_ready, 1)
            gates(0, 0)

            def body(i, j, last):
                n = 2 * i + j
                after(dve, "dve", att_ready, n + 1)
                dve.tensor_tensor(att[:, :, :], bank[4][:, 0:256].rearrange("p (t s) -> p t s", t=2),
                                  bc(ident, 1, 2), ALU.mult)
                for l in range(1, NLEV + 1):
                    dve.drain()
                    for t in range(2):
                        dve.copy_predicated(att[:, t, :], lmask[:, l - 1, :],
                                            bank[4 + l // 2][:, (l % 2) * 256 + t * P:(l % 2) * 256 + (t + 1) * P])
                after(dve, "dve", tr_taken, n + 1)
                dve.tensor_tensor(vm[:, :, :], bc(ts_[:, 1, :], 1, NS), bc(ident[0:NS, 0:NS], 2, P),
                                  ALU.mult)
                dve.drain()
                dve.sem_inc(vm_ready, 1)
                if j == 0:
                    gates(i, 1)
                elif not last:
                    gates(i + 1, 0)
                after(dve, "dve", outer_ready, n + 1)
                after(dve, "dve", fs_ready, n + 1)
                for c in range(2):
                    dve.tensor_tensor(snew[j][:, 4 * c:4 * c + 4, :], snew[j][:, 4 * c:4 * c + 4, :],
                                      bank[4 + c][:, :].rearrange("p (b v) -> p b v", b=4), ALU.add)
                dve.drain()
                dve.sem_inc(snew_ready, 1)
                dve.sem_inc(snew_taken, 1)
                after(dve, "dve", st0_ready, n + 1)
                after(dve, "dve", st_slot[j], 32 * (i + 1))
                dve.scalar_tensor_tensor(stf[j], st0[:, :], glast[j], bank[2][:, P:2 * P],
                                         ALU.mult, ALU.add)
                dve.drain()
                dve.sem_inc(sp_ready, 1)
                dve.sem_inc(sp_taken, 1)
            head_pairs(body)(dve)
            dve.wait_ge(o_taken, HH + 1)
            dve.wait_ge(hnorm_in, 16)
            sq = arena[:, 0:D]
            for t, (t0, nt) in enumerate(TILES):
                o = o_all[0:nt, t, :]
                o3 = o.rearrange("p (h v) -> p h v", h=HH)
                dve.tensor_tensor(sq[0:nt, :], o, o, ALU.mult)
                dve.drain()
                dve.tensor_reduce(std[0:nt, 0:HH], sq[0:nt, :].rearrange("p (h v) -> p h v", h=HH), AX,
                                  ALU.add).then_inc(hss_ready, 1)
                dve.tensor_tensor(o, o, lnw[0:nt, 1, :], ALU.mult)
                dve.wait_ge(hstd_ready, t + 1)
                dve.reciprocal(rstd[0:nt, 0:HH], std[0:nt, 0:HH])
                dve.drain()
                dve.tensor_tensor(o3, o3, bc(rstd[0:nt, 0:HH], 2, P), ALU.mult)
                dve.drain()
                dve.wait_ge(silu_ready, t + 1)
                dve.tensor_tensor(o, o, g_all[0:nt, t, :], ALU.mult).then_inc(x_ready, 1)
                dve.drain()

        def pe_turn(pe, seq):
            src = o_all if seq in (1, 4) else x
            if seq == 0:
                pe.wait_ge(x_in, 48)
            for t, (t0, nt) in enumerate(TILES):
                if seq:
                    pe.wait_ge(x_ready, 3 * (seq - 1) + t + 1)
                for g in range(2):
                    n = 6 * seq + 2 * t + g
                    if n >= 2:
                        pe.wait_ge(turn_taken, n - 1)
                    for k in range(4):
                        mm = pe.transpose(bank[6 + g][:, k * P:k * P + nt], src[0:nt, t, (4 * g + k) * P:(4 * g + k + 1) * P],
                                          cst[0:nt, C_ID:C_ID + nt])
                    mm.then_inc(turn_ready, 1)

        def act_turn(act, seq):
            for t, (t0, nt) in enumerate(TILES):
                for g in range(2):
                    n = 6 * seq + 2 * t + g
                    act.wait_ge(turn_ready, n + 1)
                    act.activation(xT[:, 4 * g:4 * g + 4, t0:t0 + nt],
                                   bank[6 + g][:, :].rearrange("p (k s) -> p k s", k=4)[:, :, 0:nt],
                                   ACT.Copy).then_inc(turn_taken, 1)

        def pe_join(pe, seq):
            pe.wait_ge(wbig_in, 16 * (seq + 1))
            for t, (t0, nt) in enumerate(TILES):
                pe.wait_ge(turn_taken, 6 * (3 * seq + 1) + 2 * t + 2)
                for c in range(2):
                    cols = slice(512 * c, 512 * c + 512)
                    pe.matmul(ybank(t, c, nt), cst[0:nt, C_AID:C_AID + nt], x[0:nt, t, cols], start=True, stop=False)
                    for k in range(KO):
                        mm = pe.matmul(ybank(t, c, nt), xT[:, k, t0:t0 + nt], wbig[:, k, cols],
                                       start=False, stop=(k == KO - 1))
                mm.then_inc(y_ready, 1)

        def sp_ln(sp, seq):
            if seq:
                sp.wait_ge(x_ready, 3 * NORM_AT[seq - 1])
            else:
                sp.wait_ge(x_ready, 3)
            l, s = divmod(seq, 2)
            sp.dma_start(lnw[:, 0, :], ln_g[l, s:s + 1, :].broadcast_to([P, D])).then_inc(lnw_in, 16)
            sp.dma_start(lnw[:, 1, :], ln_b[l, s:s + 1, :].broadcast_to([P, D])).then_inc(lnw_in, 16)

        NORM_AT = (2, 3, 5, 6)

        def dve_ln(dve, seq):
            for t, (t0, nt) in enumerate(TILES):
                n = 3 * seq + t
                dve.wait_ge(y_ready, n + 1)
                for c in range(2):
                    dve.bn_stats(stats[0:nt, c, :], ybank(t, c, nt))
                dve.drain()
                dve.bn_aggr(mv[0:nt, :], stats[0:nt, :, :].rearrange("p a b -> p (a b)"))
                dve.drain()
                dve.tensor_copy(std[0:nt, 0:1], mv[0:nt, 1:2]).then_inc(stat_ready, 1)
                dve.wait_ge(std_ready, n + 1)
                dve.reciprocal(rstd[0:nt, 0:1], std[0:nt, 0:1])
                dve.drain()
                for c in range(2):
                    ins = dve.tensor_scalar(x[0:nt, t, 512 * c:512 * c + 512], ybank(t, c, nt),
                                            mv[0:nt, 0:1], rstd[0:nt, 0:1], ALU.subtract, ALU.mult)
                ins.then_inc(y_free, 1)
                dve.drain()
                dve.wait_ge(lnw_in, 32 * (seq + 1))
                dve.tensor_tensor(x[0:nt, t, :], x[0:nt, t, :], lnw[0:nt, 0, :], ALU.mult)
                dve.drain()
                dve.tensor_tensor(x[0:nt, t, :], x[0:nt, t, :], lnw[0:nt, 1, :], ALU.add).then_inc(x_ready, 1)
                dve.drain()

        def act_ln(act, seq):
            for t, (t0, nt) in enumerate(TILES):
                act.wait_ge(stat_ready, 3 * seq + t + 1)
                act.activation(std[0:nt, 0:1], std[0:nt, 0:1], ACT.Sqrt, scale=1.0,
                               bias=cst[0:nt, C_EPS:C_EPS + 1]).then_inc(std_ready, 1)

        wflat = wbig[:, :, :].rearrange("p k n -> p (k n)")
        wq = [wflat[:, 2048 * j:2048 * (j + 1)].rearrange("p (k n) -> p k n", k=KO) for j in range(2)]
        keys = [wflat[:, 4096 + 256 * j:4096 + 256 * (j + 1)].rearrange("p (s d) -> p s d", s=2) for j in range(2)]
        xrep = wflat[:, 5120:6144]
        us, vs = wflat[:, 6144:7168], wflat[:, 7168:8192]
        uring = arena[:, 0:RING * D].rearrange("p (r d) -> p r d", r=RING)
        vring = arena[:, RING * D:2 * RING * D].rearrange("p (r d) -> p r d", r=RING)
        gflat = g_all[:, :, :].rearrange("p a b -> p (a b)")
        goff = [0]

        def gview(n, dt=None):
            v = gflat[:, goff[0]:goff[0] + n]
            goff[0] += n
            return v.bitcast(dt) if dt else v

        kT = gview(2 * P).rearrange("p (s n) -> p s n", s=2)
        qT = gview(2 * NT).rearrange("p (s n) -> p s n", s=2)
        sc = gview(6 * P).rearrange("p (t s n) -> p t s n", t=3, s=2)
        sc2 = sb("sc2", [P, 2, NKEYS])
        v12 = sb("v12", [P, 2, TOPK])
        i12 = sb("i12", [P, 2, TOPK], U32)
        i12f = sb("i12f", [P, 2, TOPK])
        cand = sb("cand", [P, TOPK, TOPK])
        cand2 = sb("cand2", [P, TOPK, TOPK])
        sv = sb("sv", [P, TOPK])
        si = sb("si", [P, TOPK], U32)
        ab = sb("ab", [P, 2, TOPK], U32)
        abf = sb("abf", [P, 2, TOPK])
        oh = sb("oh", [P, 2, TOPK, TOPK])
        e12 = sb("e12", [P, 2, TOPK])
        ef = sb("ef", [P, TOPK])
        idx = [[sb(f"idx{t}{j}", [P, TOPK], U32) for j in range(2)] for t in range(2)]
        dif = [[sb(f"dif{t}{j}", [P, TOPK]) for j in range(2)] for t in range(2)]
        dif_s = sb("dif_s", [NS, TOPK])
        gex = [sb(f"gex{t}", [P, TOPK]) for t in range(2)]
        gsum = [sb(f"gsum{t}", [P, 1]) for t in range(2)]
        gsum_s = sb("gsum_s", [NS, 1])
        rp = sb("rp", [NS, 2, TOPK])
        pick = sb("pick", [P, 2, TOPK])
        sidf = sb("sidf", [P, 1])
        sidx = [sb(f"sidx{j}", [P, 1], U32) for j in range(2)]
        sgate = [sb(f"sgate{j}", [P, 1]) for j in range(2)]
        dots = [sb(f"dots{t}", [P, TOPK]) for t in range(2)]
        acts = [sb(f"acts{t}", [P, TOPK]) for t in range(2)]
        w = [sb(f"w{t}", [P, TOPK]) for t in range(2)]
        dot_s = sb("dot_s", [P, 1])
        act_s = sb("act_s", [P, 1])
        wmask = sb("wmask", [P, NS])
        dg = sb("dg", [P, 4, P])

        rt_in = [sem(f"rt_in{j}") for j in range(2)]
        rs_ready = sem("rs_ready")
        rs_taken = sem("rs_taken")
        sc_free = sem("sc_free")
        idx_ready = sem("idx_ready")
        dif_s_ready = sem("dif_s_ready")
        gex_s_ready = sem("gex_s_ready")
        rp_ready = sem("rp_ready")
        repack_ready = sem("repack_ready")
        sidx_ready = sem("sidx_ready")
        unpacked = sem("unpacked")
        u_free = sem("u_free")
        v_free = sem("v_free")
        us_free = sem("us_free")
        vs_free = sem("vs_free")
        u_land = [sem(f"u_land{r}") for r in range(RING)]
        v_land = [sem(f"v_land{r}") for r in range(RING)]
        us_land = sem("us_land")
        vs_land = sem("vs_land")
        dots_ready = sem("dots_ready")
        gelu_ready = sem("gelu_ready")
        w_ready = sem("w_ready")
        dg_ready = sem("dg_ready")
        dot_s_ready = sem("dot_s_ready")
        gelu_s_ready = sem("gelu_s_ready")
        wmask_ready = sem("wmask_ready")
        rep_ready = sem("rep_ready")
        rep_taken = sem("rep_taken")
        V0 = 32 + RING

        def sp_peer(sp, l):
            wq_v = peer_w_q[l].rearrange("(ko ki) (h n) -> ki ko h n", ki=P, h=HH)

            def load_route(h, j):
                sp.dma_start(wq[j], wq_v[:, :, h, :]).then_inc(rt_in[j], 16)
                sp.dma_start(keys[j][:, 0, :], peer_k1[l, h]).then_inc(rt_in[j], 16)
                sp.dma_start(keys[j][:, 1, :], peer_k2[l, h]).then_inc(rt_in[j], 16)
            sp.wait_ge(y_ready, 3 * (2 * l + 1))
            load_route(0, 0)
            load_route(1, 1)

            def body(i, j, last):
                n = 2 * i + j
                if not last:
                    after(sp, "sp", rs_ready, 6 * (HH * l + n) + 3)
                    load_route(n + 2, j)
            with sp.Fori(0, HH // 2 - 1) as i:
                for j in range(2):
                    body(i, j, False)

        def pool_peer(pool, l):
            def gather(dst, table, rows, done):
                pool.indirect_dma_start(out=dst, out_offset=None, in_=table,
                                        in_offset=bass.IndirectOffsetOnAxis(ap=rows, axis=0)).then_inc(done, 16)

            def body(i, j, last):
                hg = 2 * i + j + HH * l

                def u(t, k):
                    after(pool, "pool", u_free, 32 * hg + 16 * t + k + 1)
                    gather(uring[:, k % RING, :], peer_u, idx[t][j][:, k:k + 1], u_land[k % RING])

                def v(t, k):
                    after(pool, "pool", v_free, 32 * hg + 16 * t + k + 1 + V0 - RING)
                    gather(vring[:, k % RING, :], peer_v, idx[t][j][:, k:k + 1], v_land[k % RING])
                after(pool, "pool", idx_ready, 2 * hg + 1)
                for k in range(TOPK):
                    u(0, k)
                after(pool, "pool", idx_ready, 2 * hg + 2)
                for k in range(TOPK):
                    v(0, k)
                    u(1, k)
                after(pool, "pool", sidx_ready, hg + 1)
                after(pool, "pool", us_free, hg + 1)
                gather(us, peer_u, sidx[j][:, :], us_land)
                for k in range(TOPK):
                    v(1, k)
                after(pool, "pool", vs_free, hg + 1)
                gather(vs, peer_v, sidx[j][:, :], vs_land)
            head_pairs(body)(pool)

        def pe_peer(pe, l):
            def step(hg, m):
                if not (isinstance(hg, int) and hg == 0 and m < 2):
                    after(pe, "pe", rs_taken, 6 * hg + m - 1)
                return bank[6 + m % 2]

            def route(i, j, first=False):
                hg = 2 * i + j + HH * l
                after(pe, "pe", rt_in[j], 48 * (i + 1 + 4 * l))
                after(pe, "pe", unpacked, hg + (1 if first else 0))
                b = step(hg, 0)
                for s in range(2):
                    mm = pe.transpose(b[:, s * P:(s + 1) * P], keys[j][:, s, :], ident)
                mm.then_inc(rs_ready, 1)
                for s in range(2):
                    b = step(hg, 1 + s)
                    for k in range(KO):
                        mm = pe.matmul(b[:, 0:NT], wq[j][:, k, s * P:(s + 1) * P], xT[:, k, :],
                                       start=(k == 0), stop=(k == KO - 1))
                    mm.then_inc(rs_ready, 1)
                for t, (t0, nt) in enumerate(TILES):
                    b = step(hg, 3 + t)
                    if t == 0:
                        after(pe, "pe", rs_taken, 6 * hg + 3)
                    for s in range(2):
                        mm = pe.matmul(b[0:nt, s * P:(s + 1) * P], qT[:, s, t0:t0 + nt], kT[:, s, :],
                                       start=True, stop=True)
                    mm.then_inc(rs_ready, 1)

            def repack(hg, ahead):
                after(pe, "pe", rs_taken, 6 * hg + (12 if ahead else 6))
                after(pe, "pe", rp_ready, hg + 1)
                pe.matmul(bank[6][:, 0:2 * TOPK], cst[0:NS, C_BLKT:C_BLKT + P],
                          rp[:, :, :].rearrange("p a b -> p (a b)"), start=True, stop=True).then_inc(repack_ready, 1)

            def add_rows(hg, t):
                for k in range(TOPK):
                    after(pe, "pe", v_land[k % RING], 16 * (4 * hg + 2 * t + k // RING + 1))
                    after(pe, "pe", dg_ready, 32 * hg + 16 * t + k + 1)
                    for c in range(2):
                        mm = pe.matmul(ybank(t, c, P), dg[:, k % 4, :], vring[:, k % RING, 512 * c:512 * c + 512],
                                       start=False, stop=False, skip_group_check=True)
                    mm.then_inc(v_free, 1)

            pe_turn(pe, (2, 5)[l])
            pe.wait_ge(turn_taken, 6 * (3, 6)[l])
            pe.wait_ge(y_free, 3 * (2 * l + 1))
            for c in range(2):
                mm = pe.matmul(bank[4 + c][:, :], cst[0:NS, C_BLKT:C_BLKT + P], x[0:NS, 2, 512 * c:512 * c + 512],
                               start=True, stop=True)
            mm.then_inc(rep_ready, 1)
            pe.wait_ge(rep_taken, l + 1)
            for t, (t0, nt) in enumerate(TILES):
                for c in range(2):
                    pe.matmul(ybank(t, c, nt), cst[0:nt, C_AID:C_AID + nt], x[0:nt, t, 512 * c:512 * c + 512],
                              start=True, stop=False, skip_group_check=True)
            route(0, 0, True)

            def body(i, j, last):
                n = 2 * i + j
                hg = n + HH * l
                ahead = not (last and j == 1)
                if ahead:
                    route(i + j, 1 - j)
                repack(hg, ahead)
                add_rows(hg, 0)
                add_rows(hg, 1)
                after(pe, "pe", vs_land, 16 * (hg + 1))
                after(pe, "pe", wmask_ready, hg + 1)
                for c in range(2):
                    mm = pe.matmul(ybank(2, c, NS), wmask[:, :], vs[:, 512 * c:512 * c + 512],
                                   start=False, stop=False, skip_group_check=True)
                mm.then_inc(vs_free, 1)
            head_pairs(body)(pe)
            pe.drain()
            pe.sem_inc(y_ready, 3)

        def act_peer(act, l):
            act_turn(act, (2, 5)[l])
            act.wait_ge(rep_ready, l + 1)
            for c in range(2):
                ins = act.activation(xrep[:, 512 * c:512 * c + 512], bank[4 + c][:, :], ACT.Copy)
            ins.then_inc(rep_taken, 1)

            def route(hg, m0):
                if m0 == 0:
                    after(act, "act", rs_ready, 6 * hg + 1)
                    act.activation(kT, bank[6][:, 0:2 * P].rearrange("p (s n) -> p s n", s=2), ACT.Copy).then_inc(rs_taken, 1)
                    for s in range(2):
                        after(act, "act", rs_ready, 6 * hg + 2 + s)
                        act.activation(qT[:, s, :], bank[7 - s][:, 0:NT], ACT.Copy).then_inc(rs_taken, 1)
                    for t, (t0, nt) in enumerate(TILES):
                        after(act, "act", rs_ready, 6 * hg + 4 + t)
                        after(act, "act", sc_free, 3 * hg + t + 1)
                        act.activation(sc[0:nt, t, :, :], bank[6 + (t + 1) % 2][0:nt, 0:2 * P].rearrange("p (s n) -> p s n", s=2),
                                       ACT.Copy).then_inc(rs_taken, 1)

            def exp_s(hg):
                after(act, "act", dif_s_ready, hg + 1)
                act.activation(rp[:, 1, :], dif_s[:, :], ACT.Exp, accum_out=gsum_s[:, :]).then_inc(gex_s_ready, 1)

            def gelu(hg, t, j):
                after(act, "act", dots_ready, 2 * hg + t + 1)
                act.activation(gex[t][:, :], dif[t][j][:, :], ACT.Exp, accum_out=gsum[t][:, :])
                act.activation(acts[t][:, :], dots[t][:, :], ACT.Gelu).then_inc(gelu_ready, 1)

            def diags(hg, t, ks):
                after(act, "act", w_ready, 2 * hg + t + 1)
                for k in ks:
                    after(act, "act", v_free, 32 * hg + 16 * t + k - 3 + V0)
                    act.activation(dg[:, k % 4, :], ident, ACT.Copy, scale=w[t][:, k:k + 1]).then_inc(dg_ready, 1)

            route(HH * l, 0)

            def body(i, j, last):
                hg = 2 * i + j + HH * l
                ahead = not (last and j == 1)
                if ahead:
                    route(hg + 1, 0)
                exp_s(hg)
                gelu(hg, 0, j)
                diags(hg, 0, range(TOPK))
                gelu(hg, 1, j)
                after(act, "act", dot_s_ready, hg + 1)
                act.activation(act_s[:, :], dot_s[:, :], ACT.Gelu).then_inc(gelu_s_ready, 1)
                diags(hg, 1, range(TOPK))
            head_pairs(body)(act)

        def dve_peer(dve, l):
            def top16(*rows):
                for v_, i_, src, tmp in rows:
                    dve.max(v_[:, 0:8], src)
                dve.drain()
                for v_, i_, src, tmp in rows:
                    dve.max_index(i_[:, 0:8], v_[:, 0:8], src)
                    dve.match_replace(tmp, v_[:, 0:8], src, -3.0e38)
                dve.drain()
                for v_, i_, src, tmp in rows:
                    dve.max(v_[:, 8:16], tmp)
                dve.drain()
                for v_, i_, src, tmp in rows:
                    dve.max_index(i_[:, 8:16], v_[:, 8:16], tmp)

            def route(hg, t, j):
                nt = TILES[t][1]
                after(dve, "dve", rs_taken, 6 * hg + 4 + t)
                top16(*[(v12[0:nt, s, :], i12[0:nt, s, :], sc[0:nt, t, s, :], sc2[0:nt, s, :]) for s in range(2)])
                dve.drain()
                dve.sem_inc(sc_free, 1)
                dve.tensor_tensor(cand[0:nt, :, :], bc(v12[0:nt, 0, :], 2, TOPK), bc(v12[0:nt, 1, :], 1, TOPK), ALU.add)
                dve.tensor_copy(i12f[0:nt, :, :], i12[0:nt, :, :])
                dve.drain()
                top16((sv[0:nt, :], si[0:nt, :], cand[0:nt, :, :].rearrange("p a b -> p (a b)"),
                       cand2[0:nt, :, :].rearrange("p a b -> p (a b)")))
                dve.drain()
                dve.tensor_scalar(ab[0:nt, 0, :], si[0:nt, :], 4, None, ALU.logical_shift_right)
                dve.tensor_scalar(ab[0:nt, 1, :], si[0:nt, :], 15, None, ALU.bitwise_and)
                if t < 2:
                    after(dve, "dve", v_free, 32 * hg + V0 - 32)
                    dve.tensor_scalar(dif[t][j][:, :], sv[:, :], sv[:, 0:1], None, ALU.subtract)
                else:
                    dve.tensor_scalar(dif_s[:, :], sv[0:nt, :], sv[0:nt, 0:1], None, ALU.subtract).then_inc(dif_s_ready, 1)
                dve.drain()
                dve.tensor_copy(abf[0:nt, :, :], ab[0:nt, :, :])
                dve.drain()
                places = bc(bc(iota[0:nt, :], 1, TOPK), 1, 2)
                dve.tensor_tensor(oh[0:nt], bc(abf[0:nt, :, :], 3, TOPK), places, ALU.is_equal)
                dve.drain()
                dve.tensor_tensor(oh[0:nt], oh[0:nt], bc(i12f[0:nt, :, :], 2, TOPK), ALU.mult)
                dve.drain()
                dve.tensor_reduce(e12[0:nt, :, :], oh[0:nt], AX, ALU.add)
                dve.drain()
                dve.scalar_tensor_tensor(ef[0:nt, :], e12[0:nt, 0, :], float(NKEYS), e12[0:nt, 1, :], ALU.mult, ALU.add)
                dve.drain()
                if t < 2:
                    dve.tensor_scalar(idx[t][j][:, :], ef[:, :], float(NEXP * l), None, ALU.add).then_inc(idx_ready, 1)
                else:
                    dve.tensor_scalar(rp[:, 0, :], ef[0:nt, :], float(NEXP * l), None, ALU.add)
                dve.drain()

            def gate_s(hg):
                after(dve, "dve", gex_s_ready, hg + 1)
                dve.reciprocal(gsum_s[:, :], gsum_s[:, :])
                dve.drain()
                dve.tensor_scalar(rp[:, 1, :], rp[:, 1, :], gsum_s[:, 0:1], None, ALU.mult).then_inc(rp_ready, 1)

            def unpack_s(hg, j):
                after(dve, "dve", repack_ready, hg + 1)
                if not (isinstance(hg, int) and hg == 0):
                    after(dve, "dve", vs_free, hg)
                dve.tensor_tensor(pick[:, :, :], bank[6][:, 0:2 * TOPK].rearrange("p (a k) -> p a k", a=2),
                                  bc(cst[:, C_SEL:C_SEL + TOPK], 1, 2), ALU.mult)
                dve.drain()
                dve.tensor_reduce(sidf[:, :], pick[:, 0, :], AX, ALU.add)
                dve.tensor_reduce(sgate[j][:, :], pick[:, 1, :], AX, ALU.add)
                dve.drain()
                dve.tensor_copy(sidx[j][:, :], sidf[:, :]).then_inc(sidx_ready, 1)
                dve.sem_inc(unpacked, 1)

            def dot(hg, t):
                for k in range(TOPK):
                    after(dve, "dve", u_land[k % RING], 16 * (4 * hg + 2 * t + k // RING + 1))
                    dve.scalar_tensor_tensor(uring[:, k % RING, :], uring[:, k % RING, :], 1.0, x[:, t, :],
                                             ALU.mult, ALU.mult, accum_out=dots[t][:, k:k + 1]).then_inc(u_free, 1)
                dve.drain()
                dve.sem_inc(dots_ready, 1)

            def weigh(hg, t):
                after(dve, "dve", gelu_ready, 2 * hg + t + 1)
                dve.reciprocal(gsum[t][:, :], gsum[t][:, :])
                dve.drain()
                dve.scalar_tensor_tensor(w[t][:, :], gex[t][:, :], gsum[t][:, 0:1], acts[t][:, :],
                                         ALU.mult, ALU.mult).then_inc(w_ready, 1)

            if l == 0:
                dve.sem_inc(u_free, RING)
                dve.sem_inc(v_free, V0)
                dve.sem_inc(sc_free, 3)
                dve.sem_inc(us_free, 1)
                dve.sem_inc(vs_free, 1)
                dve.sem_inc(unpacked, 1)
            for t in range(3):
                route(HH * l, t, 0)

            def body(i, j, last):
                hg = 2 * i + j + HH * l
                ahead = not (last and j == 1)
                dot(hg, 0)
                gate_s(hg)
                if ahead:
                    route(hg + 1, 0, 1 - j)
                unpack_s(hg, j)
                weigh(hg, 0)
                dot(hg, 1)
                after(dve, "dve", us_land, 16 * (hg + 1))
                dve.scalar_tensor_tensor(us, us, 1.0, xrep, ALU.mult, ALU.mult, accum_out=dot_s[:, :]).then_inc(us_free, 1)
                dve.drain()
                dve.sem_inc(dot_s_ready, 1)
                weigh(hg, 1)
                after(dve, "dve", gelu_s_ready, hg + 1)
                after(dve, "dve", vs_free, hg + 1)
                dve.tensor_scalar(wmask[:, :], blk, act_s[:, 0:1], sgate[j][:, 0:1], ALU.mult, ALU.mult).then_inc(wmask_ready, 1)
                if ahead:
                    route(hg + 1, 1, 1 - j)
                    route(hg + 1, 2, 1 - j)
            head_pairs(body)(dve)

        soff[0] = 0
        WKVQ = LORA + ROPE + QLORA
        cbuf = [arena[:, 4608 * j:4608 * j + 4096].rearrange("p (g l) -> p g l", g=PAGES) for j in range(2)]
        kbuf = [arena[:, 4608 * j + 4096:4608 * (j + 1)].rearrange("p (g r) -> p g r", g=PAGES) for j in range(2)]
        HP = PAGES // 2
        cT = arena[:, 9216:11264].rearrange("p (c k) -> p c k", c=2)
        kpT = arena[0:ROPE, 11264:12288]
        w_ukv = arena[:, 12288:16384].rearrange("p (c n) -> p c n", c=2)
        w_dkvq = arena[:, 0:KO * WKVQ].rearrange("p (k n) -> p k n", k=KO)
        w_uq = arena[:, 5376:9984].rearrange("p (k n) -> p k n", k=3)
        kvq = arena[:, 9984:12000].rearrange("p (t n) -> p t n", t=3)
        gkq = gflat[:, 0:LORA + QLORA]
        cqT = gflat[:, 640:640 + 3 * NT].rearrange("p (k t) -> p k t", k=3)
        ckvT = gflat[:, 1432:1432 + 2 * NT].rearrange("p (k t) -> p k t", k=2)
        qs = sview(3 * HG * QD).rearrange("p (t h n) -> p t h n", t=3, h=HG)
        kf = sview(2 * HG * QD).rearrange("p (t h n) -> p t h n", t=2, h=HG)
        vv = sview(2 * HG * VD).rearrange("p (t h n) -> p t h n", t=2, h=HG)
        qfT = sview(2 * HG * P).rearrange("p (t h s) -> p t h s", t=2, h=HG)[0:QD]
        kfT = sview(2 * HG * P).rearrange("p (t h s) -> p t h s", t=2, h=HG)[0:QD]
        ukst = sview(2 * HG * NOPE).rearrange("p (c h n) -> p c h n", c=2, h=HG)
        ukT = sview(2 * HG * P).rearrange("p (c h l) -> p c h l", c=2, h=HG)[0:NOPE]
        pr = sview(12 * P).rearrange("p (a s) -> p a s", a=12)
        pT = sview(12 * P).rearrange("p (a s) -> p a s", a=12)
        rt = sb("rt", [P, 4, HG, ROPE // 2])
        qsT = sb("qsT", [NOPE, HG, NS])
        qlT = sb("qlT", [P, 2, NS, MH])
        qpT = sb("qpT", [ROPE, NS, MH])
        knT = sb("knT", [ROPE, NS])
        ckvS = sb("ckvS", [NS, LORA])
        olT = sb("olT", [P, 2, MH, NS])
        s17 = sb("s17", [P, PAGES + 1, MH])
        m17 = sb("m17", [P, MH])
        mh = sb("mh", [MH, 1])
        dgm = sb("dgm", [MH, MH])
        den = sb("den", [P, MH])
        mx = sb("mx", [P, 2, HG])
        sm = sb("sm", [P, 2, HG])
        ptab = sb("ptab", [1, NS * PAGES], I32)

        wm_in = sem("wm_in")
        ptab_in = sem("ptab_in")
        kvq_ready = sem("kvq_ready")
        kvq_taken = sem("kvq_taken")
        kvq_std = sem("kvq_std")
        kvq_norm = sem("kvq_norm")
        lt_ready = sem("lt_ready")
        lt_taken = sem("lt_taken")
        gp_ready = sem("gp_ready")
        gp_taken = sem("gp_taken")
        ukst_ready = sem("ukst_ready")
        qk_ready = sem("qk_ready")
        qkT_ready = sem("qkT_ready")
        qkT_taken = sem("qkT_taken")
        qlat_ready = sem("qlat_ready")
        qlat_taken = sem("qlat_taken")
        s_ready = sem("s_ready")
        sm_ready = sem("sm_ready")
        p_ready = sem("p_ready")
        pT_ready = sem("pT_ready")
        pT_taken = sem("pT_taken")
        po_ready = sem("po_ready")
        po_taken = sem("po_taken")
        page_in = [sem(f"page_in{j}") for j in range(2)]
        half_ready = sem("half_ready")
        half_taken = sem("half_taken")
        ds_ready = sem("ds_ready")
        dm_ready = sem("dm_ready")
        dmT_ready = sem("dmT_ready")
        dgm_ready = sem("dgm_ready")
        dmb_ready = sem("dmb_ready")
        dsub_ready = sem("dsub_ready")
        dp_ready = sem("dp_ready")
        dsum_ready = sem("dsum_ready")
        dpv_ready = sem("dpv_ready")
        dpv_taken = sem("dpv_taken")
        os_ready = sem("os_ready")

        def sp_mla(sp):
            sp.wait_ge(y_ready, 6)
            dkv = mla_w_dkv.rearrange("(k p) n -> p k n", p=P)
            sp.dma_start(w_dkvq[:, :, 0:LORA + ROPE], dkv).then_inc(wm_in, 16)
            sp.dma_start(w_dkvq[:, :, LORA + ROPE:WKVQ], mla_w_dq[0].rearrange("(k p) n -> p k n", p=P)).then_inc(wm_in, 16)
            sp.dma_start(gkq[:, 0:LORA], mla_kv_norm_g.rearrange("(a n) -> a n", a=1).broadcast_to([P, LORA])).then_inc(wm_in, 16)
            sp.dma_start(gkq[:, LORA:LORA + QLORA], mla_q_norm_g.broadcast_to([P, QLORA])).then_inc(wm_in, 16)
            sp.dma_start(w_uq, mla_w_uq[0].rearrange("(k p) n -> p k n", p=P)).then_inc(wm_in, 16)
            sp.dma_start(w_ukv, mla_w_ukv.rearrange("(c p) h n -> p c (h n)", p=P)).then_inc(wm_in, 16)
            sp.dma_start(ptab[:, :], page_table.rearrange("b g -> (b g)").rearrange("(a n) -> a n", a=1)).then_inc(ptab_in, 16)
            sp.dma_start(wbig[:, :, :], mla_w_o[0].rearrange("(k p) n -> p k n", p=P)).then_inc(wbig_in, 16)
            for t, (t0, nt) in enumerate(TILES):
                sp.wait_ge(kvq_norm, t + 1)
                c = ckv_prompt[0, t0:t0 + nt, :] if t < 2 else ckv_sample.rearrange("b t l -> (b t) l")
                k = kpe_prompt[0, t0:t0 + nt, :] if t < 2 else kpe_sample.rearrange("b t l -> (b t) l")
                sp.dma_start(c, kvq[0:nt, t, 0:LORA]).then_inc(stored, 16)
                sp.dma_start(k, kvq[0:nt, t, LORA:LORA + ROPE]).then_inc(stored, 16)
            sp.wait_ge(stored, 96)
            sp.wait_ge(ptab_in, 16)
            sp.wait_ge(gp_ready, NG)
            def body(i, j, first):
                if not first:
                    after(sp, "sp", dpv_ready, 2 * i + j - 1)
                for g in range(PAGES):
                    page = sp.value_load(ptab[0:1, bass.ds((2 * i + j) * PAGES + g, 1)], min_val=0,
                                         max_val=cache_ckv.shape[0] - 1)
                    sp.dma_start(cbuf[j][:, g, :], cache_ckv[page]).then_inc(page_in[j], 16)
                    sp.dma_start(kbuf[j][:, g, :], cache_kpe[page]).then_inc(page_in[j], 16)
            for j in range(2):
                body(0, j, True)
            with sp.Fori(1, NS // 2) as i:
                for j in range(2):
                    body(i, j, False)

        def pe_mla(pe):
            pe_turn(pe, 3)
            pe.wait_ge(turn_taken, 24)
            pe.wait_ge(wm_in, 16 * 6)
            pe.wait_ge(y_free, 6)
            for t, (t0, nt) in enumerate(TILES):
                for b, (c0, c1) in enumerate(((0, LORA + ROPE), (LORA + ROPE, WKVQ))):
                    for k in range(KO):
                        mm = pe.matmul(bank[2 * t + b][0:nt, 0:c1 - c0], xT[:, k, t0:t0 + nt], w_dkvq[:, k, c0:c1],
                                       start=(k == 0), stop=(k == KO - 1))
                mm.then_inc(kvq_ready, 1)
            for t, (t0, nt) in enumerate(TILES):
                idt = cst[0:nt, C_ID:C_ID + nt]
                pe.wait_ge(kvq_norm, t + 1)
                if t:
                    pe.wait_ge(lt_taken, t)
                for k in range(3):
                    pe.transpose(bank[6][:, k * P:k * P + nt], kvq[0:nt, t, LORA + ROPE + k * P:LORA + ROPE + (k + 1) * P], idt)
                for k in range(2):
                    mm = pe.transpose(bank[7][:, k * P:k * P + nt], kvq[0:nt, t, k * P:(k + 1) * P], idt)
                if t == 2:
                    mm = pe.transpose(bank[7][0:ROPE, 2 * P:2 * P + nt], kvq[0:nt, t, LORA:LORA + ROPE], idt)
                mm.then_inc(lt_ready, 1)
            pe.wait_ge(lt_taken, 3)
            with pe.Fori(0, NG) as g:
                after(pe, "pe", po_taken, g + 1)
                for t, (t0, nt) in enumerate(TILES):
                    for k in range(3):
                        pe.matmul(bank[t][0:nt, 0:HG * QD], cqT[:, k, t0:t0 + nt], w_uq[:, k, bass.ts(g, HG * QD)],
                                  start=(k == 0), stop=(k == 2))
                for t in range(2):
                    for c in range(2):
                        mm = pe.matmul(bank[3 + t][:, :], ckvT[:, c, t * P:(t + 1) * P], w_ukv[:, c, bass.ts(g, 512)],
                                       start=(c == 0), stop=(c == 1))
                mm.then_inc(gp_ready, 1)
                after(pe, "pe", ukst_ready, g + 1)
                after(pe, "pe", gp_taken, g + 1)
                for c in range(2):
                    for h in range(HG):
                        pe.transpose(bank[2 + c][0:NOPE, h * P:(h + 1) * P], ukst[:, c, h, :], ident)
                after(pe, "pe", qk_ready, g + 1)
                for h in range(HG):
                    cols = slice(h * P, (h + 1) * P)
                    pe.transpose(bank[5][0:QD, cols], qs[:, 0, h, :], ident)
                    pe.transpose(bank[6][0:QD, cols], qs[:, 1, h, :], ident)
                    pe.transpose(bank[7][0:QD, cols], kf[:, 0, h, :], ident)
                    pe.transpose(bank[0][0:QD, cols], kf[:, 1, h, :], ident)
                    id8 = cst[0:NS, C_ID:C_ID + NS]
                    pe.transpose(bank[1][0:NOPE, h * NS:(h + 1) * NS], qs[0:NS, 2, h, 0:NOPE], id8)
                    mm = pe.transpose(bank[1][0:ROPE, 64 + h * NS:64 + (h + 1) * NS], qs[0:NS, 2, h, NOPE:QD], id8)
                mm.then_inc(qkT_ready, 1)
                after(pe, "pe", qkT_taken, g + 1)
                for h in range(HG):
                    pe.matmul(bank[5][:, h * P:(h + 1) * P], qfT[:, 0, h, :], kfT[:, 0, h, :], start=True, stop=True)
                    mm = pe.matmul(bank[6 + h // 2][:, (h % 2) * 256:(h % 2) * 256 + 256], qfT[:, 1, h, :], kfT[:, :, h, :],
                                   start=True, stop=True)
                mm.then_inc(s_ready, 1)
                for c in range(2):
                    for h in range(HG):
                        mm = pe.matmul(bank[1][:, (c * HG + h) * NS:(c * HG + h + 1) * NS], ukT[:, c, h, :], qsT[:, h, :],
                                       start=True, stop=True)
                mm.then_inc(qlat_ready, 1)
                after(pe, "pe", p_ready, g + 1)
                for a in range(12):
                    mm = pe.transpose(bank[2 + a // 4][:, (a % 4) * P:(a % 4 + 1) * P], pr[:, a, :], ident)
                mm.then_inc(pT_ready, 1)
                after(pe, "pe", pT_taken, g + 1)
                for h in range(HG):
                    pe.matmul(bank[5][:, h * VD:(h + 1) * VD], pT[:, h, :], vv[:, 0, h, :], start=True, stop=True)
                for h in range(HG):
                    for t in range(2):
                        mm = pe.matmul(bank[6][:, h * VD:(h + 1) * VD], pT[:, HG + 2 * h + t, :], vv[:, t, h, :],
                                       start=(t == 0), stop=(t == 1))
                mm.then_inc(po_ready, 1)
            pe.wait_ge(po_taken, NG + 1)
            pe.wait_ge(qlat_taken, NG)

            def body(i, j, last):
                b = 2 * i + j
                after(pe, "pe", page_in[j], 512 * (i + 1))
                for half in range(2):
                    for q in range(2):
                        after(pe, "pe", half_taken, 4 * b + 2 * half + q + 4)
                        for g in range(4):
                            pg = HP * half + 4 * q + g
                            for c in range(2):
                                pe.transpose(bank[g // 2][:, ((g % 2) * 2 + c) * P:((g % 2) * 2 + c + 1) * P],
                                             cbuf[j][:, pg, c * P:(c + 1) * P], ident)
                            mm = pe.transpose(bank[2][0:ROPE, g * P:(g + 1) * P], kbuf[j][:, pg, :], ident)
                        mm.then_inc(half_ready, 1)
                    after(pe, "pe", half_taken, 4 * b + 2 * half + 2 + 4)
                    if half == 0:
                        after(pe, "pe", ds_taken, b + 1)
                        after(pe, "pe", qst_ready, b + 1)
                    for g in range(HP):
                        out = bank[4][:, (HP * half + g) * MH:(HP * half + g + 1) * MH]
                        for c in range(2):
                            pe.matmul(out, cT[:, c, g * P:(g + 1) * P], qst[:, c, :], start=(c == 0), stop=False)
                        mm = pe.matmul(out, kpT[:, g * P:(g + 1) * P], qst[0:ROPE, 2, :], start=False, stop=True)
                    mm.then_inc(scored, 1)
                out = bank[4][0:NS, PAGES * MH:(PAGES + 1) * MH]
                for c in range(2):
                    pe.matmul(out, ckvT[:, c, 2 * P:NT], qst[:, c, :], start=(c == 0), stop=False)
                pe.matmul(out, knT[:, :], qst[0:ROPE, 2, :], start=False, stop=True).then_inc(ds_ready, 1)
                after(pe, "pe", dm_ready, b + 1)
                pe.transpose(bank[5][0:MH, 0:P], m17[:, :], ident).then_inc(dmT_ready, 1)
                after(pe, "pe", dgm_ready, b + 1)
                pe.matmul(bank[5][:, 0:MH], cst[0:MH, C_ONE:C_ONE + P], dgm[:, :], start=True, stop=True).then_inc(dmb_ready, 1)
                after(pe, "pe", dp_ready, b + 1)
                after(pe, "pe", dpv_taken, b + 1)
                for c in range(2):
                    out = bank[6][:, c * MH:(c + 1) * MH]
                    for pg in range(PAGES):
                        pe.matmul(out, cbuf[j][:, pg, c * P:(c + 1) * P], s17[:, pg, :], start=(pg == 0), stop=False)
                    pe.matmul(out, ckvS[:, c * P:(c + 1) * P], s17[0:NS, PAGES, :], start=False, stop=True)
                after(pe, "pe", dsum_ready, b + 1)
                pe.matmul(bank[6][:, 2 * MH:3 * MH], ones, m17[:, :], start=True, stop=True).then_inc(dpv_ready, 1)
            with pe.Fori(0, NS // 2) as i:
                for j in range(2):
                    body(i, j, False)
            pe.wait_ge(dpv_taken, NS + 1)
            for h in range(MH):
                for c in range(2):
                    mm = pe.matmul(bank[h // 8][0:NS, (h % 8) * VD:(h % 8 + 1) * VD], olT[:, c, h, :],
                                   w_ukv[:, c, h * 128 + NOPE:(h + 1) * 128], start=(c == 0), stop=(c == 1))
            mm.then_inc(os_ready, 1)

        qst = sb("qst", [P, 3, MH])
        qst_ready = sem("qst_ready")
        scored = sem("scored")
        ds_taken = sem("ds_taken")

        def pool_mla(pool):
            pool.wait_ge(qlat_taken, NG)
            with pool.Fori(0, NS) as b:
                after(pool, "pool", ds_taken, b + 1)
                pool.tensor_copy(qst[:, 0:2, :], qlT[:, :, bass.ds(b, 1), :].rearrange("p c b h -> p c (b h)"))
                pool.tensor_copy(qst[0:ROPE, 2, :], qpT[:, bass.ds(b, 1), :].rearrange("p b h -> p (b h)"))
                pool.drain()
                pool.sem_inc(qst_ready, 1)

        def act_mla(act):
            act_turn(act, 3)
            for t, (t0, nt) in enumerate(TILES):
                act.wait_ge(kvq_ready, t + 1)
                act.activation(kvq[0:nt, t, 0:LORA + ROPE], bank[2 * t][0:nt, 0:LORA + ROPE], ACT.Copy)
                act.activation(kvq[0:nt, t, LORA + ROPE:WKVQ], bank[2 * t + 1][0:nt, 0:QLORA], ACT.Copy)
                act.activation(pr[0:nt, 0:2, :].rearrange("p a b -> p (a b)"), bank[2 * t][0:nt, 0:LORA], ACT.Square,
                               accum_out=std[0:nt, 2 * t:2 * t + 1])
                act.activation(pr[0:nt, 2:5, :].rearrange("p a b -> p (a b)"), bank[2 * t + 1][0:nt, 0:QLORA], ACT.Square,
                               accum_out=std[0:nt, 2 * t + 1:2 * t + 2])
                act.drain()
                for s, n in enumerate((LORA, QLORA)):
                    ins = act.activation(std[0:nt, 2 * t + s:2 * t + s + 1], std[0:nt, 2 * t + s:2 * t + s + 1], ACT.Sqrt,
                                         scale=1.0 / n, bias=cst[0:nt, C_EPS + 1:C_EPS + 2])
                act.drain()
                act.sem_inc(kvq_taken, 1)
            for t, (t0, nt) in enumerate(TILES):
                act.wait_ge(lt_ready, t + 1)
                act.activation(cqT[:, :, t0:t0 + nt], bank[6][:, 0:3 * P].rearrange("p (k s) -> p k s", k=3)[:, :, 0:nt], ACT.Copy)
                ins = act.activation(ckvT[:, :, t0:t0 + nt], bank[7][:, 0:2 * P].rearrange("p (k s) -> p k s", k=2)[:, :, 0:nt], ACT.Copy)
                if t == 2:
                    ins = act.activation(knT[:, :], bank[7][0:ROPE, 2 * P:2 * P + NS], ACT.Copy)
                ins.then_inc(lt_taken, 1)
            with act.Fori(0, NG) as g:
                after(act, "act", gp_ready, g + 1)
                for t, (t0, nt) in enumerate(TILES):
                    act.activation(qs[0:nt, t, :, :], bank[t][0:nt, 0:HG * QD].rearrange("p (h n) -> p h n", h=HG), ACT.Copy)
                for t in range(2):
                    kv = bank[3 + t][:, :].rearrange("p (h n) -> p h n", h=HG)
                    act.activation(kf[:, t, :, 0:NOPE], kv[:, :, 0:NOPE], ACT.Copy)
                    ins = act.activation(vv[:, t, :, :], kv[:, :, NOPE:128], ACT.Copy)
                act.drain()
                act.sem_inc(gp_taken, 1)
                after(act, "act", qkT_ready, g + 1)
                for t, b in ((0, 5), (1, 6)):
                    act.activation(qfT[:, t, :, :], bank[b][0:QD, :].rearrange("p (h s) -> p h s", h=HG), ACT.Copy)
                for t, b in ((0, 7), (1, 0)):
                    act.activation(kfT[:, t, :, :], bank[b][0:QD, :].rearrange("p (h s) -> p h s", h=HG), ACT.Copy)
                act.activation(qsT[:, :, :], bank[1][0:NOPE, 0:HG * NS].rearrange("p (h b) -> p h b", h=HG), ACT.Copy)
                act.activation(qpT[:, :, bass.ts(g, HG)], bank[1][0:ROPE, 64:64 + HG * NS].rearrange("p (h b) -> p b h", h=HG), ACT.Copy)
                for c in range(2):
                    ins = act.activation(ukT[:, c, :, :], bank[2 + c][0:NOPE, :].rearrange("p (h l) -> p h l", h=HG), ACT.Copy)
                ins.then_inc(qkT_taken, 1)
                after(act, "act", qlat_ready, g + 1)
                for c in range(2):
                    ins = act.activation(qlT[:, c, :, bass.ts(g, HG)],
                                         bank[1][:, c * HG * NS:(c + 1) * HG * NS].rearrange("p (h b) -> p b h", h=HG), ACT.Copy)
                ins.then_inc(qlat_taken, 1)
                after(act, "act", sm_ready, g + 1)
                act.activation(pr, pr, ACT.Exp).then_inc(p_ready, 1)
                after(act, "act", pT_ready, g + 1)
                for a in range(3):
                    ins = act.activation(pT[:, 4 * a:4 * a + 4, :], bank[2 + a][:, :].rearrange("p (a s) -> p a s", a=4), ACT.Copy)
                ins.then_inc(pT_taken, 1)
            with act.Fori(0, NS) as b:
                for half in range(2):
                    for q in range(2):
                        after(act, "act", half_ready, 4 * b + 2 * half + q + 1)
                        if q == 0:
                            after(act, "act", scored, 2 * b + half + 1)
                        for a in range(2):
                            act.activation(cT[:, :, (4 * q + 2 * a) * P:(4 * q + 2 * a + 2) * P].rearrange("p c (g s) -> p g c s", g=2),
                                           bank[a][:, :].rearrange("p (g c s) -> p g c s", g=2, c=2), ACT.Copy)
                        act.activation(kpT[:, 4 * q * P:(4 * q + 4) * P], bank[2][0:ROPE, :], ACT.Copy).then_inc(half_taken, 1)
                after(act, "act", dsub_ready, b + 1)
                act.activation(s17[:, :, :], s17[:, :, :], ACT.Exp).then_inc(dp_ready, 1)
            act.wait_ge(os_ready, 1)
            for c in range(2):
                ins = act.activation(o_all[0:NS, 2, 512 * c:512 * c + 512], bank[c][0:NS, :], ACT.Copy)
            ins.then_inc(x_ready, 1)

        def rotate(dve, v, nt, t, heads):
            cos = bc(cst[0:nt, C_ROPE + 32 * t:C_ROPE + 32 * t + 16], 1, heads)
            sin_ = bc(cst[0:nt, C_ROPE + 32 * t + 16:C_ROPE + 32 * t + 32], 1, heads)
            a, b = v[:, :, 0:16], v[:, :, 16:32]
            r = rt[0:nt]
            for m, (p_, q_) in enumerate(((a, cos), (b, sin_), (b, cos), (a, sin_))):
                dve.tensor_tensor(r[:, m, 0:heads, :], p_, q_, ALU.mult)
            dve.drain()
            dve.tensor_tensor(a, r[:, 0, 0:heads, :], r[:, 1, 0:heads, :], ALU.subtract)
            dve.tensor_tensor(b, r[:, 2, 0:heads, :], r[:, 3, 0:heads, :], ALU.add)
            dve.drain()

        def dve_mla(dve):
            dve.wait_ge(wm_in, 16 * 6)
            for t, (t0, nt) in enumerate(TILES):
                dve.wait_ge(kvq_taken, t + 1)
                dve.reciprocal(rstd[0:nt, 2 * t:2 * t + 2], std[0:nt, 2 * t:2 * t + 2])
                dve.drain()
                for s, (c0, c1, g0) in enumerate(((0, LORA, 0), (LORA + ROPE, WKVQ, LORA))):
                    dve.scalar_tensor_tensor(kvq[0:nt, t, c0:c1], kvq[0:nt, t, c0:c1], rstd[0:nt, 2 * t + s:2 * t + s + 1],
                                             gkq[0:nt, g0:g0 + c1 - c0], ALU.mult, ALU.mult)
                rotate(dve, kvq[0:nt, t, LORA:LORA + ROPE].unsqueeze(1), nt, t, 1)
                if t < 2:
                    dve.tensor_copy(kf[:, t, :, NOPE:QD], bc(kvq[:, t, LORA:LORA + ROPE], 1, HG))
                else:
                    dve.tensor_copy(ckvS[:, :], kvq[0:NS, 2, 0:LORA])
                dve.drain()
                dve.sem_inc(kvq_norm, 1)
            dve.memset(s17[:, :, :], NEG)
            dve.sem_inc(po_taken, 1)
            dve.sem_inc(dpv_taken, 1)
            dve.sem_inc(ds_taken, 1)
            dve.sem_inc(scored, 1)
            dve.sem_inc(half_taken, 4)
            with dve.Fori(0, NG) as g:
                dve.tensor_copy(ukst, w_ukv.rearrange("p c (h n) -> p c h n", n=128)[:, :, bass.ts(g, HG), 0:NOPE]).then_inc(ukst_ready, 1)
                after(dve, "dve", gp_taken, g + 1)
                for t, (t0, nt) in enumerate(TILES):
                    rotate(dve, qs[0:nt, t, :, NOPE:QD], nt, t, HG)
                dve.sem_inc(qk_ready, 1)
                after(dve, "dve", s_ready, g + 1)
                own = bc(causal, 1, HG)
                dve.scalar_tensor_tensor(pr[:, 0:HG, :], bank[5][:, :].rearrange("p (h s) -> p h s", h=HG), SCALE, own,
                                         ALU.mult, ALU.add)
                for a in range(2):
                    s4 = bank[6 + a][:, :].rearrange("p (h t s) -> p h t s", h=2, t=2)
                    d4 = pr[:, HG + 4 * a:HG + 4 * a + 4, :].rearrange("p (h t) s -> p h t s", h=2)
                    dve.tensor_scalar(d4[:, :, 0, :], s4[:, :, 0, :], SCALE, None, ALU.mult)
                    dve.scalar_tensor_tensor(d4[:, :, 1, :], s4[:, :, 1, :], SCALE, bc(causal, 1, 2), ALU.mult, ALU.add)
                dve.drain()
                p1 = pr[:, HG:12, :].rearrange("p (h t) s -> p h (t s)", t=2)
                dve.tensor_reduce(mx[:, 0, :], pr[:, 0:HG, :], AX, ALU.max)
                dve.tensor_reduce(mx[:, 1, :], p1, AX, ALU.max)
                dve.drain()
                dve.tensor_tensor(pr[:, 0:HG, :], pr[:, 0:HG, :], bc(mx[:, 0, :], 2, P), ALU.subtract)
                dve.tensor_tensor(p1, p1, bc(mx[:, 1, :], 2, 2 * P), ALU.subtract)
                dve.drain()
                dve.sem_inc(sm_ready, 1)
                after(dve, "dve", p_ready, g + 1)
                dve.tensor_reduce(sm[:, 0, :], pr[:, 0:HG, :], AX, ALU.add)
                dve.tensor_reduce(sm[:, 1, :], p1, AX, ALU.add)
                dve.drain()
                dve.reciprocal(sm[:, :, :], sm[:, :, :])
                dve.drain()
                after(dve, "dve", po_ready, g + 1)
                for t in range(2):
                    dve.tensor_tensor(o_all[:, t, bass.ts(g, HG * VD)].rearrange("p (h v) -> p h v", h=HG),
                                      bank[5 + t][:, 0:HG * VD].rearrange("p (h v) -> p h v", h=HG),
                                      bc(sm[:, t, :], 2, VD), ALU.mult)
                dve.drain()
                dve.sem_inc(po_taken, 1)
            dve.sem_inc(x_ready, 2)
            with dve.Fori(0, NS) as b:
                after(dve, "dve", ds_ready, b + 1)
                dve.tensor_scalar(s17[:, 0:PAGES, :], bank[4][:, 0:PAGES * MH].rearrange("p (g h) -> p g h", g=PAGES), SCALE, None, ALU.mult)
                dve.tensor_scalar(s17[0:NS, PAGES, :], bank[4][0:NS, PAGES * MH:(PAGES + 1) * MH], SCALE,
                                  cst[0:NS, bass.ds(b + C_KEYM, 1)], ALU.mult, ALU.add)
                dve.drain()
                dve.sem_inc(ds_taken, 1)
                dve.tensor_reduce(m17[:, :], s17[:, :, :].rearrange("p g h -> p h g"), AX, ALU.max).then_inc(dm_ready, 1)
                after(dve, "dve", dmT_ready, b + 1)
                dve.tensor_reduce(mh[:, :], bank[5][0:MH, 0:P], AX, ALU.max)
                dve.drain()
                dve.tensor_scalar(dgm[:, :], cst[0:MH, C_ID:C_ID + MH], mh[:, 0:1], None, ALU.mult).then_inc(dgm_ready, 1)
                after(dve, "dve", dmb_ready, b + 1)
                dve.tensor_tensor(s17[:, :, :], s17[:, :, :], bc(bank[5][:, 0:MH], 1, PAGES + 1), ALU.subtract).then_inc(dsub_ready, 1)
                after(dve, "dve", dp_ready, b + 1)
                dve.tensor_reduce(m17[:, :], s17[:, :, :].rearrange("p g h -> p h g"), AX, ALU.add).then_inc(dsum_ready, 1)
                after(dve, "dve", dpv_ready, b + 1)
                dve.reciprocal(den[:, :], bank[6][:, 2 * MH:3 * MH])
                dve.drain()
                dve.tensor_tensor(olT[:, :, :, bass.ds(b, 1)].rearrange("p c h b -> p c (h b)"), bank[6][:, 0:2 * MH].rearrange("p (c h) -> p c h", c=2),
                                  bc(den[:, :], 1, 2), ALU.mult)
                dve.tensor_scalar(s17[:, PAGES, :], s17[:, PAGES, :], 0.0, NEG, ALU.mult, ALU.add)
                dve.drain()
                dve.sem_inc(dpv_taken, 1)

        block = ctx.enter_context(nc.Block())

        @block.sync
        def _(sp):
            sp_hgrn(sp)
            sp_ln(sp, 0)
            sp_peer(sp, 0)
            sp_ln(sp, 1)
            sp_mla(sp)
            sp_ln(sp, 2)
            sp_peer(sp, 1)
            sp_ln(sp, 3)
            for t, (t0, nt) in enumerate(TILES):
                sp.wait_ge(x_ready, 15 + t + 1)
                dst = y_prompt[0, t0:t0 + nt, :] if t < 2 else y_sample.rearrange("b t d -> (b t) d")
                sp.dma_start(dst, x[0:nt, t, :]).then_inc(stored, 16)
            sp.wait_ge(stored, 144)
            for j in range(2):
                sp.wait_ge(st_out[j], 32 * (HH // 2 + 1))

        @block.tensor
        def _(pe):
            pe_hgrn(pe)
            pe_turn(pe, 1)
            pe_join(pe, 0)
            pe_peer(pe, 0)
            pe_mla(pe)
            pe_turn(pe, 4)
            pe_join(pe, 1)
            pe_peer(pe, 1)

        @block.scalar
        def _(act):
            act_hgrn(act)
            act_turn(act, 1)
            act_ln(act, 0)
            act_peer(act, 0)
            act_ln(act, 1)
            act_mla(act)
            act_turn(act, 4)
            act_ln(act, 2)
            act_peer(act, 1)
            act_ln(act, 3)

        @block.gpsimd
        def _(pool):
            pool.sem_inc(st_out[0], 32)
            pool.sem_inc(st_out[1], 32)
            pool_hgrn(pool)
            pool_peer(pool, 0)
            pool_mla(pool)
            pool_peer(pool, 1)

        @block.vector
        def _(dve):
            dve_hgrn(dve)
            dve_ln(dve, 0)
            dve_peer(dve, 0)
            dve_ln(dve, 1)
            dve_mla(dve)
            dve_ln(dve, 2)
            dve_peer(dve, 1)
            dve_ln(dve, 3)


_INS = ['x_prompt', 'x_sample', 'state_hgrn', 'cache_ckv', 'cache_kpe', 'page_table',
        'hgrn_w_in', 'hgrn_lb_logits', 'hgrn_norm_g', 'hgrn_w_out',
        'mla_w_dkv', 'mla_kv_norm_g', 'mla_w_ukv', 'mla_w_dq', 'mla_q_norm_g', 'mla_w_uq', 'mla_w_o',
        'peer_w_q', 'peer_k1', 'peer_k2', 'peer_u', 'peer_v', 'ln_g', 'ln_b']
_OUTS = [(1, 256, 1024), (8, 1, 1024), (1, 1, 8, 128, 128), (1, 8, 8, 128, 128),
         (1, 256, 256), (1, 256, 32), (8, 1, 256), (8, 1, 32)]


def kernel(**inputs):
    import numpy as _np
    import concourse.bacc as _bacc
    from concourse import mybir as _mybir
    from concourse.bass_utils import run_bass_kernel_spmd as _run

    nc = _bacc.Bacc("TRN2", target_bir_lowering=False, num_devices=1)
    c, lev = shape_constants(_np)
    arrays = {"in_consts": c, "in_levels": lev}
    for name in _INS:
        a = _np.ascontiguousarray(inputs[name])
        if name in ("peer_u", "peer_v"):
            a = a.reshape(-1, a.shape[-1])
        arrays[f"in_{name}"] = a
    args = [nc.dram_tensor(n, a.shape, _mybir.dt.from_np(a.dtype), kind="ExternalInput").ap()
            for n, a in arrays.items()]
    for i, shape in enumerate(_OUTS):
        args.append(nc.dram_tensor(f"out_{i}", shape, _mybir.dt.float32, kind="ExternalOutput").ap())
    trunk_kernel(nc, *args)
    r = _run(nc, [arrays], core_ids=[0])
    return tuple(r.results[0][f"out_{i}"] for i in range(len(_OUTS)))
```

```python
from contextlib import ExitStack

import concourse.bass as bass
from concourse import mybir

F32 = mybir.dt.float32
I32 = mybir.dt.int32
U32 = mybir.dt.uint32
ALU = mybir.AluOpType
ACT = mybir.ActivationFunctionType
AX = mybir.AxisListType.X

P = 128
D = 1024
KO = D // P
NS = 8
NT = 2 * P + NS
TILES = ((0, P), (P, P), (2 * P, NS))
HH = 8
NLEV = 7
TOPK = 16
NKEYS = 128
NEXP = NKEYS * NKEYS
MH = 16
NOPE, ROPE, VD = 64, 32, 64
QD = NOPE + ROPE
LORA, QLORA = 256, 384
SCALE = float(QD) ** -0.5
HG = 4
NG = MH // HG
PAGES = 16
PAGE = 128
RING = 8
ALPHA = 4.0 ** 0.25
LN_EPS, RMS_EPS = 1e-5, 1e-6
NEG = -1e30
SCRATCH = 9216

C_ID, C_AID, C_CAUSAL, C_EYE8, C_BLK, C_IOTA, C_KEYM, C_BLKT, C_ROPE, C_EPS, C_ONE, C_SEL = (
    0, 128, 256, 384, 448, 456, 472, 480, 608, 704, 706, 834)
C_W = C_SEL + 16


def shape_constants(np):
    c = np.zeros((P, C_W), np.float32)
    p = np.arange(P)
    c[p, C_ID + p] = 1.0
    c[p, C_AID + p] = ALPHA
    c[:, C_CAUSAL:C_CAUSAL + P] = np.where(p[None, :] <= p[:, None], 0.0, NEG)
    c[:, C_EYE8:C_EYE8 + 64] = np.eye(NS, dtype=np.float32).reshape(1, 64)
    c[:, C_BLK:C_BLK + NS] = p[:, None] // TOPK == np.arange(NS)[None, :]
    c[:, C_IOTA:C_IOTA + TOPK] = np.arange(TOPK)[None, :]
    c[:NS, C_KEYM:C_KEYM + NS] = np.where(np.eye(NS) > 0, 0.0, NEG)
    c[:NS, C_BLKT:C_BLKT + P] = p[None, :] // TOPK == np.arange(NS)[:, None]
    inv = np.float32(10000.0) ** (-np.arange(ROPE // 2, dtype=np.float32) / np.float32(ROPE // 2))
    for t in range(3):
        pos = (p + P * t) if t < 2 else np.full(P, PAGES * PAGE)
        ang = pos.astype(np.float32)[:, None] * inv[None, :].astype(np.float32)
        c[:, C_ROPE + 32 * t:C_ROPE + 32 * t + 16] = np.cos(ang)
        c[:, C_ROPE + 32 * t + 16:C_ROPE + 32 * t + 32] = np.sin(ang)
    c[:, C_EPS] = LN_EPS
    c[:, C_EPS + 1] = RMS_EPS
    c[:, C_ONE:C_ONE + P] = 1.0
    c[:, C_SEL:C_SEL + TOPK] = p[:, None] % TOPK == np.arange(TOPK)[None, :]
    lev = np.zeros((P, NLEV, P), np.int32)
    x = p[:, None] ^ p[None, :]
    for l in range(NLEV):
        lev[:, l] = (p[:, None] < p[None, :]) & (x >= 1 << l) & (x < 2 << l)
    return c, lev.reshape(P, NLEV * P)


def bc(ap, axis, n):
    ap = ap.unsqueeze(axis)
    shape = list(ap.shape)
    shape[axis] = n
    return ap.broadcast_to(shape)


def trunk_kernel(nc, consts, level_masks, x_prompt, x_sample, state_hgrn, cache_ckv, cache_kpe, page_table,
                 hgrn_w_in, hgrn_lb_logits, hgrn_norm_g, hgrn_w_out,
                 mla_w_dkv, mla_kv_norm_g, mla_w_ukv, mla_w_dq, mla_q_norm_g, mla_w_uq, mla_w_o,
                 peer_w_q, peer_k1, peer_k2, peer_u, peer_v, ln_g, ln_b,
                 y_prompt, y_sample, st_prompt, st_sample, ckv_prompt, kpe_prompt, ckv_sample, kpe_sample):
    with ExitStack() as ctx:
        def sb(name, shape, dt=F32):
            return ctx.enter_context(nc.sbuf_tensor(name, shape, dt))

        def sem(name):
            return ctx.enter_context(nc.semaphore(name))

        cst = sb("cst", [P, C_W])
        ident = cst[:, C_ID:C_ID + P]
        aident = cst[:, C_AID:C_AID + P]
        causal = cst[:, C_CAUSAL:C_CAUSAL + P]
        eye8 = cst[:, C_EYE8:C_EYE8 + 64].rearrange("p (b c) -> p b c", b=NS)
        blk = cst[:, C_BLK:C_BLK + NS]
        iota = cst[:, C_IOTA:C_IOTA + TOPK]
        ones = cst[:, C_ONE:C_ONE + P]
        x = sb("x", [P, 3, D])
        xT = sb("xT", [P, KO, NT])
        o_all = sb("o_all", [P, 3, D])
        g_all = sb("g_all", [P, 3, D])
        wbig = sb("wbig", [P, KO, D])
        lnw = sb("lnw", [P, 2, D])
        stats = sb("stats", [P, 2, 6])
        mv = sb("mv", [P, 2])
        std = sb("std", [P, MH])
        rstd = sb("rstd", [P, MH])
        arena = sb("arena", [P, 16384])

        bank = [ctx.enter_context(nc.psum_tensor(f"bank{i}", [P, 512], F32)) for i in range(8)]

        consts_in = sem("consts_in")
        x_in = sem("x_in")
        x_ready = sem("x_ready")
        turn_ready = sem("turn_ready")
        turn_taken = sem("turn_taken")
        y_ready = sem("y_ready")
        y_free = sem("y_free")
        stat_ready = sem("stat_ready")
        std_ready = sem("std_ready")
        lnw_in = sem("lnw_in")
        wbig_in = sem("wbig_in")
        passed = {e: sem(f"{e}_passed") for e in ("pe", "act", "dve", "pool", "sp")}
        stored = sem("stored")

        def ybank(t, c, nt):
            return bank[2 * t + c][0:nt, :]

        def nonzero(n):
            return not (isinstance(n, int) and n == 0)

        def after(eng, name, s, value):
            eng.wait_ge(s, value)
            eng.sem_inc(passed[name], 1)

        A = arena
        def view(off, shape):
            n = 1
            for s in shape:
                n *= s
            v = A[:, off:off + n]
            if len(shape) == 2:
                v = v.rearrange("p (a b) -> p a b", a=shape[0])
            elif len(shape) == 3:
                v = v.rearrange("p (a b c) -> p a b c", a=shape[0], b=shape[1])
            return v, off + n

        off = 0
        wh, sin, snew, kk, qq, iT, gT, stf = [], [], [], [], [], [], [], []
        for j in range(2):
            v, off = view(off, [KO, 4, P]); wh.append(v)
        for j in range(2):
            v, off = view(off, [NS, P]); sin.append(v)
            v, off = view(off, [NS, P]); snew.append(v)
        for j in range(2):
            for lst in (kk, qq, iT, gT):
                v, off = view(off, [NT]); lst.append(v)
            v, off = view(off, [P]); stf.append(v)
        ksg, off = view(off, [NT])
        sgp, off = view(off, [NT])
        lf, off = view(off, [NT])
        assert off <= 16384, off
        WB = wbig[:, :, :].rearrange("p k n -> p (k n)")
        scratch = sb("scratch", [P, SCRATCH])
        soff = [0]

        def sview(n, dt=None):
            v = scratch[:, soff[0]:soff[0] + n]
            soff[0] += n
            assert soff[0] <= SCRATCH
            return v.bitcast(dt) if dt else v

        bb = sview(2 * P)
        lev = sview(NLEV * 2 * P).rearrange("p (l t) -> p l t", l=NLEV)
        lmask = sview(NLEV * P, I32).rearrange("p (l t) -> p l t", l=NLEV)
        kdec = sview(2 * P)
        kd = sview(2 * P)
        qe = [sview(P) for j in range(2)]
        eb = sview(P)
        glast = [sview(1) for j in range(2)]
        ffs = [sview(NS) for j in range(2)]
        tr = sview(4 * P).rearrange("p (a s) -> p a s", a=4)
        ts_ = sview(2 * P).rearrange("p (a s) -> p a s", a=2)[0:NS]
        vm = sview(NS * P).rearrange("p (a s) -> p a s", a=NS)[0:NS]
        qm = [sview(NS * NS).rearrange("p (a s) -> p a s", a=NS) for j in range(2)]
        att = sview(2 * P).rearrange("p (a s) -> p a s", a=2)
        st0 = sview(P)
        lbl = sb("lbl", [2 * HH, P])
        lbe = sb("lbe", [P, 2, HH])
        lbs = sb("lbs", [P, HH])
        lb = sb("lb", [P, HH])
        omlb = sb("omlb", [P, HH])

        wh_in = [sem(f"wh_in{j}") for j in range(2)]
        sin_in = [sem(f"sin_in{j}") for j in range(2)]
        lb_in = sem("lb_in")
        lbT_ready = sem("lbT_ready")
        lb_max = sem("lb_max")
        lb_exp = sem("lb_exp")
        omlb_ready = sem("omlb_ready")
        proj_ready = sem("proj_ready")
        proj_taken = sem("proj_taken")
        f_ready = sem("f_ready")
        lf_ready = sem("lf_ready")
        b_ready = sem("b_ready")
        lev_ready = sem("lev_ready")
        e_ready = sem("e_ready")
        xlev_ready = sem("xlev_ready")
        tr_ready = sem("tr_ready")
        tr_taken = sem("tr_taken")
        vm_ready = sem("vm_ready")
        att_ready = sem("att_ready")
        s0_ready = sem("s0_ready")
        st0_ready = sem("st0_ready")
        outer_ready = sem("outer_ready")
        fs_ready = sem("fs_ready")
        snew_ready = sem("snew_ready")
        o_ready = sem("o_ready")
        o_taken = sem("o_taken")
        sp_ready = sem("sp_ready")
        st_out = [sem(f"st_out{j}") for j in range(2)]
        hnorm_in = sem("hnorm_in")
        hss_ready = sem("hss_ready")
        hstd_ready = sem("hstd_ready")
        silu_ready = sem("silu_ready")

        w_in_v = hgrn_w_in[0].rearrange("(ko ki) (c h n) -> ki ko c h n", ki=P, c=4, h=HH)
        s_in_v = state_hgrn[0].rearrange("b h k v -> h k b v")
        s_out_v = st_sample[0].rearrange("b h k v -> h k b v")

        def head_pairs(body):
            def run(eng):
                with eng.Fori(0, HH // 2 - 1) as i:
                    for j in range(2):
                        body(i, j, False)
                for j in range(2):
                    body(HH // 2 - 1, j, True)
            return run

        def sp_hgrn(sp):
            sp.dma_start(cst[:, :], consts).then_inc(consts_in, 16)
            sp.dma_start(lmask[:, :, :].rearrange("p a b -> p (a b)"), level_masks).then_inc(consts_in, 16)
            sp.dma_start(x[:, 0, :], x_prompt[0, 0:P, :]).then_inc(x_in, 16)
            sp.dma_start(x[:, 1, :], x_prompt[0, P:2 * P, :]).then_inc(x_in, 16)
            sp.dma_start(x[0:NS, 2, :], x_sample.rearrange("b t d -> (b t) d")).then_inc(x_in, 16)
            sp.dma_start(lbl[:, :], hgrn_lb_logits.rearrange("r (h k) -> (r h) k", h=HH)).then_inc(lb_in, 16)

            def load_head(h, j):
                for c in range(4):
                    sp.dma_start(wh[j][:, :, c, :], w_in_v[:, :, c, h, :]).then_inc(wh_in[j], 16)
                sp.dma_start(sin[j], s_in_v[h]).then_inc(sin_in[j], 16)
            load_head(0, 0)
            load_head(1, 1)
            sp.dma_start(lnw[:, 1, :], hgrn_norm_g.rearrange("l h v -> l (h v)").broadcast_to([P, D])).then_inc(hnorm_in, 16)
            sp.dma_start(wbig[:, :, :], hgrn_w_out[0].rearrange("(k p) n -> p k n", p=P)).then_inc(wbig_in, 16)

            def body(i, j, last):
                n = 2 * i + j
                if not last:
                    after(sp, "sp", proj_ready, 4 * n + 4)
                    after(sp, "sp", fs_ready, n + 1)
                    load_head(n + 2, j)
                after(sp, "sp", snew_ready, n + 1)
                sp.dma_start(s_out_v[n], snew[j]).then_inc(st_out[j], 16)
                after(sp, "sp", sp_ready, n + 1)
                sp.dma_start(st_prompt[0, 0, n], stf[j]).then_inc(st_out[j], 16)
            head_pairs(body)(sp)

        def pe_hgrn(pe):
            pe.wait_ge(consts_in, 32)
            pe.wait_ge(lb_in, 16)
            pe.transpose(bank[2][:, 0:2 * HH], lbl[:, :], cst[0:2 * HH, C_ID:C_ID + 2 * HH]).then_inc(lbT_ready, 1)

            def project(i, j, nxt):
                n = 2 * i + j
                after(pe, "pe", wh_in[j], 64 * (i + 1))
                for g, c in enumerate((1, 0, 2, 3)):
                    if not (nxt == "first" and g < 2):
                        after(pe, "pe", proj_taken, 4 * n + g - 1)
                    for k in range(KO):
                        mm = pe.matmul(bank[g % 2][:, 0:NT], wh[j][:, k, c, :], xT[:, k, :],
                                       start=(k == 0), stop=(k == KO - 1))
                    mm.then_inc(proj_ready, 1)

            pe_turn(pe, 0)
            pe.wait_ge(turn_taken, 6)
            project(0, 0, "first")

            def body(i, j, last):
                n = 2 * i + j
                after(pe, "pe", proj_taken, 4 * n + 4)
                after(pe, "pe", xlev_ready, n + 1)
                after(pe, "pe", o_taken, n + 1)
                after(pe, "pe", sp_taken, n + 1)
                after(pe, "pe", snew_taken, n + 1)
                for t in range(2):
                    pe.transpose(bank[2][:, t * P:(t + 1) * P], iT[j][:, t * P:(t + 1) * P], ident)
                    pe.transpose(bank[2][:, (2 + t) * P:(3 + t) * P], kd[:, t * P:(t + 1) * P], ident)
                pe.transpose(bank[3][0:NS, 0:P], kk[j][:, 2 * P:NT], ident)
                pe.transpose(bank[3][0:NS, P:2 * P], iT[j][:, 2 * P:NT], ident)
                pe.transpose(bank[3][0:NS, 2 * P:3 * P], gT[j][:, 2 * P:NT], ident)
                pe.transpose(bank[3][:, 3 * P:4 * P], gT[j][:, 0:P], ident).then_inc(tr_ready, 1)
                for l in range(NLEV + 1):
                    for t in range(2):
                        cols = slice(t * P, (t + 1) * P)
                        left = kk[j][:, cols] if l == 0 else lev[:, l - 1, cols]
                        right = qq[j][:, cols] if l == 0 else lev[:, l - 1, cols]
                        mm = pe.matmul(bank[4 + l // 2][:, (l % 2) * 256 + t * P:(l % 2) * 256 + (t + 1) * P],
                                       left, right, start=True, stop=True)
                mm.then_inc(att_ready, 1)
                if j == 0:
                    project(i, 1, "")
                elif not last:
                    project(i + 1, 0, "")
                after(pe, "pe", tr_taken, n + 1)
                pe.matmul(bank[2][:, 0:P], tr[:, 2, :], tr[:, 0, :], start=True, stop=True)
                pe.matmul(bank[2][:, P:2 * P], tr[:, 3, :], tr[:, 1, :], start=True, stop=True).then_inc(s0_ready, 1)
                after(pe, "pe", vm_ready, n + 1)
                for c in range(2):
                    mm = pe.matmul(bank[4 + c][:, :], ts_[:, 0, :], vm[:, 4 * c:4 * c + 4, :],
                                   start=True, stop=True)
                mm.then_inc(outer_ready, 1)
                pe.transpose(bank[3][:, 0:P], gT[j][:, P:2 * P], ident)
                pe.matmul(bank[6][:, 0:P], att[:, 0, :], tr[:, 0, :], start=True, stop=True)
                after(pe, "pe", st0_ready, n + 1)
                pe.matmul(bank[6][:, P:2 * P], att[:, 1, :], tr[:, 1, :], start=True, stop=False)
                pe.matmul(bank[6][:, P:2 * P], qe[j], st0[:, :], start=False, stop=True)
                after(pe, "pe", snew_taken, n + 2)
                for b in range(NS):
                    mm = pe.matmul(bank[3][0:NS, P:2 * P], qm[j][:, b, :], snew[j][:, b, :],
                                   start=(b == 0), stop=(b == NS - 1))
                mm.then_inc(o_ready, 1)
            head_pairs(body)(pe)

        snew_taken = sem("snew_taken")
        sp_taken = sem("sp_taken")

        def act_hgrn(act):
            act.wait_ge(lb_max, 1)
            act.activation(lbe[:, :, :], lbe[:, :, :], ACT.Exp).then_inc(lb_exp, 1)
            act_turn(act, 0)
            act.sem_inc(o_taken, 1)

            def gates(i, j, first):
                n = 2 * i + j
                after(act, "act", proj_ready, 4 * n + 1)
                act.activation(ksg, bank[0][:, 0:NT], ACT.Sigmoid, scale=-1.0)
                act.activation(sgp, bank[0][:, 0:NT], ACT.Sigmoid).then_inc(proj_taken, 1)
                act.drain()
                act.activation(lf, sgp, ACT.Ln, scale=omlb[:, bass.ds(n, 1)], bias=lb[:, bass.ds(n, 1)]).then_inc(lf_ready, 1)
                for g, dst in ((1, qq[j]), (2, iT[j])):
                    after(act, "act", proj_ready, 4 * n + g + 1)
                    act.activation(dst, bank[g % 2][:, 0:NT], ACT.Copy).then_inc(proj_taken, 1)
                after(act, "act", b_ready, n + 1)
                act.activation(eb[:, :], bb[:, P:2 * P], ACT.Exp)
                act.activation(glast[j], bb[:, 2 * P - 1:2 * P], ACT.Exp)
                for t in range(2):
                    act.activation(kdec[:, t * P:(t + 1) * P], bb[:, t * P:(t + 1) * P], ACT.Exp,
                                   scale=-1.0, bias=bb[:, (t + 1) * P - 1:(t + 1) * P])
                after(act, "act", lev_ready, n + 1)
                act.activation(lev[:, :, :], lev[:, :, :], ACT.Exp).then_inc(e_ready, 1)
                after(act, "act", proj_ready, 4 * n + 4)
                act.activation(gT[j], bank[1][:, 0:NT], ACT.Copy).then_inc(proj_taken, 1)
            act.wait_ge(omlb_ready, 1)
            gates(0, 0, True)

            def body(i, j, last):
                n = 2 * i + j
                after(act, "act", tr_ready, n + 1)
                act.activation(tr[:, :, :].rearrange("p a b -> p (a b)"), bank[2][:, :], ACT.Copy)
                act.activation(ts_[:, :, :].rearrange("p a b -> p (a b)"), bank[3][0:NS, 0:2 * P], ACT.Copy)
                act.activation(g_all[0:NS, 2, bass.ts(n, P)], bank[3][0:NS, 2 * P:3 * P], ACT.Copy)
                act.activation(g_all[:, 0, bass.ts(n, P)], bank[3][:, 3 * P:4 * P], ACT.Copy).then_inc(tr_taken, 1)
                if j == 0:
                    gates(i, 1, False)
                elif not last:
                    gates(i + 1, 0, False)
                after(act, "act", s0_ready, n + 1)
                act.activation(st0[:, :], bank[2][:, 0:P], ACT.Copy).then_inc(st0_ready, 1)
                after(act, "act", o_ready, n + 1)
                act.activation(o_all[:, 0, bass.ts(n, P)], bank[6][:, 0:P], ACT.Copy)
                act.activation(o_all[:, 1, bass.ts(n, P)], bank[6][:, P:2 * P], ACT.Copy)
                act.activation(g_all[:, 1, bass.ts(n, P)], bank[3][:, 0:P], ACT.Copy)
                act.activation(o_all[0:NS, 2, bass.ts(n, P)], bank[3][0:NS, P:2 * P], ACT.Copy).then_inc(o_taken, 1)
            head_pairs(body)(act)
            act.drain()
            for t, (t0, nt) in enumerate(TILES):
                act.activation(g_all[0:nt, t, :], g_all[0:nt, t, :], ACT.Silu).then_inc(silu_ready, 1)
            for t, (t0, nt) in enumerate(TILES):
                act.wait_ge(hss_ready, t + 1)
                act.activation(std[0:nt, 0:HH], std[0:nt, 0:HH], ACT.Sqrt, scale=1.0 / P,
                               bias=cst[0:nt, C_EPS + 1:C_EPS + 2]).then_inc(hstd_ready, 1)

        def pool_hgrn(pool):
            def body(i, j, last):
                n = 2 * i + j
                after(pool, "pool", b_ready, n + 1)
                for l in range(1, NLEV + 1):
                    half = 1 << (l - 1)
                    b4 = bb[:, :].rearrange("p (n two s) -> p n two s", two=2, s=half)
                    d4 = lev[:, l - 1, :].rearrange("p (n two s) -> p n two s", two=2, s=half)
                    ref = b4[:, :, 0, half - 1]
                    ref = bc(ref, 2, half)
                    pool.tensor_tensor(d4[:, :, 0, :], ref, b4[:, :, 0, :], ALU.subtract)
                    ins = pool.tensor_tensor(d4[:, :, 1, :], b4[:, :, 1, :], ref, ALU.subtract)
                pool.drain()
                ins = pool.sem_inc(lev_ready, 1)
                after(pool, "pool", sin_in[j], 16 * (i + 1))
                after(pool, "pool", st_slot[j], 32 * (i + 1))
                pool.tensor_tensor(snew[j], sin[j], bc(ffs[j], 2, P), ALU.mult).then_inc(fs_ready, 1)
            head_pairs(body)(pool)

        st_slot = st_out

        def dve_hgrn(dve):
            dve.wait_ge(lbT_ready, 1)
            dve.tensor_copy(lbe[:, :, :], bank[2][:, 0:2 * HH].rearrange("p (r h) -> p r h", r=2))
            dve.drain()
            dve.tensor_tensor(lbs[:, :], lbe[:, 0, :], lbe[:, 1, :], ALU.max)
            dve.drain()
            dve.tensor_tensor(lbe[:, :, :], lbe[:, :, :], bc(lbs[:, :], 1, 2), ALU.subtract).then_inc(lb_max, 1)
            dve.wait_ge(lb_exp, 1)
            dve.tensor_tensor(lbs[:, :], lbe[:, 0, :], lbe[:, 1, :], ALU.add)
            dve.drain()
            dve.reciprocal(lbs[:, :], lbs[:, :])
            dve.drain()
            dve.tensor_tensor(lb[:, :], lbe[:, 0, :], lbs[:, :], ALU.mult)
            dve.drain()
            dve.tensor_scalar(omlb[:, :], lb[:, :], -1.0, 1.0, ALU.mult, ALU.add).then_inc(omlb_ready, 1)
            dve.drain()
            dve.sem_inc(snew_taken, 1)
            dve.sem_inc(sp_taken, 1)

            def gates(i, j):
                n = 2 * i + j
                after(dve, "dve", proj_taken, 4 * n + 1)
                dve.tensor_scalar(kk[j], ksg, omlb[:, bass.ds(n, 1)], None, ALU.mult)
                dve.tensor_scalar(ffs[j], sgp[:, 2 * P:NT], omlb[:, bass.ds(n, 1)], lb[:, bass.ds(n, 1)],
                                  ALU.mult, ALU.add).then_inc(f_ready, 1)
                after(dve, "dve", lf_ready, n + 1)
                for t in range(2):
                    ins = dve.tensor_tensor_scan(bb[:, t * P:(t + 1) * P], ones, lf[:, t * P:(t + 1) * P], 0.0,
                                                 ALU.mult, ALU.add)
                dve.drain()
                dve.sem_inc(b_ready, 1)
                after(dve, "dve", proj_taken, 4 * n + 2)
                after(dve, "dve", e_ready, n + 1)
                for l in range(1, NLEV + 1):
                    half = 1 << (l - 1)
                    e4 = lev[:, l - 1, :].rearrange("p (n two s) -> p n two s", two=2, s=half)
                    k4 = kk[j][:, 0:2 * P].rearrange("p (n two s) -> p n two s", two=2, s=half)
                    q4 = qq[j][:, 0:2 * P].rearrange("p (n two s) -> p n two s", two=2, s=half)
                    dve.tensor_tensor(e4[:, :, 0, :], e4[:, :, 0, :], k4[:, :, 0, :], ALU.mult)
                    dve.tensor_tensor(e4[:, :, 1, :], e4[:, :, 1, :], q4[:, :, 1, :], ALU.mult)
                dve.tensor_tensor(qm[j], bc(qq[j][:, 2 * P:NT], 1, NS), eye8, ALU.mult)
                dve.tensor_tensor(qe[j], qq[j][:, P:2 * P], eb[:, :], ALU.mult)
                dve.tensor_tensor(kd[:, :], kk[j][:, 0:2 * P], kdec[:, :], ALU.mult)
                dve.drain()
                dve.sem_inc(xlev_ready, 1)
            gates(0, 0)

            def body(i, j, last):
                n = 2 * i + j
                after(dve, "dve", att_ready, n + 1)
                dve.tensor_tensor(att[:, :, :], bank[4][:, 0:256].rearrange("p (t s) -> p t s", t=2),
                                  bc(ident, 1, 2), ALU.mult)
                for l in range(1, NLEV + 1):
                    dve.drain()
                    for t in range(2):
                        dve.copy_predicated(att[:, t, :], lmask[:, l - 1, :],
                                            bank[4 + l // 2][:, (l % 2) * 256 + t * P:(l % 2) * 256 + (t + 1) * P])
                after(dve, "dve", tr_taken, n + 1)
                dve.tensor_tensor(vm[:, :, :], bc(ts_[:, 1, :], 1, NS), bc(ident[0:NS, 0:NS], 2, P),
                                  ALU.mult)
                dve.drain()
                dve.sem_inc(vm_ready, 1)
                if j == 0:
                    gates(i, 1)
                elif not last:
                    gates(i + 1, 0)
                after(dve, "dve", outer_ready, n + 1)
                after(dve, "dve", fs_ready, n + 1)
                for c in range(2):
                    dve.tensor_tensor(snew[j][:, 4 * c:4 * c + 4, :], snew[j][:, 4 * c:4 * c + 4, :],
                                      bank[4 + c][:, :].rearrange("p (b v) -> p b v", b=4), ALU.add)
                dve.drain()
                dve.sem_inc(snew_ready, 1)
                dve.sem_inc(snew_taken, 1)
                after(dve, "dve", st0_ready, n + 1)
                after(dve, "dve", st_slot[j], 32 * (i + 1))
                dve.scalar_tensor_tensor(stf[j], st0[:, :], glast[j], bank[2][:, P:2 * P],
                                         ALU.mult, ALU.add)
                dve.drain()
                dve.sem_inc(sp_ready, 1)
                dve.sem_inc(sp_taken, 1)
            head_pairs(body)(dve)
            dve.wait_ge(o_taken, HH + 1)
            dve.wait_ge(hnorm_in, 16)
            sq = arena[:, 0:D]
            for t, (t0, nt) in enumerate(TILES):
                o = o_all[0:nt, t, :]
                o3 = o.rearrange("p (h v) -> p h v", h=HH)
                dve.tensor_tensor(sq[0:nt, :], o, o, ALU.mult)
                dve.drain()
                dve.tensor_reduce(std[0:nt, 0:HH], sq[0:nt, :].rearrange("p (h v) -> p h v", h=HH), AX,
                                  ALU.add).then_inc(hss_ready, 1)
                dve.tensor_tensor(o, o, lnw[0:nt, 1, :], ALU.mult)
                dve.wait_ge(hstd_ready, t + 1)
                dve.reciprocal(rstd[0:nt, 0:HH], std[0:nt, 0:HH])
                dve.drain()
                dve.tensor_tensor(o3, o3, bc(rstd[0:nt, 0:HH], 2, P), ALU.mult)
                dve.drain()
                dve.wait_ge(silu_ready, t + 1)
                dve.tensor_tensor(o, o, g_all[0:nt, t, :], ALU.mult).then_inc(x_ready, 1)
                dve.drain()

        def pe_turn(pe, seq, use=None):
            src = o_all if seq in (1, 4) else x
            if seq == 0:
                pe.wait_ge(x_in, 48)
            for t, (t0, nt) in enumerate(TILES):
                if seq:
                    pe.wait_ge(x_ready, 3 * (seq - 1) + t + 1)
                for g in range(2):
                    n = 6 * seq + 2 * t + g
                    if n >= 2:
                        pe.wait_ge(turn_taken, n - 1)
                    for k in range(4):
                        mm = pe.transpose(bank[6 + g][:, k * P:k * P + nt], src[0:nt, t, (4 * g + k) * P:(4 * g + k + 1) * P],
                                          cst[0:nt, C_ID:C_ID + nt])
                    mm.then_inc(turn_ready, 1)
                if use:
                    pe.wait_ge(turn_taken, 6 * seq + 2 * t + 2)
                    use(t, t0, nt)

        def act_turn(act, seq):
            for t, (t0, nt) in enumerate(TILES):
                for g in range(2):
                    n = 6 * seq + 2 * t + g
                    act.wait_ge(turn_ready, n + 1)
                    act.activation(xT[:, 4 * g:4 * g + 4, t0:t0 + nt],
                                   bank[6 + g][:, :].rearrange("p (k s) -> p k s", k=4)[:, :, 0:nt],
                                   ACT.Copy).then_inc(turn_taken, 1)

        def pe_join(pe, seq):
            def tile(t, t0, nt):
                if t == 0:
                    pe.wait_ge(wbig_in, 16 * (seq + 1))
                for c in range(2):
                    cols = slice(512 * c, 512 * c + 512)
                    pe.matmul(ybank(t, c, nt), cst[0:nt, C_AID:C_AID + nt], x[0:nt, t, cols], start=True, stop=False)
                    for k in range(KO):
                        mm = pe.matmul(ybank(t, c, nt), xT[:, k, t0:t0 + nt], wbig[:, k, cols],
                                       start=False, stop=(k == KO - 1))
                mm.then_inc(y_ready, 1)
            pe_turn(pe, (1, 4)[seq], tile)

        def sp_ln(sp, seq):
            if seq:
                sp.wait_ge(x_ready, 3 * NORM_AT[seq - 1])
            else:
                sp.wait_ge(x_ready, 3)
            l, s = divmod(seq, 2)
            sp.dma_start(lnw[:, 0, :], ln_g[l, s:s + 1, :].broadcast_to([P, D])).then_inc(lnw_in, 16)
            sp.dma_start(lnw[:, 1, :], ln_b[l, s:s + 1, :].broadcast_to([P, D])).then_inc(lnw_in, 16)

        NORM_AT = (2, 3, 5, 6)

        def dve_ln(dve, seq):
            for t, (t0, nt) in enumerate(TILES):
                n = 3 * seq + t
                dve.wait_ge(y_ready, n + 1)
                for c in range(2):
                    dve.bn_stats(stats[0:nt, c, :], ybank(t, c, nt))
                dve.drain()
                dve.bn_aggr(mv[0:nt, :], stats[0:nt, :, :].rearrange("p a b -> p (a b)"))
                dve.drain()
                dve.tensor_copy(std[0:nt, 0:1], mv[0:nt, 1:2]).then_inc(stat_ready, 1)
                dve.wait_ge(lnw_in, 32 * (seq + 1))
                for c in range(2):
                    cols = slice(512 * c, 512 * c + 512)
                    ins = dve.scalar_tensor_tensor(x[0:nt, t, cols], ybank(t, c, nt), mv[0:nt, 0:1], lnw[0:nt, 0, cols],
                                                   ALU.subtract, ALU.mult)
                ins.then_inc(y_free, 1)
                dve.wait_ge(std_ready, n + 1)
                dve.reciprocal(rstd[0:nt, 0:1], std[0:nt, 0:1])
                dve.drain()
                dve.scalar_tensor_tensor(x[0:nt, t, :], x[0:nt, t, :], rstd[0:nt, 0:1], lnw[0:nt, 1, :],
                                         ALU.mult, ALU.add).then_inc(x_ready, 1)
                dve.drain()

        def act_ln(act, seq):
            for t, (t0, nt) in enumerate(TILES):
                act.wait_ge(stat_ready, 3 * seq + t + 1)
                act.activation(std[0:nt, 0:1], std[0:nt, 0:1], ACT.Sqrt, scale=1.0,
                               bias=cst[0:nt, C_EPS:C_EPS + 1]).then_inc(std_ready, 1)

        wflat = wbig[:, :, :].rearrange("p k n -> p (k n)")
        wq = [wflat[:, 2048 * j:2048 * (j + 1)].rearrange("p (k n) -> p k n", k=KO) for j in range(2)]
        keys = [wflat[:, 4096 + 256 * j:4096 + 256 * (j + 1)].rearrange("p (s d) -> p s d", s=2) for j in range(2)]
        xrep = wflat[:, 5120:6144]
        us, vs = wflat[:, 6144:7168], wflat[:, 7168:8192]
        uring = arena[:, 0:RING * D].rearrange("p (r d) -> p r d", r=RING)
        vring = arena[:, RING * D:2 * RING * D].rearrange("p (r d) -> p r d", r=RING)
        gflat = g_all[:, :, :].rearrange("p a b -> p (a b)")
        goff = [0]

        def gview(n, dt=None):
            v = gflat[:, goff[0]:goff[0] + n]
            goff[0] += n
            return v.bitcast(dt) if dt else v

        kT = gview(2 * P).rearrange("p (s n) -> p s n", s=2)
        qT = gview(2 * NT).rearrange("p (s n) -> p s n", s=2)
        sc = gview(6 * P).rearrange("p (t s n) -> p t s n", t=3, s=2)
        sc2 = sb("sc2", [P, 2, NKEYS])
        v12 = sb("v12", [P, 2, TOPK])
        i12 = sb("i12", [P, 2, TOPK], U32)
        i12f = sb("i12f", [P, 2, TOPK])
        cand = sb("cand", [P, TOPK, TOPK])
        cand2 = sb("cand2", [P, TOPK, TOPK])
        sv = sb("sv", [P, TOPK])
        si = sb("si", [P, TOPK], U32)
        ab = sb("ab", [P, 2, TOPK], U32)
        abf = sb("abf", [P, 2, TOPK])
        oh = sb("oh", [P, 2, TOPK, TOPK])
        e12 = sb("e12", [P, 2, TOPK])
        ef = sb("ef", [P, TOPK])
        idx = [[sb(f"idx{t}{j}", [P, TOPK], U32) for j in range(2)] for t in range(2)]
        dif = [[sb(f"dif{t}{j}", [P, TOPK]) for j in range(2)] for t in range(2)]
        dif_s = sb("dif_s", [NS, TOPK])
        gex = [sb(f"gex{t}", [P, TOPK]) for t in range(2)]
        gsum = [sb(f"gsum{t}", [P, 1]) for t in range(2)]
        gsum_s = sb("gsum_s", [NS, 1])
        rp = sb("rp", [NS, 2, TOPK])
        pick = sb("pick", [P, 2, TOPK])
        sidf = sb("sidf", [P, 1])
        sidx = [sb(f"sidx{j}", [P, 1], U32) for j in range(2)]
        sgate = [sb(f"sgate{j}", [P, 1]) for j in range(2)]
        dots = [sb(f"dots{t}", [P, TOPK]) for t in range(2)]
        acts = [sb(f"acts{t}", [P, TOPK]) for t in range(2)]
        w = [sb(f"w{t}", [P, TOPK]) for t in range(2)]
        dot_s = sb("dot_s", [P, 1])
        act_s = sb("act_s", [P, 1])
        wmask = sb("wmask", [P, NS])
        dg = sb("dg", [P, 4, P])

        rt_in = [sem(f"rt_in{j}") for j in range(2)]
        rs_ready = sem("rs_ready")
        rs_taken = sem("rs_taken")
        sc_free = sem("sc_free")
        idx_ready = sem("idx_ready")
        dif_s_ready = sem("dif_s_ready")
        gex_s_ready = sem("gex_s_ready")
        rp_ready = sem("rp_ready")
        repack_ready = sem("repack_ready")
        sidx_ready = sem("sidx_ready")
        unpacked = sem("unpacked")
        u_free = sem("u_free")
        v_free = sem("v_free")
        us_free = sem("us_free")
        vs_free = sem("vs_free")
        u_land = [sem(f"u_land{r}") for r in range(RING)]
        v_land = [sem(f"v_land{r}") for r in range(RING)]
        us_land = sem("us_land")
        vs_land = sem("vs_land")
        dots_ready = sem("dots_ready")
        gelu_ready = sem("gelu_ready")
        w_ready = sem("w_ready")
        dg_ready = sem("dg_ready")
        dot_s_ready = sem("dot_s_ready")
        gelu_s_ready = sem("gelu_s_ready")
        wmask_ready = sem("wmask_ready")
        rep_ready = sem("rep_ready")
        rep_taken = sem("rep_taken")
        V0 = 32 + RING

        def sp_peer(sp, l):
            wq_v = peer_w_q[l].rearrange("(ko ki) (h n) -> ki ko h n", ki=P, h=HH)

            def load_route(h, j):
                sp.dma_start(wq[j], wq_v[:, :, h, :]).then_inc(rt_in[j], 16)
                sp.dma_start(keys[j][:, 0, :], peer_k1[l, h]).then_inc(rt_in[j], 16)
                sp.dma_start(keys[j][:, 1, :], peer_k2[l, h]).then_inc(rt_in[j], 16)
            sp.wait_ge(y_ready, 3 * (2 * l + 1))
            load_route(0, 0)
            load_route(1, 1)

            def body(i, j, last):
                n = 2 * i + j
                if not last:
                    after(sp, "sp", rs_ready, 6 * (HH * l + n) + 3)
                    load_route(n + 2, j)
            with sp.Fori(0, HH // 2 - 1) as i:
                for j in range(2):
                    body(i, j, False)

        def pool_peer(pool, l):
            def gather(dst, table, rows, done):
                pool.indirect_dma_start(out=dst, out_offset=None, in_=table,
                                        in_offset=bass.IndirectOffsetOnAxis(ap=rows, axis=0)).then_inc(done, 16)

            def body(i, j, last):
                hg = 2 * i + j + HH * l

                def u(t, k):
                    after(pool, "pool", u_free, 32 * hg + 16 * t + k + 1)
                    gather(uring[:, k % RING, :], peer_u, idx[t][j][:, k:k + 1], u_land[k % RING])

                def v(t, k):
                    after(pool, "pool", v_free, 32 * hg + 16 * t + k + 1 + V0 - RING)
                    gather(vring[:, k % RING, :], peer_v, idx[t][j][:, k:k + 1], v_land[k % RING])
                after(pool, "pool", idx_ready, 2 * hg + 1)
                for k in range(TOPK):
                    u(0, k)
                after(pool, "pool", idx_ready, 2 * hg + 2)
                for k in range(TOPK):
                    v(0, k)
                    u(1, k)
                after(pool, "pool", sidx_ready, hg + 1)
                after(pool, "pool", us_free, hg + 1)
                gather(us, peer_u, sidx[j][:, :], us_land)
                for k in range(TOPK):
                    v(1, k)
                after(pool, "pool", vs_free, hg + 1)
                gather(vs, peer_v, sidx[j][:, :], vs_land)
            head_pairs(body)(pool)

        def pe_peer(pe, l):
            def step(hg, m):
                if not (isinstance(hg, int) and hg == 0 and m < 2):
                    after(pe, "pe", rs_taken, 6 * hg + m - 1)
                return bank[6 + m % 2]

            def route(i, j, first=False):
                hg = 2 * i + j + HH * l
                after(pe, "pe", rt_in[j], 48 * (i + 1 + 4 * l))
                after(pe, "pe", unpacked, hg + (1 if first else 0))
                b = step(hg, 0)
                for s in range(2):
                    mm = pe.transpose(b[:, s * P:(s + 1) * P], keys[j][:, s, :], ident)
                mm.then_inc(rs_ready, 1)
                for s in range(2):
                    b = step(hg, 1 + s)
                    for k in range(KO):
                        mm = pe.matmul(b[:, 0:NT], wq[j][:, k, s * P:(s + 1) * P], xT[:, k, :],
                                       start=(k == 0), stop=(k == KO - 1))
                    mm.then_inc(rs_ready, 1)
                for t, (t0, nt) in enumerate(TILES):
                    b = step(hg, 3 + t)
                    if t == 0:
                        after(pe, "pe", rs_taken, 6 * hg + 3)
                    for s in range(2):
                        mm = pe.matmul(b[0:nt, s * P:(s + 1) * P], qT[:, s, t0:t0 + nt], kT[:, s, :],
                                       start=True, stop=True)
                    mm.then_inc(rs_ready, 1)

            def repack(hg, ahead):
                after(pe, "pe", rs_taken, 6 * hg + (12 if ahead else 6))
                after(pe, "pe", rp_ready, hg + 1)
                pe.matmul(bank[6][:, 0:2 * TOPK], cst[0:NS, C_BLKT:C_BLKT + P],
                          rp[:, :, :].rearrange("p a b -> p (a b)"), start=True, stop=True).then_inc(repack_ready, 1)

            def add_rows(hg, t):
                for k in range(TOPK):
                    after(pe, "pe", v_land[k % RING], 16 * (4 * hg + 2 * t + k // RING + 1))
                    after(pe, "pe", dg_ready, 32 * hg + 16 * t + k + 1)
                    for c in range(2):
                        mm = pe.matmul(ybank(t, c, P), dg[:, k % 4, :], vring[:, k % RING, 512 * c:512 * c + 512],
                                       start=False, stop=False, skip_group_check=True)
                    mm.then_inc(v_free, 1)

            pe_turn(pe, (2, 5)[l])
            pe.wait_ge(turn_taken, 6 * (3, 6)[l])
            pe.wait_ge(y_free, 3 * (2 * l + 1))
            for c in range(2):
                mm = pe.matmul(bank[4 + c][:, :], cst[0:NS, C_BLKT:C_BLKT + P], x[0:NS, 2, 512 * c:512 * c + 512],
                               start=True, stop=True)
            mm.then_inc(rep_ready, 1)
            pe.wait_ge(rep_taken, l + 1)
            for t, (t0, nt) in enumerate(TILES):
                for c in range(2):
                    pe.matmul(ybank(t, c, nt), cst[0:nt, C_AID:C_AID + nt], x[0:nt, t, 512 * c:512 * c + 512],
                              start=True, stop=False, skip_group_check=True)
            route(0, 0, True)

            def body(i, j, last):
                n = 2 * i + j
                hg = n + HH * l
                ahead = not (last and j == 1)
                if ahead:
                    route(i + j, 1 - j)
                repack(hg, ahead)
                add_rows(hg, 0)
                add_rows(hg, 1)
                after(pe, "pe", vs_land, 16 * (hg + 1))
                after(pe, "pe", wmask_ready, hg + 1)
                for c in range(2):
                    mm = pe.matmul(ybank(2, c, NS), wmask[:, :], vs[:, 512 * c:512 * c + 512],
                                   start=False, stop=False, skip_group_check=True)
                mm.then_inc(vs_free, 1)
            head_pairs(body)(pe)
            pe.drain()
            pe.sem_inc(y_ready, 3)

        def act_peer(act, l):
            act_turn(act, (2, 5)[l])
            act.wait_ge(rep_ready, l + 1)
            for c in range(2):
                ins = act.activation(xrep[:, 512 * c:512 * c + 512], bank[4 + c][:, :], ACT.Copy)
            ins.then_inc(rep_taken, 1)

            def route(hg, m0):
                if m0 == 0:
                    after(act, "act", rs_ready, 6 * hg + 1)
                    act.activation(kT, bank[6][:, 0:2 * P].rearrange("p (s n) -> p s n", s=2), ACT.Copy).then_inc(rs_taken, 1)
                    for s in range(2):
                        after(act, "act", rs_ready, 6 * hg + 2 + s)
                        act.activation(qT[:, s, :], bank[7 - s][:, 0:NT], ACT.Copy).then_inc(rs_taken, 1)
                    for t, (t0, nt) in enumerate(TILES):
                        after(act, "act", rs_ready, 6 * hg + 4 + t)
                        after(act, "act", sc_free, 3 * hg + t + 1)
                        act.activation(sc[0:nt, t, :, :], bank[6 + (t + 1) % 2][0:nt, 0:2 * P].rearrange("p (s n) -> p s n", s=2),
                                       ACT.Copy).then_inc(rs_taken, 1)

            def exp_s(hg):
                after(act, "act", dif_s_ready, hg + 1)
                act.activation(rp[:, 1, :], dif_s[:, :], ACT.Exp, accum_out=gsum_s[:, :]).then_inc(gex_s_ready, 1)

            def gelu(hg, t, j):
                after(act, "act", dots_ready, 2 * hg + t + 1)
                act.activation(gex[t][:, :], dif[t][j][:, :], ACT.Exp, accum_out=gsum[t][:, :])
                act.activation(acts[t][:, :], dots[t][:, :], ACT.Gelu).then_inc(gelu_ready, 1)

            def diags(hg, t, ks):
                after(act, "act", w_ready, 2 * hg + t + 1)
                for k in ks:
                    after(act, "act", v_free, 32 * hg + 16 * t + k - 3 + V0)
                    act.activation(dg[:, k % 4, :], ident, ACT.Copy, scale=w[t][:, k:k + 1]).then_inc(dg_ready, 1)

            route(HH * l, 0)

            def body(i, j, last):
                hg = 2 * i + j + HH * l
                ahead = not (last and j == 1)
                if ahead:
                    route(hg + 1, 0)
                exp_s(hg)
                gelu(hg, 0, j)
                diags(hg, 0, range(TOPK))
                gelu(hg, 1, j)
                after(act, "act", dot_s_ready, hg + 1)
                act.activation(act_s[:, :], dot_s[:, :], ACT.Gelu).then_inc(gelu_s_ready, 1)
                diags(hg, 1, range(TOPK))
            head_pairs(body)(act)

        def dve_peer(dve, l):
            def top16(*rows):
                for v_, i_, src, tmp in rows:
                    dve.max(v_[:, 0:8], src)
                dve.drain()
                for v_, i_, src, tmp in rows:
                    dve.max_index(i_[:, 0:8], v_[:, 0:8], src)
                    dve.match_replace(tmp, v_[:, 0:8], src, -3.0e38)
                dve.drain()
                for v_, i_, src, tmp in rows:
                    dve.max(v_[:, 8:16], tmp)
                dve.drain()
                for v_, i_, src, tmp in rows:
                    dve.max_index(i_[:, 8:16], v_[:, 8:16], tmp)

            def route(hg, t, j):
                nt = TILES[t][1]
                after(dve, "dve", rs_taken, 6 * hg + 4 + t)
                top16(*[(v12[0:nt, s, :], i12[0:nt, s, :], sc[0:nt, t, s, :], sc2[0:nt, s, :]) for s in range(2)])
                dve.drain()
                dve.sem_inc(sc_free, 1)
                dve.tensor_tensor(cand[0:nt, :, :], bc(v12[0:nt, 0, :], 2, TOPK), bc(v12[0:nt, 1, :], 1, TOPK), ALU.add)
                dve.tensor_copy(i12f[0:nt, :, :], i12[0:nt, :, :])
                dve.drain()
                top16((sv[0:nt, :], si[0:nt, :], cand[0:nt, :, :].rearrange("p a b -> p (a b)"),
                       cand2[0:nt, :, :].rearrange("p a b -> p (a b)")))
                dve.drain()
                dve.tensor_scalar(ab[0:nt, 0, :], si[0:nt, :], 4, None, ALU.logical_shift_right)
                dve.tensor_scalar(ab[0:nt, 1, :], si[0:nt, :], 15, None, ALU.bitwise_and)
                if t < 2:
                    after(dve, "dve", v_free, 32 * hg + V0 - 32)
                    dve.tensor_scalar(dif[t][j][:, :], sv[:, :], sv[:, 0:1], None, ALU.subtract)
                else:
                    dve.tensor_scalar(dif_s[:, :], sv[0:nt, :], sv[0:nt, 0:1], None, ALU.subtract).then_inc(dif_s_ready, 1)
                dve.drain()
                dve.tensor_copy(abf[0:nt, :, :], ab[0:nt, :, :])
                dve.drain()
                places = bc(bc(iota[0:nt, :], 1, TOPK), 1, 2)
                dve.tensor_tensor(oh[0:nt], bc(abf[0:nt, :, :], 3, TOPK), places, ALU.is_equal)
                dve.drain()
                dve.tensor_tensor(oh[0:nt], oh[0:nt], bc(i12f[0:nt, :, :], 2, TOPK), ALU.mult)
                dve.drain()
                dve.tensor_reduce(e12[0:nt, :, :], oh[0:nt], AX, ALU.add)
                dve.drain()
                dve.scalar_tensor_tensor(ef[0:nt, :], e12[0:nt, 0, :], float(NKEYS), e12[0:nt, 1, :], ALU.mult, ALU.add)
                dve.drain()
                if t < 2:
                    dve.tensor_scalar(idx[t][j][:, :], ef[:, :], float(NEXP * l), None, ALU.add).then_inc(idx_ready, 1)
                else:
                    dve.tensor_scalar(rp[:, 0, :], ef[0:nt, :], float(NEXP * l), None, ALU.add)
                dve.drain()

            def gate_s(hg):
                after(dve, "dve", gex_s_ready, hg + 1)
                dve.reciprocal(gsum_s[:, :], gsum_s[:, :])
                dve.drain()
                dve.tensor_scalar(rp[:, 1, :], rp[:, 1, :], gsum_s[:, 0:1], None, ALU.mult).then_inc(rp_ready, 1)

            def unpack_s(hg, j):
                after(dve, "dve", repack_ready, hg + 1)
                if not (isinstance(hg, int) and hg == 0):
                    after(dve, "dve", vs_free, hg)
                dve.tensor_tensor(pick[:, :, :], bank[6][:, 0:2 * TOPK].rearrange("p (a k) -> p a k", a=2),
                                  bc(cst[:, C_SEL:C_SEL + TOPK], 1, 2), ALU.mult)
                dve.drain()
                dve.tensor_reduce(sidf[:, :], pick[:, 0, :], AX, ALU.add)
                dve.tensor_reduce(sgate[j][:, :], pick[:, 1, :], AX, ALU.add)
                dve.drain()
                dve.tensor_copy(sidx[j][:, :], sidf[:, :]).then_inc(sidx_ready, 1)
                dve.sem_inc(unpacked, 1)

            def dot(hg, t):
                for k in range(TOPK):
                    after(dve, "dve", u_land[k % RING], 16 * (4 * hg + 2 * t + k // RING + 1))
                    dve.scalar_tensor_tensor(uring[:, k % RING, :], uring[:, k % RING, :], 1.0, x[:, t, :],
                                             ALU.mult, ALU.mult, accum_out=dots[t][:, k:k + 1]).then_inc(u_free, 1)
                dve.drain()
                dve.sem_inc(dots_ready, 1)

            def weigh(hg, t):
                after(dve, "dve", gelu_ready, 2 * hg + t + 1)
                dve.reciprocal(gsum[t][:, :], gsum[t][:, :])
                dve.drain()
                dve.scalar_tensor_tensor(w[t][:, :], gex[t][:, :], gsum[t][:, 0:1], acts[t][:, :],
                                         ALU.mult, ALU.mult).then_inc(w_ready, 1)

            if l == 0:
                dve.sem_inc(u_free, RING)
                dve.sem_inc(v_free, V0)
                dve.sem_inc(sc_free, 3)
                dve.sem_inc(us_free, 1)
                dve.sem_inc(vs_free, 1)
                dve.sem_inc(unpacked, 1)
            for t in range(3):
                route(HH * l, t, 0)

            def body(i, j, last):
                hg = 2 * i + j + HH * l
                ahead = not (last and j == 1)
                dot(hg, 0)
                gate_s(hg)
                if ahead:
                    route(hg + 1, 0, 1 - j)
                unpack_s(hg, j)
                weigh(hg, 0)
                dot(hg, 1)
                after(dve, "dve", us_land, 16 * (hg + 1))
                dve.scalar_tensor_tensor(us, us, 1.0, xrep, ALU.mult, ALU.mult, accum_out=dot_s[:, :]).then_inc(us_free, 1)
                dve.drain()
                dve.sem_inc(dot_s_ready, 1)
                weigh(hg, 1)
                after(dve, "dve", gelu_s_ready, hg + 1)
                after(dve, "dve", vs_free, hg + 1)
                dve.tensor_scalar(wmask[:, :], blk, act_s[:, 0:1], sgate[j][:, 0:1], ALU.mult, ALU.mult).then_inc(wmask_ready, 1)
                if ahead:
                    route(hg + 1, 1, 1 - j)
                    route(hg + 1, 2, 1 - j)
            head_pairs(body)(dve)

        soff[0] = 0
        WKVQ = LORA + ROPE + QLORA
        PW = PAGES * (LORA + ROPE)
        slots = [arena[:, 0:PW], arena[:, PW:2 * PW], scratch[:, 0:PW]]
        cbuf = [v[:, 0:PAGES * LORA].rearrange("p (g l) -> p g l", g=PAGES) for v in slots]
        kbuf = [v[:, PAGES * LORA:PW].rearrange("p (g r) -> p g r", g=PAGES) for v in slots]
        QP = 4
        NQ = PAGES // QP
        cT = arena[:, 9216:11264].rearrange("p (s c k) -> p s c k", s=2, c=2)
        kpT = arena[0:ROPE, 11264:12288].rearrange("p (s k) -> p s k", s=2)
        NKEY = PAGES * PAGE + NS
        dsc = scratch[0:MH, PW:PW + NKEY]
        dp = scratch[0:MH, PW + NKEY:PW + 2 * NKEY]
        dol = scratch[0:MH, PW + 2 * NKEY:PW + 2 * NKEY + LORA]
        w_ukv = arena[:, 12288:16384].rearrange("p (c n) -> p c n", c=2)
        w_dkvq = arena[:, 0:KO * WKVQ].rearrange("p (k n) -> p k n", k=KO)
        w_uq = arena[:, 5376:9984].rearrange("p (k n) -> p k n", k=3)
        kvq = arena[:, 9984:12000].rearrange("p (t n) -> p t n", t=3)
        gkq = gflat[:, 0:LORA + QLORA]
        cqT = gflat[:, 640:640 + 3 * NT].rearrange("p (k t) -> p k t", k=3)
        ckvT = gflat[:, 1432:1432 + 2 * NT].rearrange("p (k t) -> p k t", k=2)
        qs = sview(3 * HG * QD).rearrange("p (t h n) -> p t h n", t=3, h=HG)
        kf = sview(2 * HG * QD).rearrange("p (t h n) -> p t h n", t=2, h=HG)
        vv = sview(2 * HG * VD).rearrange("p (t h n) -> p t h n", t=2, h=HG)
        qfT = sview(2 * HG * P).rearrange("p (t h s) -> p t h s", t=2, h=HG)[0:QD]
        kfT = sview(2 * HG * P).rearrange("p (t h s) -> p t h s", t=2, h=HG)[0:QD]
        ukst = sview(2 * HG * NOPE).rearrange("p (c h n) -> p c h n", c=2, h=HG)
        ukT = sview(2 * HG * P).rearrange("p (c h l) -> p c h l", c=2, h=HG)[0:NOPE]
        pr = sview(12 * P).rearrange("p (a s) -> p a s", a=12)
        pT = sview(12 * P).rearrange("p (a s) -> p a s", a=12)
        rt = sb("rt", [P, 4, HG, ROPE // 2])
        qsT = sb("qsT", [NOPE, HG, NS])
        qlT = sb("qlT", [P, 2, NS, MH])
        qpT = sb("qpT", [ROPE, NS, MH])
        knT = sb("knT", [ROPE, NS])
        ckvS = sb("ckvS", [NS, LORA])
        olT = sb("olT", [P, 2, MH, NS])
        dpT = sb("dpT", [P, PAGES + 1, MH])
        dmx = sb("dmx", [MH, NQ + 1])
        dneg = sb("dneg", [MH, 1])
        dsum = sb("dsum", [MH, 1])
        drs = sb("drs", [MH, 1])
        mx = sb("mx", [P, 2, HG])
        sm = sb("sm", [P, 2, HG])
        ptab = sb("ptab", [1, NS * PAGES], I32)

        wd_in = sem("wd_in")
        wm_in = sem("wm_in")
        ptab_in = sem("ptab_in")
        kvq_ready = sem("kvq_ready")
        kvq_taken = sem("kvq_taken")
        kvq_std = sem("kvq_std")
        kvq_norm = sem("kvq_norm")
        lt_ready = sem("lt_ready")
        lt_taken = sem("lt_taken")
        q_ready = sem("q_ready")
        q_taken = sem("q_taken")
        qrot_ready = sem("qrot_ready")
        kv_ready = sem("kv_ready")
        kv_taken = sem("kv_taken")
        ukst_ready = sem("ukst_ready")
        qT_ready = sem("qT_ready")
        qT_taken = sem("qT_taken")
        kT_ready = sem("kT_ready")
        kT_taken = sem("kT_taken")
        ukT_ready = sem("ukT_ready")
        ukT_taken = sem("ukT_taken")
        s_taken = sem("s_taken")
        qlat_ready = sem("qlat_ready")
        qlat_taken = sem("qlat_taken")
        s_ready = sem("s_ready")
        sm_ready = sem("sm_ready")
        p_ready = sem("p_ready")
        pT_ready = sem("pT_ready")
        pT_taken = sem("pT_taken")
        po_ready = sem("po_ready")
        po_taken = sem("po_taken")
        page_in = [sem(f"page_in{j}") for j in range(3)]
        rot_in = [sem(f"rot_in{j}") for j in range(3)]
        ct_ready = sem("ct_ready")
        ct_taken = sem("ct_taken")
        ds_ready = sem("ds_ready")
        ds_taken = sem("ds_taken")
        dn_ready = sem("dn_ready")
        dm_ready = sem("dm_ready")
        dp_ready = sem("dp_ready")
        dpT_ready = sem("dpT_ready")
        dpT_taken = sem("dpT_taken")
        dpv_ready = sem("dpv_ready")
        dol_ready = sem("dol_ready")
        dolT_ready = sem("dolT_ready")
        dolT_taken = sem("dolT_taken")
        os_ready = sem("os_ready")

        def sp_mla(sp):
            sp.wait_ge(y_ready, 6)
            dkv = mla_w_dkv.rearrange("(k p) n -> p k n", p=P)
            sp.dma_start(w_dkvq[:, :, 0:LORA + ROPE], dkv).then_inc(wd_in, 16)
            sp.dma_start(w_dkvq[:, :, LORA + ROPE:WKVQ], mla_w_dq[0].rearrange("(k p) n -> p k n", p=P)).then_inc(wd_in, 16)
            sp.dma_start(gkq[:, 0:LORA], mla_kv_norm_g.rearrange("(a n) -> a n", a=1).broadcast_to([P, LORA])).then_inc(wm_in, 16)
            sp.dma_start(gkq[:, LORA:LORA + QLORA], mla_q_norm_g.broadcast_to([P, QLORA])).then_inc(wm_in, 16)
            sp.dma_start(w_uq, mla_w_uq[0].rearrange("(k p) n -> p k n", p=P)).then_inc(wm_in, 16)
            sp.dma_start(w_ukv, mla_w_ukv.rearrange("(c p) h n -> p c (h n)", p=P)).then_inc(wm_in, 16)
            sp.dma_start(ptab[:, :], page_table.rearrange("b g -> (b g)").rearrange("(a n) -> a n", a=1)).then_inc(ptab_in, 16)
            sp.dma_start(wbig[:, :, :], mla_w_o[0].rearrange("(k p) n -> p k n", p=P)).then_inc(wbig_in, 16)
            for t, (t0, nt) in enumerate(TILES):
                sp.wait_ge(kvq_norm, t + 1)
                c = ckv_prompt[0, t0:t0 + nt, :] if t < 2 else ckv_sample.rearrange("b t l -> (b t) l")
                k = kpe_prompt[0, t0:t0 + nt, :] if t < 2 else kpe_sample.rearrange("b t l -> (b t) l")
                sp.dma_start(c, kvq[0:nt, t, 0:LORA]).then_inc(stored, 16)
                sp.dma_start(k, kvq[0:nt, t, LORA:LORA + ROPE]).then_inc(stored, 16)
            load_pages(sp, cbuf, cache_ckv, page_in)

        def load_pages(eng, buf, cache, landed):
            eng.wait_ge(ptab_in, 16)
            eng.wait_ge(stored, 96)
            eng.wait_ge(q_ready, NG)
            for b in range(NS):
                if b == 2:
                    eng.wait_ge(po_taken, NG + 1)
                if b >= 3:
                    eng.wait_ge(dpv_ready, b - 2)
                with eng.Fori(0, PAGES) as g:
                    page = eng.value_load(ptab[0:1, bass.ds(g + b * PAGES, 1)], min_val=0,
                                          max_val=cache.shape[0] - 1)
                    eng.dma_start(buf[b % 3][:, bass.ds(g, 1), :].rearrange("p a l -> p (a l)"),
                                  cache[page]).then_inc(landed[b % 3], 16)

        def pe_mla(pe):
            def down(t, t0, nt):
                if t == 0:
                    pe.wait_ge(wd_in, 32)
                pe.wait_ge(y_free, 3 + t + 1)
                for b, (c0, c1) in enumerate(((0, LORA + ROPE), (LORA + ROPE, WKVQ))):
                    for k in range(KO):
                        mm = pe.matmul(bank[2 * t + b][0:nt, 0:c1 - c0], xT[:, k, t0:t0 + nt], w_dkvq[:, k, c0:c1],
                                       start=(k == 0), stop=(k == KO - 1))
                mm.then_inc(kvq_ready, 1)
            pe_turn(pe, 3, down)
            for t, (t0, nt) in enumerate(TILES):
                idt = cst[0:nt, C_ID:C_ID + nt]
                pe.wait_ge(kvq_norm, t + 1)
                if t:
                    pe.wait_ge(lt_taken, t)
                for k in range(3):
                    pe.transpose(bank[6][:, k * P:k * P + nt], kvq[0:nt, t, LORA + ROPE + k * P:LORA + ROPE + (k + 1) * P], idt)
                for k in range(2):
                    mm = pe.transpose(bank[7][:, k * P:k * P + nt], kvq[0:nt, t, k * P:(k + 1) * P], idt)
                if t == 2:
                    mm = pe.transpose(bank[7][0:ROPE, 2 * P:2 * P + nt], kvq[0:nt, t, LORA:LORA + ROPE], idt)
                mm.then_inc(lt_ready, 1)
            pe.wait_ge(lt_taken, 3)
            pe.wait_ge(wm_in, 16 * 4)

            def queries(g, tiles):
                for t in tiles:
                    t0, nt = TILES[t]
                    for k in range(3):
                        mm = pe.matmul(bank[(0, 1, 7)[t]][0:nt, 0:HG * QD], cqT[:, k, t0:t0 + nt],
                                       w_uq[:, k, bass.ds(g * (HG * QD), HG * QD)], start=(k == 0), stop=(k == 2))
                return mm

            def group(g, last):
                for t in range(2):
                    for c in range(2):
                        mm = pe.matmul(bank[3 + t][:, :], ckvT[:, c, t * P:(t + 1) * P], w_ukv[:, c, bass.ts(g, 512)],
                                       start=(c == 0), stop=(c == 1))
                mm.then_inc(kv_ready, 1)
                after(pe, "pe", qrot_ready, g + 1)
                after(pe, "pe", po_taken, g + 1)
                for h in range(HG):
                    cols = slice(h * P, (h + 1) * P)
                    pe.transpose(bank[5][0:QD, cols], qs[:, 0, h, :], ident)
                    pe.transpose(bank[6][0:QD, cols], qs[:, 1, h, :], ident)
                    id8 = cst[0:NS, C_ID:C_ID + NS]
                    pe.transpose(bank[1][0:NOPE, h * NS:(h + 1) * NS], qs[0:NS, 2, h, 0:NOPE], id8)
                    mm = pe.transpose(bank[1][0:ROPE, 64 + h * NS:64 + (h + 1) * NS], qs[0:NS, 2, h, NOPE:QD], id8)
                mm.then_inc(qT_ready, 1)
                after(pe, "pe", ukst_ready, g + 1)
                for h in range(HG):
                    pe.transpose(bank[2][0:NOPE, h * P:(h + 1) * P], ukst[:, 0, h, :], ident)
                after(pe, "pe", kv_taken, g + 1)
                for h in range(HG):
                    cols = slice(h * P, (h + 1) * P)
                    pe.transpose(bank[7][0:QD, cols], kf[:, 0, h, :], ident)
                    mm = pe.transpose(bank[0][0:QD, cols], kf[:, 1, h, :], ident)
                mm.then_inc(kT_ready, 1)
                for h in range(HG):
                    mm = pe.transpose(bank[3][0:NOPE, h * P:(h + 1) * P], ukst[:, 1, h, :], ident)
                mm.then_inc(ukT_ready, 1)
                after(pe, "pe", qT_taken, g + 1)
                after(pe, "pe", kT_taken, g + 1)
                for h in range(HG):
                    pe.matmul(bank[5][:, h * P:(h + 1) * P], qfT[:, 0, h, :], kfT[:, 0, h, :], start=True, stop=True)
                    mm = pe.matmul(bank[6 + h // 2][:, (h % 2) * 256:(h % 2) * 256 + 256], qfT[:, 1, h, :], kfT[:, :, h, :],
                                   start=True, stop=True)
                mm.then_inc(s_ready, 1)
                after(pe, "pe", ukT_taken, g + 1)
                for c in range(2):
                    for h in range(HG):
                        mm = pe.matmul(bank[1][:, (c * HG + h) * NS:(c * HG + h + 1) * NS], ukT[:, c, h, :], qsT[:, h, :],
                                       start=True, stop=True)
                mm.then_inc(qlat_ready, 1)
                if not last:
                    queries(g + 1, (0,))
                    after(pe, "pe", qlat_taken, g + 1)
                    queries(g + 1, (1,))
                    after(pe, "pe", s_taken, g + 1)
                    queries(g + 1, (2,)).then_inc(q_ready, 1)
                after(pe, "pe", p_ready, g + 1)
                for a in range(12):
                    mm = pe.transpose(bank[2 + a // 4][:, (a % 4) * P:(a % 4 + 1) * P], pr[:, a, :], ident)
                mm.then_inc(pT_ready, 1)
                after(pe, "pe", pT_taken, 2 * (g + 1))
                for h in range(HG):
                    pe.matmul(bank[5][:, h * VD:(h + 1) * VD], pT[:, h, :], vv[:, 0, h, :], start=True, stop=True)
                for h in range(HG):
                    for t in range(2):
                        mm = pe.matmul(bank[6][:, h * VD:(h + 1) * VD], pT[:, HG + 2 * h + t, :], vv[:, t, h, :],
                                       start=(t == 0), stop=(t == 1))
                mm.then_inc(po_ready, 1)

            queries(0, (0, 1, 2)).then_inc(q_ready, 1)
            with pe.Fori(0, NG - 1) as g:
                group(g, False)
            group(NG - 1, True)
            pe.wait_ge(po_taken, NG + 1)
            pe.wait_ge(qlat_taken, NG)

            def turn_pages(b, q, slot):
                if nonzero(b) or q:
                    after(pe, "pe", ct_taken, NQ * b + q)
                for g in range(QP):
                    cols = slice(g * P, (g + 1) * P)
                    for c in range(2):
                        pe.transpose(bank[c][:, cols], cbuf[slot][:, QP * q + g, c * P:(c + 1) * P], ident)
                    mm = pe.transpose(bank[2][0:ROPE, cols], kbuf[slot][:, QP * q + g, :], ident)
                mm.then_inc(ct_ready, 1)

            def score(b, q):
                if nonzero(b) or q >= 2:
                    after(pe, "pe", ds_taken, NQ * b + q - 1)
                out = bank[3 + q % 2][0:MH, :]
                for c in range(2):
                    pe.matmul(out, qst[:, c, :], cT[:, q % 2, c, :], start=(c == 0), stop=False)
                pe.matmul(out, qst[0:ROPE, 2, :], kpT[:, q % 2, :], start=False, stop=True).then_inc(ds_ready, 1)

            def score_new(b):
                out = bank[5][0:MH, 0:NS]
                for c in range(2):
                    pe.matmul(out, qst[:, c, :], ckvT[:, c, 2 * P:NT], start=(c == 0), stop=False)
                pe.matmul(out, qst[0:ROPE, 2, :], knT[:, :], start=False, stop=True).then_inc(dn_ready, 1)

            def turn_probs(b):
                after(pe, "pe", dp_ready, b + 1)
                if nonzero(b):
                    after(pe, "pe", dolT_taken, b)
                for pg in range(PAGES):
                    pe.transpose(bank[6][:, pg * MH:(pg + 1) * MH], dp[:, pg * P:(pg + 1) * P], id16)
                pe.transpose(bank[6][0:NS, PAGES * MH:(PAGES + 1) * MH], dp[:, PAGES * P:NKEY], id16).then_inc(dpT_ready, 1)

            def weigh_pages(b, slot):
                after(pe, "pe", dpT_taken, b + 1)
                out = bank[7][0:MH, 0:LORA]
                for pg in range(PAGES):
                    pe.matmul(out, dpT[:, pg, :], cbuf[slot][:, pg, :], start=(pg == 0), stop=False)
                pe.matmul(out, dpT[0:NS, PAGES, :], ckvS[:, :], start=False, stop=True).then_inc(dpv_ready, 1)

            def turn_out(b):
                after(pe, "pe", dol_ready, b + 1)
                for c in range(2):
                    mm = pe.transpose(bank[6][:, c * MH:(c + 1) * MH], dol[:, c * P:(c + 1) * P], id16)
                mm.then_inc(dolT_ready, 1)

            id16 = cst[0:MH, C_ID:C_ID + MH]

            def token(b, slot, loads):
                behind = nonzero(b)
                after(pe, "pe", page_in[slot], 16 * PAGES * loads)
                after(pe, "pe", rot_in[slot], 16 * PAGES * loads)
                turn_pages(b, 0, slot)
                if behind:
                    score(b - 1, NQ - 1)
                    score_new(b - 1)
                turn_pages(b, 1, slot)
                after(pe, "pe", qst_ready, b + 1)
                score(b, 0)
                turn_pages(b, 2, slot)
                score(b, 1)
                if behind:
                    turn_probs(b - 1)
                turn_pages(b, 3, slot)
                if behind:
                    weigh_pages(b - 1, (slot + 2) % 3)
                score(b, 2)
                if behind:
                    turn_out(b - 1)

            token(0, 0, 1)
            with pe.Fori(0, (NS - 2) // 3) as i:
                for j in range(3):
                    token(3 * i + (j + 1), (j + 1) % 3, i + (1 + (j + 1) // 3))
            token(NS - 1, (NS - 1) % 3, (NS - 1) // 3 + 1)
            pe.wait_ge(ct_taken, NQ * NS)
            score(NS - 1, NQ - 1)
            score_new(NS - 1)
            turn_probs(NS - 1)
            weigh_pages(NS - 1, (NS - 1) % 3)
            turn_out(NS - 1)
            pe.wait_ge(dolT_taken, NS)
            for h in range(MH):
                for c in range(2):
                    mm = pe.matmul(bank[h // 8][0:NS, (h % 8) * VD:(h % 8 + 1) * VD], olT[:, c, h, :],
                                   w_ukv[:, c, h * 128 + NOPE:(h + 1) * 128], start=(c == 0), stop=(c == 1))
            mm.then_inc(os_ready, 1)

        qst = sb("qst", [P, 3, MH])
        qst_ready = sem("qst_ready")

        def pool_mla(pool):
            load_pages(pool, kbuf, cache_kpe, rot_in)

        def act_mla(act):
            act_turn(act, 3)
            for t, (t0, nt) in enumerate(TILES):
                act.wait_ge(kvq_ready, t + 1)
                act.activation(kvq[0:nt, t, 0:LORA + ROPE], bank[2 * t][0:nt, 0:LORA + ROPE], ACT.Copy)
                act.activation(kvq[0:nt, t, LORA + ROPE:WKVQ], bank[2 * t + 1][0:nt, 0:QLORA], ACT.Copy)
                act.activation(pr[0:nt, 0:2, :].rearrange("p a b -> p (a b)"), bank[2 * t][0:nt, 0:LORA], ACT.Square,
                               accum_out=std[0:nt, 2 * t:2 * t + 1])
                act.activation(pr[0:nt, 2:5, :].rearrange("p a b -> p (a b)"), bank[2 * t + 1][0:nt, 0:QLORA], ACT.Square,
                               accum_out=std[0:nt, 2 * t + 1:2 * t + 2])
                act.drain()
                for s, n in enumerate((LORA, QLORA)):
                    ins = act.activation(std[0:nt, 2 * t + s:2 * t + s + 1], std[0:nt, 2 * t + s:2 * t + s + 1], ACT.Sqrt,
                                         scale=1.0 / n, bias=cst[0:nt, C_EPS + 1:C_EPS + 2])
                act.drain()
                act.sem_inc(kvq_taken, 1)
            for t, (t0, nt) in enumerate(TILES):
                act.wait_ge(lt_ready, t + 1)
                act.activation(cqT[:, :, t0:t0 + nt], bank[6][:, 0:3 * P].rearrange("p (k s) -> p k s", k=3)[:, :, 0:nt], ACT.Copy)
                ins = act.activation(ckvT[:, :, t0:t0 + nt], bank[7][:, 0:2 * P].rearrange("p (k s) -> p k s", k=2)[:, :, 0:nt], ACT.Copy)
                if t == 2:
                    ins = act.activation(knT[:, :], bank[7][0:ROPE, 2 * P:2 * P + NS], ACT.Copy)
                ins.then_inc(lt_taken, 1)
            def take_queries(g):
                after(act, "act", q_ready, g + 1)
                for t, (t0, nt) in enumerate(TILES):
                    act.activation(qs[0:nt, t, :, :], bank[(0, 1, 7)[t]][0:nt, 0:HG * QD].rearrange("p (h n) -> p h n", h=HG), ACT.Copy)
                act.drain()
                act.sem_inc(q_taken, 1)

            def group(g, last):
                after(act, "act", kv_ready, g + 1)
                for t in range(2):
                    kv = bank[3 + t][:, :].rearrange("p (h n) -> p h n", h=HG)
                    act.activation(kf[:, t, :, 0:NOPE], kv[:, :, 0:NOPE], ACT.Copy)
                    ins = act.activation(vv[:, t, :, :], kv[:, :, NOPE:128], ACT.Copy)
                act.drain()
                act.sem_inc(kv_taken, 1)
                after(act, "act", qT_ready, g + 1)
                for t, b in ((0, 5), (1, 6)):
                    ins = act.activation(qfT[:, t, :, :], bank[b][0:QD, :].rearrange("p (h s) -> p h s", h=HG), ACT.Copy)
                ins.then_inc(qT_taken, 1)
                act.activation(qsT[:, :, :], bank[1][0:NOPE, 0:HG * NS].rearrange("p (h b) -> p h b", h=HG), ACT.Copy)
                act.activation(qpT[:, :, bass.ts(g, HG)], bank[1][0:ROPE, 64:64 + HG * NS].rearrange("p (h b) -> p b h", h=HG), ACT.Copy)
                after(act, "act", ukT_ready, g + 1)
                for c in range(2):
                    ins = act.activation(ukT[:, c, :, :], bank[2 + c][0:NOPE, :].rearrange("p (h l) -> p h l", h=HG), ACT.Copy)
                ins.then_inc(ukT_taken, 1)
                after(act, "act", qlat_ready, g + 1)
                for c in range(2):
                    ins = act.activation(qlT[:, c, :, bass.ts(g, HG)],
                                         bank[1][:, c * HG * NS:(c + 1) * HG * NS].rearrange("p (h b) -> p b h", h=HG), ACT.Copy)
                ins.then_inc(qlat_taken, 1)
                after(act, "act", sm_ready, g + 1)
                act.activation(pr, pr, ACT.Exp).then_inc(p_ready, 1)
                if not last:
                    take_queries(g + 1)
                after(act, "act", pT_ready, g + 1)
                for a in range(2):
                    ins = act.activation(pT[:, 4 * a:4 * a + 4, :], bank[2 + a][:, :].rearrange("p (a s) -> p a s", a=4), ACT.Copy)
                ins.then_inc(pT_taken, 1)

            take_queries(0)
            with act.Fori(0, NG - 1) as g:
                group(g, False)
            group(NG - 1, True)
            def take_pages(b, q):
                after(act, "act", ct_ready, NQ * b + q + 1)
                for c in range(2):
                    act.activation(cT[:, q % 2, c, :], bank[c][:, :], ACT.Copy)
                act.activation(kpT[:, q % 2, :], bank[2][0:ROPE, :], ACT.Copy).then_inc(ct_taken, 1)

            def exp_scores(b):
                after(act, "act", dm_ready, b + 1)
                act.activation(dp, dsc, ACT.Exp, scale=SCALE, bias=dneg[:, 0:1], accum_out=dsum[:, 0:1])
                act.drain()
                act.sem_inc(dp_ready, 1)

            for q in range(NQ):
                take_pages(0, q)
            with act.Fori(1, NS) as b:
                take_pages(b, 0)
                take_pages(b, 1)
                exp_scores(b - 1)
                take_pages(b, 2)
                take_pages(b, 3)
            exp_scores(NS - 1)
            act.wait_ge(os_ready, 1)
            for c in range(2):
                ins = act.activation(o_all[0:NS, 2, 512 * c:512 * c + 512], bank[c][0:NS, :], ACT.Copy)
            ins.then_inc(x_ready, 1)

        def rotate(dve, v, nt, t, heads):
            cos = bc(cst[0:nt, C_ROPE + 32 * t:C_ROPE + 32 * t + 16], 1, heads)
            sin_ = bc(cst[0:nt, C_ROPE + 32 * t + 16:C_ROPE + 32 * t + 32], 1, heads)
            a, b = v[:, :, 0:16], v[:, :, 16:32]
            r = rt[0:nt]
            for m, (p_, q_) in enumerate(((a, cos), (b, sin_), (b, cos), (a, sin_))):
                dve.tensor_tensor(r[:, m, 0:heads, :], p_, q_, ALU.mult)
            dve.drain()
            dve.tensor_tensor(a, r[:, 0, 0:heads, :], r[:, 1, 0:heads, :], ALU.subtract)
            dve.tensor_tensor(b, r[:, 2, 0:heads, :], r[:, 3, 0:heads, :], ALU.add)
            dve.drain()

        def dve_mla(dve):
            dve.wait_ge(wm_in, 16 * 4)
            for t, (t0, nt) in enumerate(TILES):
                dve.wait_ge(kvq_taken, t + 1)
                dve.reciprocal(rstd[0:nt, 2 * t:2 * t + 2], std[0:nt, 2 * t:2 * t + 2])
                dve.drain()
                for s, (c0, c1, g0) in enumerate(((0, LORA, 0), (LORA + ROPE, WKVQ, LORA))):
                    dve.scalar_tensor_tensor(kvq[0:nt, t, c0:c1], kvq[0:nt, t, c0:c1], rstd[0:nt, 2 * t + s:2 * t + s + 1],
                                             gkq[0:nt, g0:g0 + c1 - c0], ALU.mult, ALU.mult)
                rotate(dve, kvq[0:nt, t, LORA:LORA + ROPE].unsqueeze(1), nt, t, 1)
                if t < 2:
                    dve.tensor_copy(kf[:, t, :, NOPE:QD], bc(kvq[:, t, LORA:LORA + ROPE], 1, HG))
                else:
                    dve.tensor_copy(ckvS[:, :], kvq[0:NS, 2, 0:LORA])
                dve.drain()
                dve.sem_inc(kvq_norm, 1)
            dve.sem_inc(po_taken, 1)
            def own_queries(g):
                dve.tensor_copy(ukst, w_ukv.rearrange("p c (h n) -> p c h n", n=128)[:, :, bass.ts(g, HG), 0:NOPE]).then_inc(ukst_ready, 1)
                after(dve, "dve", q_taken, g + 1)
                for t, (t0, nt) in enumerate(TILES):
                    rotate(dve, qs[0:nt, t, :, NOPE:QD], nt, t, HG)
                dve.sem_inc(qrot_ready, 1)

            def group(g, last):
                after(dve, "dve", kT_ready, g + 1)
                for t, b in ((0, 7), (1, 0)):
                    ins = dve.tensor_copy(kfT[:, t, :, :], bank[b][0:QD, :].rearrange("p (h s) -> p h s", h=HG))
                ins.then_inc(kT_taken, 1)
                after(dve, "dve", s_ready, g + 1)
                own = bc(causal, 1, HG)
                dve.scalar_tensor_tensor(pr[:, 0:HG, :], bank[5][:, :].rearrange("p (h s) -> p h s", h=HG), SCALE, own,
                                         ALU.mult, ALU.add)
                for a in range(2):
                    s4 = bank[6 + a][:, :].rearrange("p (h t s) -> p h t s", h=2, t=2)
                    d4 = pr[:, HG + 4 * a:HG + 4 * a + 4, :].rearrange("p (h t) s -> p h t s", h=2)
                    dve.tensor_scalar(d4[:, :, 0, :], s4[:, :, 0, :], SCALE, None, ALU.mult)
                    dve.scalar_tensor_tensor(d4[:, :, 1, :], s4[:, :, 1, :], SCALE, bc(causal, 1, 2), ALU.mult, ALU.add)
                dve.drain()
                dve.sem_inc(s_taken, 1)
                p1 = pr[:, HG:12, :].rearrange("p (h t) s -> p h (t s)", t=2)
                dve.tensor_reduce(mx[:, 0, :], pr[:, 0:HG, :], AX, ALU.max)
                dve.tensor_reduce(mx[:, 1, :], p1, AX, ALU.max)
                dve.drain()
                dve.tensor_tensor(pr[:, 0:HG, :], pr[:, 0:HG, :], bc(mx[:, 0, :], 2, P), ALU.subtract)
                dve.tensor_tensor(p1, p1, bc(mx[:, 1, :], 2, 2 * P), ALU.subtract)
                dve.drain()
                dve.sem_inc(sm_ready, 1)
                after(dve, "dve", p_ready, g + 1)
                dve.tensor_reduce(sm[:, 0, :], pr[:, 0:HG, :], AX, ALU.add)
                dve.tensor_reduce(sm[:, 1, :], p1, AX, ALU.add)
                dve.drain()
                dve.reciprocal(sm[:, :, :], sm[:, :, :])
                after(dve, "dve", pT_ready, g + 1)
                dve.tensor_copy(pT[:, 8:12, :], bank[4][:, :].rearrange("p (a s) -> p a s", a=4)).then_inc(pT_taken, 1)
                dve.drain()
                if not last:
                    own_queries(g + 1)
                after(dve, "dve", po_ready, g + 1)
                for t in range(2):
                    dve.tensor_tensor(o_all[:, t, bass.ts(g, HG * VD)].rearrange("p (h v) -> p h v", h=HG),
                                      bank[5 + t][:, 0:HG * VD].rearrange("p (h v) -> p h v", h=HG),
                                      bc(sm[:, t, :], 2, VD), ALU.mult)
                dve.drain()
                dve.sem_inc(po_taken, 1)

            own_queries(0)
            with dve.Fori(0, NG - 1) as g:
                group(g, False)
            group(NG - 1, True)
            dve.sem_inc(x_ready, 2)

            def take_scores(b, q):
                after(dve, "dve", ds_ready, NQ * b + q + 1)
                s = bank[3 + q % 2][0:MH, :]
                dve.tensor_copy(dsc[:, 512 * q:512 * q + 512], s)
                dve.tensor_reduce(dmx[:, q:q + 1], s, AX, ALU.max).then_inc(ds_taken, 1)

            def maximum(b):
                dve.memset(dsc[:, PAGES * PAGE:NKEY], NEG)
                after(dve, "dve", dn_ready, b + 1)
                dve.drain()
                dve.tensor_copy(dsc[:, bass.ds(b + PAGES * PAGE, 1)], bank[5][0:MH, bass.ds(b, 1)])
                dve.tensor_copy(dmx[:, NQ:NQ + 1], bank[5][0:MH, bass.ds(b, 1)])
                dve.drain()
                dve.tensor_reduce(dneg[:, :], dmx[:, :], AX, ALU.max)
                dve.drain()
                dve.tensor_scalar(dneg[:, :], dneg[:, :], -SCALE, None, ALU.mult)
                dve.drain()
                dve.sem_inc(dm_ready, 1)

            def take_probs(b):
                after(dve, "dve", dpT_ready, b + 1)
                dve.tensor_copy(dpT[:, 0:PAGES, :], bank[6][:, 0:PAGES * MH].rearrange("p (g h) -> p g h", g=PAGES))
                dve.tensor_copy(dpT[0:NS, PAGES, :], bank[6][0:NS, PAGES * MH:(PAGES + 1) * MH])
                dve.reciprocal(drs[:, :], dsum[:, :])
                dve.drain()
                dve.sem_inc(dpT_taken, 1)

            def normalise(b):
                after(dve, "dve", dpv_ready, b + 1)
                dve.tensor_scalar(dol, bank[7][0:MH, 0:LORA], drs[:, 0:1], None, ALU.mult).then_inc(dol_ready, 1)

            def take_out(b):
                after(dve, "dve", dolT_ready, b + 1)
                dve.tensor_copy(olT[:, :, :, bass.ds(b, 1)].rearrange("p c h b -> p c (h b)"),
                                bank[6][:, 0:2 * MH].rearrange("p (c h) -> p c h", c=2))
                dve.drain()
                dve.sem_inc(dolT_taken, 1)

            def queries(b):
                dve.tensor_copy(qst[:, 0:2, :], qlT[:, :, bass.ds(b, 1), :].rearrange("p c b h -> p c (b h)"))
                dve.tensor_copy(qst[0:ROPE, 2, :], qpT[:, bass.ds(b, 1), :].rearrange("p b h -> p (b h)"))
                dve.drain()
                dve.sem_inc(qst_ready, 1)

            dve.wait_ge(qlat_taken, NG)
            queries(0)
            for q in range(NQ - 1):
                take_scores(0, q)
            with dve.Fori(1, NS) as b:
                take_scores(b - 1, NQ - 1)
                maximum(b - 1)
                queries(b)
                after(dve, "dve", dp_ready, b)
                take_scores(b, 0)
                take_scores(b, 1)
                take_probs(b - 1)
                normalise(b - 1)
                take_scores(b, 2)
                take_out(b - 1)
            take_scores(NS - 1, NQ - 1)
            maximum(NS - 1)
            take_probs(NS - 1)
            normalise(NS - 1)
            take_out(NS - 1)

        block = ctx.enter_context(nc.Block())

        @block.sync
        def _(sp):
            sp_hgrn(sp)
            sp_ln(sp, 0)
            sp_peer(sp, 0)
            sp_ln(sp, 1)
            sp_mla(sp)
            sp_ln(sp, 2)
            sp_peer(sp, 1)
            sp_ln(sp, 3)
            for t, (t0, nt) in enumerate(TILES):
                sp.wait_ge(x_ready, 15 + t + 1)
                dst = y_prompt[0, t0:t0 + nt, :] if t < 2 else y_sample.rearrange("b t d -> (b t) d")
                sp.dma_start(dst, x[0:nt, t, :]).then_inc(stored, 16)
            sp.wait_ge(stored, 144)
            for j in range(2):
                sp.wait_ge(st_out[j], 32 * (HH // 2 + 1))

        @block.tensor
        def _(pe):
            pe_hgrn(pe)
            pe_join(pe, 0)
            pe_peer(pe, 0)
            pe_mla(pe)
            pe_join(pe, 1)
            pe_peer(pe, 1)

        @block.scalar
        def _(act):
            act_hgrn(act)
            act_turn(act, 1)
            act_ln(act, 0)
            act_peer(act, 0)
            act_ln(act, 1)
            act_mla(act)
            act_turn(act, 4)
            act_ln(act, 2)
            act_peer(act, 1)
            act_ln(act, 3)

        @block.gpsimd
        def _(pool):
            pool.sem_inc(st_out[0], 32)
            pool.sem_inc(st_out[1], 32)
            pool_hgrn(pool)
            pool_peer(pool, 0)
            pool_mla(pool)
            pool_peer(pool, 1)

        @block.vector
        def _(dve):
            dve_hgrn(dve)
            dve_ln(dve, 0)
            dve_peer(dve, 0)
            dve_ln(dve, 1)
            dve_mla(dve)
            dve_ln(dve, 2)
            dve_peer(dve, 1)
            dve_ln(dve, 3)


_INS = ['x_prompt', 'x_sample', 'state_hgrn', 'cache_ckv', 'cache_kpe', 'page_table',
        'hgrn_w_in', 'hgrn_lb_logits', 'hgrn_norm_g', 'hgrn_w_out',
        'mla_w_dkv', 'mla_kv_norm_g', 'mla_w_ukv', 'mla_w_dq', 'mla_q_norm_g', 'mla_w_uq', 'mla_w_o',
        'peer_w_q', 'peer_k1', 'peer_k2', 'peer_u', 'peer_v', 'ln_g', 'ln_b']
_OUTS = [(1, 256, 1024), (8, 1, 1024), (1, 1, 8, 128, 128), (1, 8, 8, 128, 128),
         (1, 256, 256), (1, 256, 32), (8, 1, 256), (8, 1, 32)]


def kernel(**inputs):
    import numpy as _np
    import concourse.bacc as _bacc
    from concourse import mybir as _mybir
    from concourse.bass_utils import run_bass_kernel_spmd as _run

    nc = _bacc.Bacc("TRN2", target_bir_lowering=False, num_devices=1)
    c, lev = shape_constants(_np)
    arrays = {"in_consts": c, "in_levels": lev}
    for name in _INS:
        a = _np.ascontiguousarray(inputs[name])
        if name in ("peer_u", "peer_v"):
            a = a.reshape(-1, a.shape[-1])
        arrays[f"in_{name}"] = a
    args = [nc.dram_tensor(n, a.shape, _mybir.dt.from_np(a.dtype), kind="ExternalInput").ap()
            for n, a in arrays.items()]
    for i, shape in enumerate(_OUTS):
        args.append(nc.dram_tensor(f"out_{i}", shape, _mybir.dt.float32, kind="ExternalOutput").ap())
    trunk_kernel(nc, *args)
    r = _run(nc, [arrays], core_ids=[0])
    return tuple(r.results[0][f"out_{i}"] for i in range(len(_OUTS)))
```

```python
from contextlib import ExitStack

import concourse.bass as bass
from concourse import mybir

F32 = mybir.dt.float32
I32 = mybir.dt.int32
U32 = mybir.dt.uint32
ALU = mybir.AluOpType
ACT = mybir.ActivationFunctionType
AX = mybir.AxisListType.X

P = 128
D = 1024
KO = D // P
NS = 8
NT = 2 * P + NS
TILES = ((0, P), (P, P), (2 * P, NS))
HH = 8
NLEV = 7
TOPK = 16
NKEYS = 128
NEXP = NKEYS * NKEYS
MH = 16
NOPE, ROPE, VD = 64, 32, 64
QD = NOPE + ROPE
LORA, QLORA = 256, 384
SCALE = float(QD) ** -0.5
HG = 4
NG = MH // HG
PAGES = 16
PAGE = 128
RING = 8
ALPHA = 4.0 ** 0.25
LN_EPS, RMS_EPS = 1e-5, 1e-6
NEG = -1e30
SCRATCH = 9216

C_ID, C_AID, C_CAUSAL, C_EYE8, C_BLK, C_IOTA, C_KEYM, C_BLKT, C_ROPE, C_EPS, C_ONE, C_SEL = (
    0, 128, 256, 384, 448, 456, 472, 480, 608, 704, 706, 834)
C_W = C_SEL + 16


def shape_constants(np):
    c = np.zeros((P, C_W), np.float32)
    p = np.arange(P)
    c[p, C_ID + p] = 1.0
    c[p, C_AID + p] = ALPHA
    c[:, C_CAUSAL:C_CAUSAL + P] = np.where(p[None, :] <= p[:, None], 0.0, NEG)
    c[:, C_EYE8:C_EYE8 + 64] = np.eye(NS, dtype=np.float32).reshape(1, 64)
    c[:, C_BLK:C_BLK + NS] = p[:, None] // TOPK == np.arange(NS)[None, :]
    c[:, C_IOTA:C_IOTA + TOPK] = np.arange(TOPK)[None, :]
    c[:NS, C_KEYM:C_KEYM + NS] = np.where(np.eye(NS) > 0, 0.0, NEG)
    c[:NS, C_BLKT:C_BLKT + P] = p[None, :] // TOPK == np.arange(NS)[:, None]
    inv = np.float32(10000.0) ** (-np.arange(ROPE // 2, dtype=np.float32) / np.float32(ROPE // 2))
    for t in range(3):
        pos = (p + P * t) if t < 2 else np.full(P, PAGES * PAGE)
        ang = pos.astype(np.float32)[:, None] * inv[None, :].astype(np.float32)
        c[:, C_ROPE + 32 * t:C_ROPE + 32 * t + 16] = np.cos(ang)
        c[:, C_ROPE + 32 * t + 16:C_ROPE + 32 * t + 32] = np.sin(ang)
    c[:, C_EPS] = LN_EPS
    c[:, C_EPS + 1] = RMS_EPS
    c[:, C_ONE:C_ONE + P] = 1.0
    c[:, C_SEL:C_SEL + TOPK] = p[:, None] % TOPK == np.arange(TOPK)[None, :]
    lev = np.zeros((P, NLEV, P), np.int32)
    x = p[:, None] ^ p[None, :]
    for l in range(NLEV):
        lev[:, l] = (p[:, None] < p[None, :]) & (x >= 1 << l) & (x < 2 << l)
    return c, lev.reshape(P, NLEV * P)


def bc(ap, axis, n):
    ap = ap.unsqueeze(axis)
    shape = list(ap.shape)
    shape[axis] = n
    return ap.broadcast_to(shape)


def trunk_kernel(nc, consts, level_masks, x_prompt, x_sample, state_hgrn, cache_ckv, cache_kpe, page_table,
                 hgrn_w_in, hgrn_lb_logits, hgrn_norm_g, hgrn_w_out,
                 mla_w_dkv, mla_kv_norm_g, mla_w_ukv, mla_w_dq, mla_q_norm_g, mla_w_uq, mla_w_o,
                 peer_w_q, peer_k1, peer_k2, peer_u, peer_v, ln_g, ln_b,
                 y_prompt, y_sample, st_prompt, st_sample, ckv_prompt, kpe_prompt, ckv_sample, kpe_sample):
    with ExitStack() as ctx:
        def sb(name, shape, dt=F32):
            return ctx.enter_context(nc.sbuf_tensor(name, shape, dt))

        def sem(name):
            return ctx.enter_context(nc.semaphore(name))

        cst = sb("cst", [P, C_W])
        ident = cst[:, C_ID:C_ID + P]
        causal = cst[:, C_CAUSAL:C_CAUSAL + P]
        eye8 = cst[:, C_EYE8:C_EYE8 + 64].rearrange("p (b c) -> p b c", b=NS)
        blk = cst[:, C_BLK:C_BLK + NS]
        iota = cst[:, C_IOTA:C_IOTA + TOPK]
        ones = cst[:, C_ONE:C_ONE + P]
        x = sb("x", [P, 3, D])
        xT = sb("xT", [P, KO, NT])
        o_all = sb("o_all", [P, 3, D])
        g_all = sb("g_all", [P, 3, D])
        wbig = sb("wbig", [P, KO, D])
        lnw = sb("lnw", [P, 2, D])
        stats = sb("stats", [P, 2, 6])
        mv = sb("mv", [P, 2])
        std = sb("std", [P, MH])
        rstd = sb("rstd", [P, MH])
        arena = sb("arena", [P, 16384])

        bank = [ctx.enter_context(nc.psum_tensor(f"bank{i}", [P, 512], F32)) for i in range(8)]

        consts_in = sem("consts_in")
        x_in = sem("x_in")
        x_ready = sem("x_ready")
        turn_ready = sem("turn_ready")
        turn_taken = sem("turn_taken")
        y_ready = sem("y_ready")
        y_free = sem("y_free")
        stat_ready = sem("stat_ready")
        std_ready = sem("std_ready")
        lnw_in = sem("lnw_in")
        wbig_in = sem("wbig_in")
        passed = {e: sem(f"{e}_passed") for e in ("pe", "act", "dve", "pool", "sp")}
        stored = sem("stored")

        def ybank(t, c, nt):
            return bank[2 * t + c][0:nt, :]

        def nonzero(n):
            return not (isinstance(n, int) and n == 0)

        def after(eng, name, s, value):
            eng.wait_ge(s, value)
            eng.sem_inc(passed[name], 1)

        A = arena
        def view(off, shape):
            n = 1
            for s in shape:
                n *= s
            v = A[:, off:off + n]
            if len(shape) == 2:
                v = v.rearrange("p (a b) -> p a b", a=shape[0])
            elif len(shape) == 3:
                v = v.rearrange("p (a b c) -> p a b c", a=shape[0], b=shape[1])
            return v, off + n

        off = 0
        wh, sin, snew, kk, qq, iT, gT, stf = [], [], [], [], [], [], [], []
        for j in range(2):
            v, off = view(off, [KO, 4, P]); wh.append(v)
        for j in range(2):
            v, off = view(off, [NS, P]); sin.append(v)
            v, off = view(off, [NS, P]); snew.append(v)
        for j in range(2):
            for lst in (kk, qq, iT, gT):
                v, off = view(off, [NT]); lst.append(v)
            v, off = view(off, [P]); stf.append(v)
        ksg, off = view(off, [NT])
        sgp, off = view(off, [NT])
        lf, off = view(off, [NT])
        assert off <= 16384, off
        scratch = sb("scratch", [P, SCRATCH])
        soff = [0]

        def sview(n, dt=None):
            v = scratch[:, soff[0]:soff[0] + n]
            soff[0] += n
            assert soff[0] <= SCRATCH
            return v.bitcast(dt) if dt else v

        bb = sview(2 * P)
        lev = sview(NLEV * 2 * P).rearrange("p (l t) -> p l t", l=NLEV)
        lmask = sview(NLEV * P, I32).rearrange("p (l t) -> p l t", l=NLEV)
        kdec = sview(2 * P)
        kd = sview(2 * P)
        qe = [sview(P) for j in range(2)]
        eb = sview(P)
        glast = [sview(1) for j in range(2)]
        ffs = [sview(NS) for j in range(2)]
        tr = sview(4 * P).rearrange("p (a s) -> p a s", a=4)
        ts_ = sview(2 * P).rearrange("p (a s) -> p a s", a=2)[0:NS]
        vm = sview(NS * P).rearrange("p (a s) -> p a s", a=NS)[0:NS]
        qm = [sview(NS * NS).rearrange("p (a s) -> p a s", a=NS) for j in range(2)]
        att = sview(2 * P).rearrange("p (a s) -> p a s", a=2)
        st0 = sview(P)
        lbl = sb("lbl", [2 * HH, P])
        lbe = sb("lbe", [P, 2, HH])
        lbs = sb("lbs", [P, HH])
        lb = sb("lb", [P, HH])
        omlb = sb("omlb", [P, HH])

        wh_in = [sem(f"wh_in{j}") for j in range(2)]
        sin_in = [sem(f"sin_in{j}") for j in range(2)]
        lb_in = sem("lb_in")
        lbT_ready = sem("lbT_ready")
        lb_max = sem("lb_max")
        lb_exp = sem("lb_exp")
        omlb_ready = sem("omlb_ready")
        proj_ready = sem("proj_ready")
        proj_taken = sem("proj_taken")
        f_ready = sem("f_ready")
        lf_ready = sem("lf_ready")
        b_ready = sem("b_ready")
        lev_ready = sem("lev_ready")
        levd_ready = sem("levd_ready")
        e_ready = sem("e_ready")
        xlev_ready = sem("xlev_ready")
        tr_ready = sem("tr_ready")
        tr_taken = sem("tr_taken")
        vm_ready = sem("vm_ready")
        att_ready = sem("att_ready")
        s0_ready = sem("s0_ready")
        st0_ready = sem("st0_ready")
        outer_ready = sem("outer_ready")
        fs_ready = sem("fs_ready")
        snew_ready = sem("snew_ready")
        o_ready = sem("o_ready")
        o_taken = sem("o_taken")
        sp_ready = sem("sp_ready")
        st_out = [sem(f"st_out{j}") for j in range(2)]
        hnorm_in = sem("hnorm_in")
        hss_ready = sem("hss_ready")
        hstd_ready = sem("hstd_ready")
        silu_ready = sem("silu_ready")

        w_in_v = hgrn_w_in[0].rearrange("(ko ki) (c h n) -> ki ko c h n", ki=P, c=4, h=HH)
        s_in_v = state_hgrn[0].rearrange("b h k v -> h k b v")
        s_out_v = st_sample[0].rearrange("b h k v -> h k b v")

        def head_pairs(body):
            def run(eng):
                with eng.Fori(0, HH // 2 - 1) as i:
                    for j in range(2):
                        body(i, j, False)
                for j in range(2):
                    body(HH // 2 - 1, j, True)
            return run

        def head_pairs_first(body):
            def run(eng):
                for j in range(2):
                    body(0, j, False, first=(j == 0))
                with eng.Fori(1, HH // 2 - 1) as i:
                    for j in range(2):
                        body(i, j, False)
                for j in range(2):
                    body(HH // 2 - 1, j, True)
            return run

        def sp_hgrn(sp):
            sp.dma_start(cst[:, :], consts).then_inc(consts_in, 16)
            sp.dma_start(lmask[:, :, :].rearrange("p a b -> p (a b)"), level_masks).then_inc(consts_in, 16)
            sp.dma_start(x[:, 0, :], x_prompt[0, 0:P, :]).then_inc(x_in, 16)
            sp.dma_start(x[:, 1, :], x_prompt[0, P:2 * P, :]).then_inc(x_in, 16)
            sp.dma_start(x[0:NS, 2, :], x_sample.rearrange("b t d -> (b t) d")).then_inc(x_in, 16)
            sp.dma_start(lbl[:, :], hgrn_lb_logits.rearrange("r (h k) -> (r h) k", h=HH)).then_inc(lb_in, 16)

            def load_head(h, j):
                for c in range(4):
                    sp.dma_start(wh[j][:, :, c, :], w_in_v[:, :, c, h, :]).then_inc(wh_in[j], 16)
                sp.dma_start(sin[j], s_in_v[h]).then_inc(sin_in[j], 16)
            load_head(0, 0)
            load_head(1, 1)
            sp.dma_start(lnw[:, 1, :], hgrn_norm_g.rearrange("l h v -> l (h v)").broadcast_to([P, D])).then_inc(hnorm_in, 16)
            sp.dma_start(wbig[:, :, :], hgrn_w_out[0].rearrange("(k p) n -> p k n", p=P)).then_inc(wbig_in, 16)

            def body(i, j, last):
                n = 2 * i + j
                if not last:
                    after(sp, "sp", proj_ready, 4 * n + 4)
                    after(sp, "sp", fs_ready, n + 1)
                    load_head(n + 2, j)
                after(sp, "sp", snew_ready, n + 1)
                sp.dma_start(s_out_v[n], snew[j]).then_inc(st_out[j], 16)
                after(sp, "sp", sp_ready, n + 1)
                sp.dma_start(st_prompt[0, 0, n], stf[j]).then_inc(st_out[j], 16)
            head_pairs(body)(sp)

        def pe_hgrn(pe):
            pe.wait_ge(consts_in, 32)
            pe.wait_ge(lb_in, 16)
            pe.transpose(bank[2][:, 0:2 * HH], lbl[:, :], cst[0:2 * HH, C_ID:C_ID + 2 * HH]).then_inc(lbT_ready, 1)

            def project(i, j, nxt):
                n = 2 * i + j
                after(pe, "pe", wh_in[j], 64 * (i + 1))
                for g, c in enumerate((1, 0, 2, 3)):
                    if not (nxt == "first" and g < 2):
                        after(pe, "pe", proj_taken, 4 * n + g - 1)
                    for k in range(KO):
                        mm = pe.matmul(bank[g % 2][:, 0:NT], wh[j][:, k, c, :], xT[:, k, :],
                                       start=(k == 0), stop=(k == KO - 1))
                    mm.then_inc(proj_ready, 1)

            def scores(j, levels):
                for l in levels:
                    for t in range(2):
                        cols = slice(t * P, (t + 1) * P)
                        left = kk[j][:, cols] if l == 0 else lev[:, l - 1, cols]
                        right = qq[j][:, cols] if l == 0 else lev[:, l - 1, cols]
                        mm = pe.matmul(bank[4 + l // 2][:, (l % 2) * 256 + t * P:(l % 2) * 256 + (t + 1) * P],
                                       left, right, start=True, stop=True)
                return mm

            for t in range(3):
                pe_turn(pe, 0, t)
            pe.wait_ge(turn_taken, 6)
            project(0, 0, "first")

            def body(i, j, last):
                n = 2 * i + j
                after(pe, "pe", proj_taken, 4 * n + 4)
                after(pe, "pe", xlev_ready, n + 1)
                after(pe, "pe", snew_taken, n + 1)
                scores(j, range(4))
                after(pe, "pe", o_taken, n + 1)
                after(pe, "pe", sp_taken, n + 1)
                for t in range(2):
                    pe.transpose(bank[2][:, t * P:(t + 1) * P], iT[j][:, t * P:(t + 1) * P], ident)
                    pe.transpose(bank[2][:, (2 + t) * P:(3 + t) * P], kd[:, t * P:(t + 1) * P], ident)
                pe.transpose(bank[3][0:NS, 0:P], kk[j][:, 2 * P:NT], ident)
                pe.transpose(bank[3][0:NS, P:2 * P], iT[j][:, 2 * P:NT], ident)
                pe.transpose(bank[3][0:NS, 2 * P:3 * P], gT[j][:, 2 * P:NT], ident)
                pe.transpose(bank[3][:, 3 * P:4 * P], gT[j][:, 0:P], ident).then_inc(tr_ready, 1)
                scores(j, range(4, NLEV + 1)).then_inc(att_ready, 1)
                if j == 0:
                    project(i, 1, "")
                elif not last:
                    project(i + 1, 0, "")
                after(pe, "pe", tr_taken, n + 1)
                pe.matmul(bank[2][:, 0:P], tr[:, 2, :], tr[:, 0, :], start=True, stop=True)
                pe.matmul(bank[2][:, P:2 * P], tr[:, 3, :], tr[:, 1, :], start=True, stop=True).then_inc(s0_ready, 1)
                after(pe, "pe", vm_ready, n + 1)
                for c in range(2):
                    mm = pe.matmul(bank[4 + c][:, :], ts_[:, 0, :], vm[:, 4 * c:4 * c + 4, :],
                                   start=True, stop=True)
                mm.then_inc(outer_ready, 1)
                pe.transpose(bank[3][:, 0:P], gT[j][:, P:2 * P], ident)
                pe.matmul(bank[6][:, 0:P], att[:, 0, :], tr[:, 0, :], start=True, stop=True)
                after(pe, "pe", st0_ready, n + 1)
                pe.matmul(bank[6][:, P:2 * P], att[:, 1, :], tr[:, 1, :], start=True, stop=False)
                pe.matmul(bank[6][:, P:2 * P], qe[j], st0[:, :], start=False, stop=True)
                after(pe, "pe", snew_taken, n + 2)
                for b in range(NS):
                    mm = pe.matmul(bank[3][0:NS, P:2 * P], qm[j][:, b, :], snew[j][:, b, :],
                                   start=(b == 0), stop=(b == NS - 1))
                mm.then_inc(o_ready, 1)
            head_pairs(body)(pe)

        snew_taken = sem("snew_taken")
        sp_taken = sem("sp_taken")

        def act_hgrn(act):
            act.wait_ge(lb_max, 1)
            act.activation(lbe[:, :, :], lbe[:, :, :], ACT.Exp).then_inc(lb_exp, 1)
            for t in range(3):
                act_turn(act, 0, t)
            act.sem_inc(o_taken, 1)

            def gates(i, j, first):
                n = 2 * i + j
                after(act, "act", proj_ready, 4 * n + 1)
                act.activation(ksg, bank[0][:, 0:NT], ACT.Sigmoid, scale=-1.0)
                act.activation(sgp, bank[0][:, 0:NT], ACT.Sigmoid).then_inc(proj_taken, 1)
                act.drain()
                act.activation(lf, sgp, ACT.Ln, scale=omlb[:, bass.ds(n, 1)], bias=lb[:, bass.ds(n, 1)]).then_inc(lf_ready, 1)
                after(act, "act", proj_ready, 4 * n + 2)
                act.activation(qq[j], bank[1][:, 0:NT], ACT.Copy).then_inc(proj_taken, 1)
                after(act, "act", b_ready, n + 1)
                act.activation(eb[:, :], bb[:, P:2 * P], ACT.Exp)
                act.activation(glast[j], bb[:, 2 * P - 1:2 * P], ACT.Exp)
                for t in range(2):
                    act.activation(kdec[:, t * P:(t + 1) * P], bb[:, t * P:(t + 1) * P], ACT.Exp,
                                   scale=-1.0, bias=bb[:, (t + 1) * P - 1:(t + 1) * P])
                after(act, "act", proj_ready, 4 * n + 3)
                act.activation(iT[j], bank[0][:, 0:NT], ACT.Copy).then_inc(proj_taken, 1)
                after(act, "act", lev_ready, n + 1)
                after(act, "act", levd_ready, n + 1)
                act.activation(lev[:, :, :], lev[:, :, :], ACT.Exp).then_inc(e_ready, 1)
                after(act, "act", proj_ready, 4 * n + 4)
                act.activation(gT[j], bank[1][:, 0:NT], ACT.Copy).then_inc(proj_taken, 1)
            act.wait_ge(omlb_ready, 1)
            gates(0, 0, True)

            def body(i, j, last):
                n = 2 * i + j
                after(act, "act", tr_ready, n + 1)
                act.activation(tr[:, :, :].rearrange("p a b -> p (a b)"), bank[2][:, :], ACT.Copy)
                act.activation(ts_[:, :, :].rearrange("p a b -> p (a b)"), bank[3][0:NS, 0:2 * P], ACT.Copy)
                act.activation(g_all[0:NS, 2, bass.ts(n, P)], bank[3][0:NS, 2 * P:3 * P], ACT.Copy)
                act.activation(g_all[:, 0, bass.ts(n, P)], bank[3][:, 3 * P:4 * P], ACT.Copy).then_inc(tr_taken, 1)
                if j == 0:
                    gates(i, 1, False)
                elif not last:
                    gates(i + 1, 0, False)
                after(act, "act", s0_ready, n + 1)
                act.activation(st0[:, :], bank[2][:, 0:P], ACT.Copy).then_inc(st0_ready, 1)
                after(act, "act", o_ready, n + 1)
                act.activation(o_all[:, 0, bass.ts(n, P)], bank[6][:, 0:P], ACT.Copy)
                act.activation(o_all[:, 1, bass.ts(n, P)], bank[6][:, P:2 * P], ACT.Copy)
                act.activation(g_all[:, 1, bass.ts(n, P)], bank[3][:, 0:P], ACT.Copy)
                act.activation(o_all[0:NS, 2, bass.ts(n, P)], bank[3][0:NS, P:2 * P], ACT.Copy).then_inc(o_taken, 1)
            head_pairs(body)(act)
            act.drain()
            for t, (t0, nt) in enumerate(TILES):
                act.activation(g_all[0:nt, t, :], g_all[0:nt, t, :], ACT.Silu).then_inc(silu_ready, 1)
            for t, (t0, nt) in enumerate(TILES):
                act.wait_ge(hss_ready, t + 1)
                act.activation(std[0:nt, 0:HH], std[0:nt, 0:HH], ACT.Sqrt, scale=1.0 / P,
                               bias=cst[0:nt, C_EPS + 1:C_EPS + 2]).then_inc(hstd_ready, 1)
                if t == 0:
                    act_turn(act, 1, 0)

        POOL_LEVELS = 2

        def level_decays(eng, levels):
            for l in levels:
                half = 1 << (l - 1)
                b4 = bb[:, :].rearrange("p (n two s) -> p n two s", two=2, s=half)
                d4 = lev[:, l - 1, :].rearrange("p (n two s) -> p n two s", two=2, s=half)
                ref = bc(b4[:, :, 0, half - 1], 2, half)
                eng.tensor_tensor(d4[:, :, 0, :], ref, b4[:, :, 0, :], ALU.subtract)
                eng.tensor_tensor(d4[:, :, 1, :], b4[:, :, 1, :], ref, ALU.subtract)
            eng.drain()

        def pool_hgrn(pool):
            def body(i, j, last):
                n = 2 * i + j
                after(pool, "pool", b_ready, n + 1)
                level_decays(pool, range(1, POOL_LEVELS + 1))
                pool.sem_inc(lev_ready, 1)
                after(pool, "pool", sin_in[j], 16 * (i + 1))
                after(pool, "pool", st_slot[j], 32 * (i + 1))
                pool.tensor_tensor(snew[j], sin[j], bc(ffs[j], 2, P), ALU.mult).then_inc(fs_ready, 1)
            head_pairs(body)(pool)

        st_slot = st_out

        def dve_hgrn(dve):
            dve.wait_ge(lbT_ready, 1)
            dve.tensor_copy(lbe[:, :, :], bank[2][:, 0:2 * HH].rearrange("p (r h) -> p r h", r=2))
            dve.drain()
            dve.tensor_tensor(lbs[:, :], lbe[:, 0, :], lbe[:, 1, :], ALU.max)
            dve.drain()
            dve.tensor_tensor(lbe[:, :, :], lbe[:, :, :], bc(lbs[:, :], 1, 2), ALU.subtract).then_inc(lb_max, 1)
            dve.wait_ge(lb_exp, 1)
            dve.tensor_tensor(lbs[:, :], lbe[:, 0, :], lbe[:, 1, :], ALU.add)
            dve.drain()
            dve.reciprocal(lbs[:, :], lbs[:, :])
            dve.drain()
            dve.tensor_tensor(lb[:, :], lbe[:, 0, :], lbs[:, :], ALU.mult)
            dve.drain()
            dve.tensor_scalar(omlb[:, :], lb[:, :], -1.0, 1.0, ALU.mult, ALU.add).then_inc(omlb_ready, 1)
            dve.drain()
            dve.sem_inc(snew_taken, 1)
            dve.sem_inc(sp_taken, 1)

            def gates(i, j):
                n = 2 * i + j
                after(dve, "dve", proj_taken, 4 * n + 1)
                dve.tensor_scalar(kk[j], ksg, omlb[:, bass.ds(n, 1)], None, ALU.mult)
                dve.tensor_scalar(ffs[j], sgp[:, 2 * P:NT], omlb[:, bass.ds(n, 1)], lb[:, bass.ds(n, 1)],
                                  ALU.mult, ALU.add).then_inc(f_ready, 1)
                after(dve, "dve", lf_ready, n + 1)
                for t in range(2):
                    dve.tensor_tensor_scan(bb[:, t * P:(t + 1) * P], ones, lf[:, t * P:(t + 1) * P], 0.0,
                                                 ALU.mult, ALU.add)
                dve.drain()
                dve.sem_inc(b_ready, 1)
                level_decays(dve, range(POOL_LEVELS + 1, NLEV + 1))
                dve.sem_inc(levd_ready, 1)
                after(dve, "dve", proj_taken, 4 * n + 2)
                after(dve, "dve", e_ready, n + 1)
                for l in range(1, NLEV + 1):
                    half = 1 << (l - 1)
                    e4 = lev[:, l - 1, :].rearrange("p (n two s) -> p n two s", two=2, s=half)
                    k4 = kk[j][:, 0:2 * P].rearrange("p (n two s) -> p n two s", two=2, s=half)
                    q4 = qq[j][:, 0:2 * P].rearrange("p (n two s) -> p n two s", two=2, s=half)
                    dve.tensor_tensor(e4[:, :, 0, :], e4[:, :, 0, :], k4[:, :, 0, :], ALU.mult)
                    dve.tensor_tensor(e4[:, :, 1, :], e4[:, :, 1, :], q4[:, :, 1, :], ALU.mult)
                dve.tensor_tensor(qm[j], bc(qq[j][:, 2 * P:NT], 1, NS), eye8, ALU.mult)
                dve.tensor_tensor(qe[j], qq[j][:, P:2 * P], eb[:, :], ALU.mult)
                dve.tensor_tensor(kd[:, :], kk[j][:, 0:2 * P], kdec[:, :], ALU.mult)
                dve.drain()
                dve.sem_inc(xlev_ready, 1)
            gates(0, 0)

            def body(i, j, last):
                n = 2 * i + j
                after(dve, "dve", att_ready, n + 1)
                dve.tensor_tensor(att[:, :, :], bank[4][:, 0:256].rearrange("p (t s) -> p t s", t=2),
                                  bc(ident, 1, 2), ALU.mult)
                for l in range(1, NLEV + 1):
                    dve.drain()
                    for t in range(2):
                        dve.copy_predicated(att[:, t, :], lmask[:, l - 1, :],
                                            bank[4 + l // 2][:, (l % 2) * 256 + t * P:(l % 2) * 256 + (t + 1) * P])
                after(dve, "dve", tr_taken, n + 1)
                dve.tensor_tensor(vm[:, :, :], bc(ts_[:, 1, :], 1, NS), bc(ident[0:NS, 0:NS], 2, P),
                                  ALU.mult)
                dve.drain()
                dve.sem_inc(vm_ready, 1)
                if j == 0:
                    gates(i, 1)
                elif not last:
                    gates(i + 1, 0)
                after(dve, "dve", outer_ready, n + 1)
                after(dve, "dve", fs_ready, n + 1)
                for c in range(2):
                    dve.tensor_tensor(snew[j][:, 4 * c:4 * c + 4, :], snew[j][:, 4 * c:4 * c + 4, :],
                                      bank[4 + c][:, :].rearrange("p (b v) -> p b v", b=4), ALU.add)
                dve.drain()
                dve.sem_inc(snew_ready, 1)
                dve.sem_inc(snew_taken, 1)
                after(dve, "dve", st0_ready, n + 1)
                after(dve, "dve", st_slot[j], 32 * (i + 1))
                dve.scalar_tensor_tensor(stf[j], st0[:, :], glast[j], bank[2][:, P:2 * P],
                                         ALU.mult, ALU.add)
                dve.drain()
                dve.sem_inc(sp_ready, 1)
                dve.sem_inc(sp_taken, 1)
            head_pairs(body)(dve)
            dve.wait_ge(o_taken, HH + 1)
            dve.wait_ge(hnorm_in, 16)
            sq = arena[:, 0:D]
            for t, (t0, nt) in enumerate(TILES):
                o = o_all[0:nt, t, :]
                o3 = o.rearrange("p (h v) -> p h v", h=HH)
                dve.tensor_tensor(sq[0:nt, :], o, o, ALU.mult)
                dve.drain()
                dve.tensor_reduce(std[0:nt, 0:HH], sq[0:nt, :].rearrange("p (h v) -> p h v", h=HH), AX,
                                  ALU.add).then_inc(hss_ready, 1)
                dve.tensor_tensor(o, o, lnw[0:nt, 1, :], ALU.mult)
                dve.wait_ge(hstd_ready, t + 1)
                dve.reciprocal(rstd[0:nt, 0:HH], std[0:nt, 0:HH])
                dve.drain()
                dve.tensor_tensor(o3, o3, bc(rstd[0:nt, 0:HH], 2, P), ALU.mult)
                dve.drain()
                dve.wait_ge(silu_ready, t + 1)
                dve.tensor_tensor(o, o, g_all[0:nt, t, :], ALU.mult).then_inc(x_ready, 1)
                dve.drain()

        TURNS = ([(0, t) for t in range(3)] + [(1, 0), (1, 1), (2, 0), (1, 2), (2, 1), (2, 2)]
                 + [(3, t) for t in range(3)] + [(4, 0), (4, 1), (5, 0), (5, 1), (4, 2), (5, 2)])
        X_AT = {(seq, t): 3 * (seq - 1) + t + 1 for seq, t in TURNS}
        X_AT.update({(5, 0): 12, (5, 1): 13, (4, 2): 14, (5, 2): 15})

        def turned(seq, t):
            return 2 * TURNS.index((seq, t)) + 2

        def pe_turn(pe, seq, t):
            src = o_all if seq in (1, 4) else x
            nt = TILES[t][1]
            if seq:
                pe.wait_ge(x_ready, X_AT[seq, t])
            else:
                pe.wait_ge(x_in, 48)
            for g in range(2):
                n = turned(seq, t) - 2 + g
                if n >= 2:
                    pe.wait_ge(turn_taken, n - 1)
                for k in range(4):
                    mm = pe.transpose(bank[6 + g][:, k * P:k * P + nt], src[0:nt, t, (4 * g + k) * P:(4 * g + k + 1) * P],
                                      cst[0:nt, C_ID:C_ID + nt])
                mm.then_inc(turn_ready, 1)

        def act_turn(act, seq, t):
            t0, nt = TILES[t]
            for g in range(2):
                act.wait_ge(turn_ready, turned(seq, t) - 1 + g)
                act.activation(xT[:, 4 * g:4 * g + 4, t0:t0 + nt],
                               bank[6 + g][:, :].rearrange("p (k s) -> p k s", k=4)[:, :, 0:nt],
                               ACT.Copy).then_inc(turn_taken, 1)

        def pe_join(pe, seq, t):
            t0, nt = TILES[t]
            pe_turn(pe, (1, 4)[seq], t)
            pe.wait_ge(wbig_in, 16 * (seq + 1))
            pe.wait_ge(turn_taken, turned((1, 4)[seq], t))
            for c in range(2):
                cols = slice(512 * c, 512 * c + 512)
                pe.matmul(ybank(t, c, nt), cst[0:nt, C_AID:C_AID + nt], x[0:nt, t, cols], start=True, stop=False)
                for k in range(KO):
                    mm = pe.matmul(ybank(t, c, nt), xT[:, k, t0:t0 + nt], wbig[:, k, cols],
                                   start=False, stop=(k == KO - 1))
            mm.then_inc(y_ready, 1)

        def sp_ln(sp, seq):
            if seq:
                sp.wait_ge(x_ready, 3 * NORM_AT[seq - 1])
            else:
                sp.wait_ge(x_ready, 3)
            l, s = divmod(seq, 2)
            sp.dma_start(lnw[:, 0, :], ln_g[l, s:s + 1, :].broadcast_to([P, D])).then_inc(lnw_in, 16)
            sp.dma_start(lnw[:, 1, :], ln_b[l, s:s + 1, :].broadcast_to([P, D])).then_inc(lnw_in, 16)

        NORM_AT = (2, 3, 5, 6)

        def dve_ln(dve, seq, tiles=range(3)):
            for t in tiles:
                nt = TILES[t][1]
                n = 3 * seq + t
                dve.wait_ge(y_ready, n + 1)
                for c in range(2):
                    dve.bn_stats(stats[0:nt, c, :], ybank(t, c, nt))
                dve.drain()
                dve.bn_aggr(mv[0:nt, :], stats[0:nt, :, :].rearrange("p a b -> p (a b)"))
                dve.drain()
                dve.tensor_copy(std[0:nt, 0:1], mv[0:nt, 1:2]).then_inc(stat_ready, 1)
                dve.wait_ge(lnw_in, 32 * (seq + 1))
                for c in range(2):
                    cols = slice(512 * c, 512 * c + 512)
                    ins = dve.scalar_tensor_tensor(x[0:nt, t, cols], ybank(t, c, nt), mv[0:nt, 0:1], lnw[0:nt, 0, cols],
                                                   ALU.subtract, ALU.mult)
                ins.then_inc(y_free, 1)
                dve.wait_ge(std_ready, n + 1)
                dve.reciprocal(rstd[0:nt, 0:1], std[0:nt, 0:1])
                dve.drain()
                dve.scalar_tensor_tensor(x[0:nt, t, :], x[0:nt, t, :], rstd[0:nt, 0:1], lnw[0:nt, 1, :],
                                         ALU.mult, ALU.add).then_inc(x_ready, 1)
                dve.drain()

        def act_ln(act, seq, tiles=range(3)):
            for t in tiles:
                nt = TILES[t][1]
                act.wait_ge(stat_ready, 3 * seq + t + 1)
                act.activation(std[0:nt, 0:1], std[0:nt, 0:1], ACT.Sqrt, scale=1.0,
                               bias=cst[0:nt, C_EPS:C_EPS + 1]).then_inc(std_ready, 1)

        wflat = wbig[:, :, :].rearrange("p k n -> p (k n)")
        wq = [wflat[:, 2048 * j:2048 * (j + 1)].rearrange("p (k n) -> p k n", k=KO) for j in range(2)]
        keys = [wflat[:, 4096 + 256 * j:4096 + 256 * (j + 1)].rearrange("p (s d) -> p s d", s=2) for j in range(2)]
        wq_first = o_all[:, 0:2, :].rearrange("p t n -> p (t n)").rearrange("p (k n) -> p k n", k=KO)
        keys_first = sb("keys_first", [P, 2, P])
        xrep = wflat[:, 5120:6144]
        us, vs = wflat[:, 6144:7168], wflat[:, 7168:8192]
        uring = arena[:, 0:RING * D].rearrange("p (r d) -> p r d", r=RING)
        vring = arena[:, RING * D:2 * RING * D].rearrange("p (r d) -> p r d", r=RING)
        gflat = g_all[:, :, :].rearrange("p a b -> p (a b)")
        goff = [0]

        def gview(n, dt=None):
            v = gflat[:, goff[0]:goff[0] + n]
            goff[0] += n
            return v.bitcast(dt) if dt else v

        kT = gview(2 * P).rearrange("p (s n) -> p s n", s=2)
        qT = gview(2 * NT).rearrange("p (s n) -> p s n", s=2)
        sc = gview(6 * P).rearrange("p (t s n) -> p t s n", t=3, s=2)
        sc2 = sb("sc2", [P, 2, NKEYS])
        v12 = sb("v12", [P, 2, TOPK])
        i12 = sb("i12", [P, 2, TOPK], U32)
        i12f = sb("i12f", [P, 2, TOPK])
        cand = sb("cand", [P, TOPK, TOPK])
        cand2 = sb("cand2", [P, TOPK, TOPK])
        sv = sb("sv", [P, TOPK])
        si = sb("si", [P, TOPK], U32)
        ab = sb("ab", [P, 2, TOPK], U32)
        abf = sb("abf", [P, 2, TOPK])
        oh = sb("oh", [P, 2, TOPK, TOPK])
        e12 = sb("e12", [P, 2, TOPK])
        ef = sb("ef", [P, TOPK])
        idx = [[sb(f"idx{t}{j}", [P, TOPK], U32) for j in range(2)] for t in range(2)]
        dif = [[sb(f"dif{t}{j}", [P, TOPK]) for j in range(2)] for t in range(2)]
        dif_s = sb("dif_s", [NS, TOPK])
        gex = [sb(f"gex{t}", [P, TOPK]) for t in range(2)]
        gsum = [sb(f"gsum{t}", [P, 1]) for t in range(2)]
        gsum_s = sb("gsum_s", [NS, 1])
        rp = sb("rp", [NS, 2, TOPK])
        pick = sb("pick", [P, 2, TOPK])
        sidf = sb("sidf", [P, 1])
        sidx = [sb(f"sidx{j}", [P, 1], U32) for j in range(2)]
        sgate = [sb(f"sgate{j}", [P, 1]) for j in range(2)]
        dots = [sb(f"dots{t}", [P, TOPK]) for t in range(2)]
        acts = [sb(f"acts{t}", [P, TOPK]) for t in range(2)]
        w = [sb(f"w{t}", [P, TOPK]) for t in range(2)]
        dot_s = sb("dot_s", [P, 1])
        act_s = sb("act_s", [P, 1])
        wmask = sb("wmask", [P, NS])
        dg = sb("dg", [P, 4, P])

        rt_in = [sem(f"rt_in{j}") for j in range(2)]
        rt_first_in = sem("rt_first_in")
        rs_ready = sem("rs_ready")
        rs_taken = sem("rs_taken")
        sc_free = sem("sc_free")
        idx_ready = sem("idx_ready")
        dif_s_ready = sem("dif_s_ready")
        gex_s_ready = sem("gex_s_ready")
        rp_ready = sem("rp_ready")
        repack_ready = sem("repack_ready")
        sidx_ready = sem("sidx_ready")
        unpacked = sem("unpacked")
        u_free = sem("u_free")
        v_free = sem("v_free")
        us_free = sem("us_free")
        vs_free = sem("vs_free")
        u_land = [sem(f"u_land{r}") for r in range(RING)]
        v_land = [sem(f"v_land{r}") for r in range(RING)]
        us_land = sem("us_land")
        vs_land = sem("vs_land")
        dots_ready = sem("dots_ready")
        gelu_ready = sem("gelu_ready")
        w_ready = sem("w_ready")
        dg_ready = sem("dg_ready")
        dot_s_ready = sem("dot_s_ready")
        gelu_s_ready = sem("gelu_s_ready")
        wmask_ready = sem("wmask_ready")
        rep_ready = sem("rep_ready")
        rep_taken = sem("rep_taken")
        V0 = 32 + RING

        def sp_first(sp, l):
            sp.wait_ge(turn_taken, turned((1, 4)[l], 1))
            sp.dma_start(wq_first, peer_w_q[l].rearrange("(ko ki) (h n) -> ki ko h n", ki=P, h=HH)[:, :, 0, :]).then_inc(rt_first_in, 16)
            sp.dma_start(keys_first[:, 0, :], peer_k1[l, 0]).then_inc(rt_first_in, 16)
            sp.dma_start(keys_first[:, 1, :], peer_k2[l, 0]).then_inc(rt_first_in, 16)

        def sp_peer(sp, l):
            wq_v = peer_w_q[l].rearrange("(ko ki) (h n) -> ki ko h n", ki=P, h=HH)

            def load_route(h, j):
                sp.dma_start(wq[j], wq_v[:, :, h, :]).then_inc(rt_in[j], 16)
                sp.dma_start(keys[j][:, 0, :], peer_k1[l, h]).then_inc(rt_in[j], 16)
                sp.dma_start(keys[j][:, 1, :], peer_k2[l, h]).then_inc(rt_in[j], 16)
            sp.wait_ge(y_ready, 3 * (2 * l + 1))
            load_route(1, 1)
            if l == 0:
                sp.dma_start(w_dkvq[:, :, 0:LORA + ROPE], mla_w_dkv.rearrange("(k p) n -> p k n", p=P)).then_inc(wd_in, 16)
                sp.dma_start(w_dkvq[:, :, LORA + ROPE:WKVQ], mla_w_dq[0].rearrange("(k p) n -> p k n", p=P)).then_inc(wd_in, 16)

            def body(i, j, last):
                n = 2 * i + j
                if not last:
                    after(sp, "sp", rs_ready, 6 * (HH * l + n) + 6)
                    load_route(n + 2, j)
            with sp.Fori(0, HH // 2 - 1) as i:
                for j in range(2):
                    body(i, j, False)

        def pool_peer(pool, l):
            def gather(dst, table, rows, done):
                pool.indirect_dma_start(out=dst, out_offset=None, in_=table,
                                        in_offset=bass.IndirectOffsetOnAxis(ap=rows, axis=0)).then_inc(done, 16)

            def body(i, j, last, first=False):
                hg = 2 * i + j + HH * l

                def u(t, k):
                    after(pool, "pool", u_free, 32 * hg + 16 * t + k + 1)
                    gather(uring[:, k % RING, :], peer_u, idx[t][j][:, k:k + 1], u_land[k % RING])

                def v(t, k):
                    after(pool, "pool", v_free, 32 * hg + 16 * t + k + 1 + V0 - RING)
                    gather(vring[:, k % RING, :], peer_v, idx[t][j][:, k:k + 1], v_land[k % RING])
                after(pool, "pool", idx_ready, 2 * hg + 1)
                lead = RING if first else 0
                for k in range(TOPK):
                    if k == RING:
                        if l and first:
                            pool.wait_ge(dn_ready, NS)
                        for m in range(lead // 2):
                            v(0, m)
                    u(0, k)
                if l and first:
                    pool.wait_ge(os_ready, 1)
                for k in range(lead // 2, lead):
                    v(0, k)
                after(pool, "pool", idx_ready, 2 * hg + 2)
                for k in range(TOPK):
                    if k + lead < TOPK:
                        v(0, k + lead)
                    u(1, k)
                after(pool, "pool", sidx_ready, hg + 1)
                after(pool, "pool", us_free, hg + 1)
                gather(us, peer_u, sidx[j][:, :], us_land)
                for k in range(TOPK):
                    v(1, k)
                after(pool, "pool", vs_free, hg + 1)
                gather(vs, peer_v, sidx[j][:, :], vs_land)
            if l:
                pool.wait_ge(dpv_ready, NS - 1)
            head_pairs_first(body)(pool)

        def pe_first(pe, l, t):
            t0, nt = TILES[t]
            n = 6 * HH * l + 2 * t
            pe_turn(pe, (2, 5)[l], t)
            if t == 0:
                pe.wait_ge(rt_first_in, 48 * (l + 1))
                pe.wait_ge(unpacked, HH * l + 1)
            pe.wait_ge(turn_taken, turned((2, 5)[l], t))
            if n:
                pe.wait_ge(rs_taken, n)
            if t == 0:
                for s in range(2):
                    pe.transpose(bank[7][:, s * P:(s + 1) * P], keys_first[:, s, :], ident)
            for s in range(2):
                for k in range(KO):
                    mm = pe.matmul(bank[6][:, s * P:s * P + nt], wq_first[:, k, s * P:(s + 1) * P], xT[:, k, t0:t0 + nt],
                                   start=(k == 0), stop=(k == KO - 1))
            mm.then_inc(rs_ready, 1)
            pe.wait_ge(rs_taken, n + 1)
            for s in range(2):
                mm = pe.matmul(bank[7][0:nt, s * P:(s + 1) * P], qT[:, s, t0:t0 + nt], kT[:, s, :], start=True, stop=True)
            mm.then_inc(rs_ready, 1)
            pe.wait_ge(rs_taken, n + 2)

        def act_first(act, l, t):
            t0, nt = TILES[t]
            n = 6 * HH * l + 2 * t
            act.wait_ge(rs_ready, n + 1)
            if t == 0:
                act.activation(kT, bank[7][:, 0:2 * P].rearrange("p (s n) -> p s n", s=2), ACT.Copy)
            act.activation(qT[:, :, t0:t0 + nt], bank[6][:, 0:2 * P].rearrange("p (s n) -> p s n", s=2)[:, :, 0:nt],
                           ACT.Copy).then_inc(rs_taken, 1)
            act.wait_ge(rs_ready, n + 2)
            act.wait_ge(sc_free, 3 * HH * l + t + 1)
            act.activation(sc[0:nt, t, :, :], bank[7][0:nt, 0:2 * P].rearrange("p (s n) -> p s n", s=2),
                           ACT.Copy).then_inc(rs_taken, 1)

        def pe_peer(pe, l):
            def step(hg, m):
                after(pe, "pe", rs_taken, 6 * hg + m - 1)
                return bank[6 + m % 2]

            def route(i, j, late=False):
                hg = 2 * i + j + HH * l
                after(pe, "pe", rt_in[j], 48 * (i + (1 + 4 * l if j else 3 * l)))
                after(pe, "pe", unpacked, hg + (1 if late else 0))
                b = step(hg, 0)
                for s in range(2):
                    mm = pe.transpose(b[:, s * P:(s + 1) * P], keys[j][:, s, :], ident)
                mm.then_inc(rs_ready, 1)
                for s in range(2):
                    b = step(hg, 1 + s)
                    for k in range(KO):
                        mm = pe.matmul(b[:, 0:NT], wq[j][:, k, s * P:(s + 1) * P], xT[:, k, :],
                                       start=(k == 0), stop=(k == KO - 1))
                    mm.then_inc(rs_ready, 1)
                for t, (t0, nt) in enumerate(TILES):
                    b = step(hg, 3 + t)
                    if t == 0:
                        after(pe, "pe", rs_taken, 6 * hg + 3)
                    for s in range(2):
                        mm = pe.matmul(b[0:nt, s * P:(s + 1) * P], qT[:, s, t0:t0 + nt], kT[:, s, :],
                                       start=True, stop=True)
                    mm.then_inc(rs_ready, 1)

            def repack(hg, ahead):
                after(pe, "pe", rs_taken, 6 * hg + (12 if ahead else 6))
                after(pe, "pe", rp_ready, hg + 1)
                pe.matmul(bank[6][:, 0:2 * TOPK], cst[0:NS, C_BLKT:C_BLKT + P],
                          rp[:, :, :].rearrange("p a b -> p (a b)"), start=True, stop=True).then_inc(repack_ready, 1)

            def add_rows(hg, t, ks=range(TOPK)):
                for k in ks:
                    after(pe, "pe", v_land[k % RING], 16 * (4 * hg + 2 * t + k // RING + 1))
                    after(pe, "pe", dg_ready, 32 * hg + 16 * t + k + 1)
                    for c in range(2):
                        mm = pe.matmul(ybank(t, c, P), dg[:, k % 4, :], vring[:, k % RING, 512 * c:512 * c + 512],
                                       start=False, stop=False, skip_group_check=True)
                    mm.then_inc(v_free, 1)

            pe.wait_ge(y_free, 3 * (2 * l + 1))
            for c in range(2):
                mm = pe.matmul(bank[4 + c][:, :], cst[0:NS, C_BLKT:C_BLKT + P], x[0:NS, 2, 512 * c:512 * c + 512],
                               start=True, stop=True)
            mm.then_inc(rep_ready, 1)
            pe.wait_ge(rep_taken, l + 1)
            for t, (t0, nt) in enumerate(TILES):
                for c in range(2):
                    pe.matmul(ybank(t, c, nt), cst[0:nt, C_AID:C_AID + nt], x[0:nt, t, 512 * c:512 * c + 512],
                              start=True, stop=False, skip_group_check=True)
            def body(i, j, last, first=False):
                n = 2 * i + j
                hg = n + HH * l
                ahead = not (last and j == 1)
                if ahead and not first:
                    route(i + j, 1 - j)
                if first:
                    add_rows(hg, 0, range(RING))
                repack(hg, ahead and not first)
                add_rows(hg, 0, range(RING if first else 0, TOPK))
                if last and j == 1:
                    pe.drain()
                    pe.sem_inc(y_ready, 1)
                if first:
                    route(i + j, 1 - j, True)
                add_rows(hg, 1)
                if last and j == 1:
                    pe.drain()
                    pe.sem_inc(y_ready, 1)
                after(pe, "pe", vs_land, 16 * (hg + 1))
                after(pe, "pe", wmask_ready, hg + 1)
                for c in range(2):
                    mm = pe.matmul(ybank(2, c, NS), wmask[:, :], vs[:, 512 * c:512 * c + 512],
                                   start=False, stop=False, skip_group_check=True)
                mm.then_inc(vs_free, 1)
            head_pairs_first(body)(pe)
            pe.drain()
            pe.sem_inc(y_ready, 1)

        def act_peer(act, l):
            act.wait_ge(rep_ready, l + 1)
            for c in range(2):
                ins = act.activation(xrep[:, 512 * c:512 * c + 512], bank[4 + c][:, :], ACT.Copy)
            ins.then_inc(rep_taken, 1)

            def route(hg):
                after(act, "act", rs_ready, 6 * hg + 1)
                act.activation(kT, bank[6][:, 0:2 * P].rearrange("p (s n) -> p s n", s=2), ACT.Copy).then_inc(rs_taken, 1)
                for s in range(2):
                    after(act, "act", rs_ready, 6 * hg + 2 + s)
                    act.activation(qT[:, s, :], bank[7 - s][:, 0:NT], ACT.Copy).then_inc(rs_taken, 1)
                for t, (t0, nt) in enumerate(TILES):
                    after(act, "act", rs_ready, 6 * hg + 4 + t)
                    after(act, "act", sc_free, 3 * hg + t + 1)
                    act.activation(sc[0:nt, t, :, :], bank[6 + (t + 1) % 2][0:nt, 0:2 * P].rearrange("p (s n) -> p s n", s=2),
                                   ACT.Copy).then_inc(rs_taken, 1)

            def exp_s(hg):
                after(act, "act", dif_s_ready, hg + 1)
                act.activation(rp[:, 1, :], dif_s[:, :], ACT.Exp, accum_out=gsum_s[:, :]).then_inc(gex_s_ready, 1)

            def gelu(hg, t, j):
                after(act, "act", dots_ready, 2 * hg + t + 1)
                act.activation(gex[t][:, :], dif[t][j][:, :], ACT.Exp, accum_out=gsum[t][:, :])
                act.activation(acts[t][:, :], dots[t][:, :], ACT.Gelu).then_inc(gelu_ready, 1)

            def diags(hg, t, ks):
                after(act, "act", w_ready, 2 * hg + t + 1)
                for k in ks:
                    after(act, "act", v_free, 32 * hg + 16 * t + k - 3 + V0)
                    act.activation(dg[:, k % 4, :], ident, ACT.Copy, scale=w[t][:, k:k + 1]).then_inc(dg_ready, 1)

            def body(i, j, last, first=False):
                hg = 2 * i + j + HH * l
                ahead = not (last and j == 1)
                if ahead and not first:
                    route(hg + 1)
                if not first:
                    exp_s(hg)
                gelu(hg, 0, j)
                if first:
                    diags(hg, 0, range(RING))
                    exp_s(hg)
                diags(hg, 0, range(RING if first else 0, TOPK))
                if first:
                    route(hg + 1)
                gelu(hg, 1, j)
                after(act, "act", dot_s_ready, hg + 1)
                act.activation(act_s[:, :], dot_s[:, :], ACT.Gelu).then_inc(gelu_s_ready, 1)
                diags(hg, 1, range(TOPK))
            head_pairs_first(body)(act)

        def dve_parts(dve, l):
            def top16(*rows):
                for v_, i_, src, tmp in rows:
                    dve.max(v_[:, 0:8], src)
                dve.drain()
                for v_, i_, src, tmp in rows:
                    dve.max_index(i_[:, 0:8], v_[:, 0:8], src)
                    dve.match_replace(tmp, v_[:, 0:8], src, -3.0e38)
                dve.drain()
                for v_, i_, src, tmp in rows:
                    dve.max(v_[:, 8:16], tmp)
                dve.drain()
                for v_, i_, src, tmp in rows:
                    dve.max_index(i_[:, 8:16], v_[:, 8:16], tmp)

            def route(hg, t, j, first=False):
                nt = TILES[t][1]
                after(dve, "dve", rs_taken, 6 * hg + (2 * t + 2 if first else 4 + t))
                top16(*[(v12[0:nt, s, :], i12[0:nt, s, :], sc[0:nt, t, s, :], sc2[0:nt, s, :]) for s in range(2)])
                dve.drain()
                dve.sem_inc(sc_free, 1)
                dve.tensor_tensor(cand[0:nt, :, :], bc(v12[0:nt, 0, :], 2, TOPK), bc(v12[0:nt, 1, :], 1, TOPK), ALU.add)
                dve.tensor_copy(i12f[0:nt, :, :], i12[0:nt, :, :])
                dve.drain()
                top16((sv[0:nt, :], si[0:nt, :], cand[0:nt, :, :].rearrange("p a b -> p (a b)"),
                       cand2[0:nt, :, :].rearrange("p a b -> p (a b)")))
                dve.drain()
                dve.tensor_scalar(ab[0:nt, 0, :], si[0:nt, :], 4, None, ALU.logical_shift_right)
                dve.tensor_scalar(ab[0:nt, 1, :], si[0:nt, :], 15, None, ALU.bitwise_and)
                if t < 2:
                    after(dve, "dve", v_free, 32 * hg + V0 - 32)
                    dve.tensor_scalar(dif[t][j][:, :], sv[:, :], sv[:, 0:1], None, ALU.subtract)
                else:
                    dve.tensor_scalar(dif_s[:, :], sv[0:nt, :], sv[0:nt, 0:1], None, ALU.subtract).then_inc(dif_s_ready, 1)
                dve.drain()
                dve.tensor_copy(abf[0:nt, :, :], ab[0:nt, :, :])
                dve.drain()
                places = bc(bc(iota[0:nt, :], 1, TOPK), 1, 2)
                dve.tensor_tensor(oh[0:nt], bc(abf[0:nt, :, :], 3, TOPK), places, ALU.is_equal)
                dve.drain()
                dve.tensor_tensor(oh[0:nt], oh[0:nt], bc(i12f[0:nt, :, :], 2, TOPK), ALU.mult)
                dve.drain()
                dve.tensor_reduce(e12[0:nt, :, :], oh[0:nt], AX, ALU.add)
                dve.drain()
                dve.scalar_tensor_tensor(ef[0:nt, :], e12[0:nt, 0, :], float(NKEYS), e12[0:nt, 1, :], ALU.mult, ALU.add)
                dve.drain()
                if t < 2:
                    dve.tensor_scalar(idx[t][j][:, :], ef[:, :], float(NEXP * l), None, ALU.add).then_inc(idx_ready, 1)
                else:
                    dve.tensor_scalar(rp[:, 0, :], ef[0:nt, :], float(NEXP * l), None, ALU.add)
                dve.drain()

            def gate_s(hg):
                after(dve, "dve", gex_s_ready, hg + 1)
                dve.reciprocal(gsum_s[:, :], gsum_s[:, :])
                dve.drain()
                dve.tensor_scalar(rp[:, 1, :], rp[:, 1, :], gsum_s[:, 0:1], None, ALU.mult).then_inc(rp_ready, 1)

            def unpack_s(hg, j):
                after(dve, "dve", repack_ready, hg + 1)
                if not (isinstance(hg, int) and hg == 0):
                    after(dve, "dve", vs_free, hg)
                dve.tensor_tensor(pick[:, :, :], bank[6][:, 0:2 * TOPK].rearrange("p (a k) -> p a k", a=2),
                                  bc(cst[:, C_SEL:C_SEL + TOPK], 1, 2), ALU.mult)
                dve.drain()
                dve.tensor_reduce(sidf[:, :], pick[:, 0, :], AX, ALU.add)
                dve.tensor_reduce(sgate[j][:, :], pick[:, 1, :], AX, ALU.add)
                dve.drain()
                dve.tensor_copy(sidx[j][:, :], sidf[:, :]).then_inc(sidx_ready, 1)
                dve.sem_inc(unpacked, 1)

            def dot(hg, t):
                for k in range(TOPK):
                    after(dve, "dve", u_land[k % RING], 16 * (4 * hg + 2 * t + k // RING + 1))
                    dve.scalar_tensor_tensor(uring[:, k % RING, :], uring[:, k % RING, :], 1.0, x[:, t, :],
                                             ALU.mult, ALU.mult, accum_out=dots[t][:, k:k + 1]).then_inc(u_free, 1)
                dve.drain()
                dve.sem_inc(dots_ready, 1)

            def weigh(hg, t):
                after(dve, "dve", gelu_ready, 2 * hg + t + 1)
                dve.reciprocal(gsum[t][:, :], gsum[t][:, :])
                dve.drain()
                dve.scalar_tensor_tensor(w[t][:, :], gex[t][:, :], gsum[t][:, 0:1], acts[t][:, :],
                                         ALU.mult, ALU.mult).then_inc(w_ready, 1)

            def body(i, j, last, first=False):
                hg = 2 * i + j + HH * l
                ahead = not (last and j == 1)
                if not first:
                    dot(hg, 0)
                gate_s(hg)
                if ahead and not first:
                    route(hg + 1, 0, 1 - j)
                unpack_s(hg, j)
                if not first:
                    weigh(hg, 0)
                dot(hg, 1)
                after(dve, "dve", us_land, 16 * (hg + 1))
                dve.scalar_tensor_tensor(us, us, 1.0, xrep, ALU.mult, ALU.mult, accum_out=dot_s[:, :]).then_inc(us_free, 1)
                dve.drain()
                dve.sem_inc(dot_s_ready, 1)
                weigh(hg, 1)
                after(dve, "dve", gelu_s_ready, hg + 1)
                after(dve, "dve", vs_free, hg + 1)
                dve.tensor_scalar(wmask[:, :], blk, act_s[:, 0:1], sgate[j][:, 0:1], ALU.mult, ALU.mult).then_inc(wmask_ready, 1)
                if first:
                    route(hg + 1, 0, 1 - j)
                if ahead:
                    route(hg + 1, 1, 1 - j)
                    route(hg + 1, 2, 1 - j)

            def heads():
                head_pairs_first(body)(dve)

            return route, dot, weigh, heads

        def dve_credits(dve):
            dve.sem_inc(u_free, RING)
            dve.sem_inc(v_free, V0)
            dve.sem_inc(sc_free, 3)
            dve.sem_inc(us_free, 1)
            dve.sem_inc(vs_free, 1)
            dve.sem_inc(unpacked, 1)

        soff[0] = 0
        WKVQ = LORA + ROPE + QLORA
        PW = PAGES * (LORA + ROPE)
        slots = [arena[:, 0:PW], arena[:, PW:2 * PW], scratch[:, 0:PW]]
        cbuf = [v[:, 0:PAGES * LORA].rearrange("p (g l) -> p g l", g=PAGES) for v in slots]
        kbuf = [v[:, PAGES * LORA:PW].rearrange("p (g r) -> p g r", g=PAGES) for v in slots]
        QP = 4
        NQ = PAGES // QP
        cT = arena[:, 9216:11264].rearrange("p (s c k) -> p s c k", s=2, c=2)
        kpT = arena[0:ROPE, 11264:12288].rearrange("p (s k) -> p s k", s=2)
        NKEY = PAGES * PAGE + NS
        dsc = scratch[0:MH, PW:PW + NKEY]
        dp = scratch[0:MH, PW + NKEY:PW + 2 * NKEY]
        dol = scratch[0:MH, PW + 2 * NKEY:PW + 2 * NKEY + LORA]
        w_ukv = arena[:, 12288:16384].rearrange("p (c n) -> p c n", c=2)
        w_dkvq = scratch[:, SCRATCH - KO * WKVQ:SCRATCH].rearrange("p (k n) -> p k n", k=KO)
        w_uq = arena[:, 5376:9984].rearrange("p (k n) -> p k n", k=3)
        kvq = arena[:, 9984:12000].rearrange("p (t n) -> p t n", t=3)
        gkq = gflat[:, 0:LORA + QLORA]
        cqT = gflat[:, 640:640 + 3 * NT].rearrange("p (k t) -> p k t", k=3)
        ckvT = gflat[:, 3 * D - 2 * NT:3 * D].rearrange("p (k t) -> p k t", k=2)
        qs = sview(3 * HG * QD).rearrange("p (t h n) -> p t h n", t=3, h=HG)
        kf = sview(2 * HG * QD).rearrange("p (t h n) -> p t h n", t=2, h=HG)
        vv = sview(2 * HG * VD).rearrange("p (t h n) -> p t h n", t=2, h=HG)
        qfT = sview(2 * HG * P).rearrange("p (t h s) -> p t h s", t=2, h=HG)[0:QD]
        kfT = sview(2 * HG * P).rearrange("p (t h s) -> p t h s", t=2, h=HG)[0:QD]
        ukst = sview(2 * HG * NOPE).rearrange("p (c h n) -> p c h n", c=2, h=HG)
        ukT = sview(2 * HG * P).rearrange("p (c h l) -> p c h l", c=2, h=HG)[0:NOPE]
        pr = sview(12 * P).rearrange("p (a s) -> p a s", a=12)
        pT = sview(12 * P).rearrange("p (a s) -> p a s", a=12)
        rt = sb("rt", [P, 4, HG, ROPE // 2])
        qsT = sb("qsT", [NOPE, HG, NS])
        qlT = sb("qlT", [P, 2, NS, MH])
        qpT = sb("qpT", [ROPE, NS, MH])
        knT = sb("knT", [ROPE, NS])
        ckvS = sb("ckvS", [NS, LORA])
        olT = sb("olT", [P, 2, MH, NS])
        dpT = sb("dpT", [P, PAGES + 1, MH])
        dmx = sb("dmx", [MH, NQ + 1])
        dneg = sb("dneg", [MH, 1])
        dsum = sb("dsum", [MH, 1])
        drs = sb("drs", [MH, 1])
        mx = sb("mx", [P, 2, HG])
        sm = sb("sm", [P, 2, HG])
        ptab = sb("ptab", [1, NS * PAGES], I32)

        wd_in = sem("wd_in")
        wm_in = sem("wm_in")
        ptab_in = sem("ptab_in")
        kvq_ready = sem("kvq_ready")
        kvq_taken = sem("kvq_taken")
        kvq_norm = sem("kvq_norm")
        lt_ready = sem("lt_ready")
        lt_taken = sem("lt_taken")
        q_ready = sem("q_ready")
        q_taken = sem("q_taken")
        qrot_ready = sem("qrot_ready")
        kv_ready = sem("kv_ready")
        kv_taken = sem("kv_taken")
        ukst_ready = sem("ukst_ready")
        qT_ready = sem("qT_ready")
        qT_taken = sem("qT_taken")
        kT_ready = sem("kT_ready")
        kT_taken = sem("kT_taken")
        ukT_ready = sem("ukT_ready")
        ukT_taken = sem("ukT_taken")
        s_taken = sem("s_taken")
        qlat_ready = sem("qlat_ready")
        qlat_taken = sem("qlat_taken")
        s_ready = sem("s_ready")
        sm_ready = sem("sm_ready")
        p_ready = sem("p_ready")
        pT_ready = sem("pT_ready")
        pT_taken = sem("pT_taken")
        po_ready = sem("po_ready")
        po_taken = sem("po_taken")
        page_in = [sem(f"page_in{j}") for j in range(3)]
        rot_in = [sem(f"rot_in{j}") for j in range(3)]
        ct_ready = sem("ct_ready")
        ct_taken = sem("ct_taken")
        ds_ready = sem("ds_ready")
        ds_taken = sem("ds_taken")
        dn_ready = sem("dn_ready")
        dm_ready = sem("dm_ready")
        dp_ready = sem("dp_ready")
        dpT_ready = sem("dpT_ready")
        dpT_taken = sem("dpT_taken")
        dpv_ready = sem("dpv_ready")
        dol_ready = sem("dol_ready")
        dolT_ready = sem("dolT_ready")
        dolT_taken = sem("dolT_taken")
        os_ready = sem("os_ready")

        def sp_mla(sp):
            sp.wait_ge(y_ready, 6)
            sp.dma_start(gkq[:, 0:LORA], mla_kv_norm_g.rearrange("(a n) -> a n", a=1).broadcast_to([P, LORA])).then_inc(wm_in, 16)
            sp.dma_start(gkq[:, LORA:LORA + QLORA], mla_q_norm_g.broadcast_to([P, QLORA])).then_inc(wm_in, 16)
            sp.dma_start(w_uq, mla_w_uq[0].rearrange("(k p) n -> p k n", p=P)).then_inc(wm_in, 16)
            sp.dma_start(w_ukv, mla_w_ukv.rearrange("(c p) h n -> p c (h n)", p=P)).then_inc(wm_in, 16)
            sp.dma_start(ptab[:, :], page_table.rearrange("b g -> (b g)").rearrange("(a n) -> a n", a=1)).then_inc(ptab_in, 16)
            sp.dma_start(wbig[:, :, :], mla_w_o[0].rearrange("(k p) n -> p k n", p=P)).then_inc(wbig_in, 16)
            for t, (t0, nt) in enumerate(TILES):
                sp.wait_ge(kvq_norm, t + 1)
                c = ckv_prompt[0, t0:t0 + nt, :] if t < 2 else ckv_sample.rearrange("b t l -> (b t) l")
                k = kpe_prompt[0, t0:t0 + nt, :] if t < 2 else kpe_sample.rearrange("b t l -> (b t) l")
                sp.dma_start(c, kvq[0:nt, t, 0:LORA]).then_inc(stored, 16)
                sp.dma_start(k, kvq[0:nt, t, LORA:LORA + ROPE]).then_inc(stored, 16)
            sp_ln(sp, 2)
            load_pages(sp, cbuf, cache_ckv, page_in, lambda: sp_first(sp, 1))

        def load_pages(eng, buf, cache, landed, between=None):
            eng.wait_ge(ptab_in, 16)
            eng.wait_ge(stored, 96)
            eng.wait_ge(q_ready, NG)
            for b in range(NS):
                if b == 2 and between:
                    between()
                if b == 1:
                    eng.wait_ge(po_taken, NG + 1)
                if b >= 3:
                    eng.wait_ge(dpv_ready, b - 2)
                with eng.Fori(0, PAGES) as g:
                    page = eng.value_load(ptab[0:1, bass.ds(g + b * PAGES, 1)], min_val=0,
                                          max_val=cache.shape[0] - 1)
                    eng.dma_start(buf[(b + 1) % 3][:, bass.ds(g, 1), :].rearrange("p a l -> p (a l)"),
                                  cache[page]).then_inc(landed[(b + 1) % 3], 16)

        def pe_mla(pe):
            def down(t, t0, nt):
                if t == 0:
                    pe.wait_ge(wd_in, 32)
                pe.wait_ge(y_free, 3 + t + 1)
                for b, (c0, c1) in enumerate(((0, LORA + ROPE), (LORA + ROPE, WKVQ))):
                    for k in range(KO):
                        mm = pe.matmul(bank[2 * t + b][0:nt, 0:c1 - c0], xT[:, k, t0:t0 + nt], w_dkvq[:, k, c0:c1],
                                       start=(k == 0), stop=(k == KO - 1))
                mm.then_inc(kvq_ready, 1)
            for t, (t0, nt) in enumerate(TILES):
                pe_turn(pe, 3, t)
                pe.wait_ge(turn_taken, turned(3, t))
                down(t, t0, nt)
            for t, (t0, nt) in enumerate(TILES):
                idt = cst[0:nt, C_ID:C_ID + nt]
                pe.wait_ge(kvq_norm, t + 1)
                if t:
                    pe.wait_ge(lt_taken, t)
                for k in range(3):
                    pe.transpose(bank[6][:, k * P:k * P + nt], kvq[0:nt, t, LORA + ROPE + k * P:LORA + ROPE + (k + 1) * P], idt)
                for k in range(2):
                    mm = pe.transpose(bank[7][:, k * P:k * P + nt], kvq[0:nt, t, k * P:(k + 1) * P], idt)
                if t == 2:
                    mm = pe.transpose(bank[7][0:ROPE, 2 * P:2 * P + nt], kvq[0:nt, t, LORA:LORA + ROPE], idt)
                mm.then_inc(lt_ready, 1)
            pe.wait_ge(lt_taken, 3)
            pe.wait_ge(wm_in, 16 * 4)

            def queries(g, tiles):
                for t in tiles:
                    t0, nt = TILES[t]
                    for k in range(3):
                        mm = pe.matmul(bank[(0, 1, 7)[t]][0:nt, 0:HG * QD], cqT[:, k, t0:t0 + nt],
                                       w_uq[:, k, bass.ds(g * (HG * QD), HG * QD)], start=(k == 0), stop=(k == 2))
                return mm

            def group(g, last):
                for t in range(2):
                    for c in range(2):
                        mm = pe.matmul(bank[3 + t][:, :], ckvT[:, c, t * P:(t + 1) * P], w_ukv[:, c, bass.ts(g, 512)],
                                       start=(c == 0), stop=(c == 1))
                mm.then_inc(kv_ready, 1)
                after(pe, "pe", qrot_ready, g + 1)
                after(pe, "pe", po_taken, g + 1)
                for h in range(HG):
                    cols = slice(h * P, (h + 1) * P)
                    pe.transpose(bank[5][0:QD, cols], qs[:, 0, h, :], ident)
                    pe.transpose(bank[6][0:QD, cols], qs[:, 1, h, :], ident)
                    id8 = cst[0:NS, C_ID:C_ID + NS]
                    pe.transpose(bank[1][0:NOPE, h * NS:(h + 1) * NS], qs[0:NS, 2, h, 0:NOPE], id8)
                    mm = pe.transpose(bank[1][0:ROPE, 64 + h * NS:64 + (h + 1) * NS], qs[0:NS, 2, h, NOPE:QD], id8)
                mm.then_inc(qT_ready, 1)
                after(pe, "pe", ukst_ready, g + 1)
                for h in range(HG):
                    pe.transpose(bank[2][0:NOPE, h * P:(h + 1) * P], ukst[:, 0, h, :], ident)
                after(pe, "pe", kv_taken, g + 1)
                for h in range(HG):
                    cols = slice(h * P, (h + 1) * P)
                    pe.transpose(bank[7][0:QD, cols], kf[:, 0, h, :], ident)
                    mm = pe.transpose(bank[0][0:QD, cols], kf[:, 1, h, :], ident)
                mm.then_inc(kT_ready, 1)
                for h in range(HG):
                    mm = pe.transpose(bank[3][0:NOPE, h * P:(h + 1) * P], ukst[:, 1, h, :], ident)
                mm.then_inc(ukT_ready, 1)
                after(pe, "pe", qT_taken, g + 1)
                after(pe, "pe", kT_taken, g + 1)
                for h in range(HG):
                    pe.matmul(bank[5][:, h * P:(h + 1) * P], qfT[:, 0, h, :], kfT[:, 0, h, :], start=True, stop=True)
                    mm = pe.matmul(bank[6 + h // 2][:, (h % 2) * 256:(h % 2) * 256 + 256], qfT[:, 1, h, :], kfT[:, :, h, :],
                                   start=True, stop=True)
                mm.then_inc(s_ready, 1)
                after(pe, "pe", ukT_taken, g + 1)
                for c in range(2):
                    for h in range(HG):
                        mm = pe.matmul(bank[1][:, (c * HG + h) * NS:(c * HG + h + 1) * NS], ukT[:, c, h, :], qsT[:, h, :],
                                       start=True, stop=True)
                mm.then_inc(qlat_ready, 1)
                if not last:
                    queries(g + 1, (0,))
                    after(pe, "pe", qlat_taken, g + 1)
                    queries(g + 1, (1,))
                    after(pe, "pe", s_taken, g + 1)
                    queries(g + 1, (2,)).then_inc(q_ready, 1)
                after(pe, "pe", p_ready, g + 1)
                for a in range(12):
                    mm = pe.transpose(bank[2 + a // 4][:, (a % 4) * P:(a % 4 + 1) * P], pr[:, a, :], ident)
                mm.then_inc(pT_ready, 1)
                after(pe, "pe", pT_taken, 2 * (g + 1))
                for h in range(HG):
                    pe.matmul(bank[5][:, h * VD:(h + 1) * VD], pT[:, h, :], vv[:, 0, h, :], start=True, stop=True)
                for h in range(HG):
                    for t in range(2):
                        mm = pe.matmul(bank[6][:, h * VD:(h + 1) * VD], pT[:, HG + 2 * h + t, :], vv[:, t, h, :],
                                       start=(t == 0), stop=(t == 1))
                mm.then_inc(po_ready, 1)

            queries(0, (0, 1, 2)).then_inc(q_ready, 1)
            with pe.Fori(0, NG - 1) as g:
                group(g, False)
            group(NG - 1, True)
            pe.wait_ge(po_taken, NG + 1)
            pe.wait_ge(qlat_taken, NG)
            pe_join(pe, 1, 0)
            pe_join(pe, 1, 1)
            pe_first(pe, 1, 0)
            pe_first(pe, 1, 1)
            pe.wait_ge(y_free, 8)

            def turn_pages(b, q, slot):
                if nonzero(b) or q:
                    after(pe, "pe", ct_taken, NQ * b + q)
                for g in range(QP):
                    cols = slice(g * P, (g + 1) * P)
                    for c in range(2):
                        pe.transpose(bank[c][:, cols], cbuf[slot][:, QP * q + g, c * P:(c + 1) * P], ident)
                    mm = pe.transpose(bank[2][0:ROPE, cols], kbuf[slot][:, QP * q + g, :], ident)
                mm.then_inc(ct_ready, 1)

            def score(b, q):
                if nonzero(b) or q >= 2:
                    after(pe, "pe", ds_taken, NQ * b + q - 1)
                out = bank[3 + q % 2][0:MH, :]
                for c in range(2):
                    pe.matmul(out, qst[:, c, :], cT[:, q % 2, c, :], start=(c == 0), stop=False)
                pe.matmul(out, qst[0:ROPE, 2, :], kpT[:, q % 2, :], start=False, stop=True).then_inc(ds_ready, 1)

            def score_new(b):
                out = bank[5][0:MH, 0:NS]
                for c in range(2):
                    pe.matmul(out, qst[:, c, :], ckvT[:, c, 2 * P:NT], start=(c == 0), stop=False)
                pe.matmul(out, qst[0:ROPE, 2, :], knT[:, :], start=False, stop=True).then_inc(dn_ready, 1)

            def turn_probs(b):
                after(pe, "pe", dp_ready, b + 1)
                if nonzero(b):
                    after(pe, "pe", dolT_taken, b)
                for pg in range(PAGES):
                    pe.transpose(bank[6][:, pg * MH:(pg + 1) * MH], dp[:, pg * P:(pg + 1) * P], id16)
                pe.transpose(bank[6][0:NS, PAGES * MH:(PAGES + 1) * MH], dp[:, PAGES * P:NKEY], id16).then_inc(dpT_ready, 1)

            def weigh_pages(b, slot):
                after(pe, "pe", dpT_taken, b + 1)
                out = bank[7][0:MH, 0:LORA]
                for pg in range(PAGES):
                    pe.matmul(out, dpT[:, pg, :], cbuf[slot][:, pg, :], start=(pg == 0), stop=False)
                pe.matmul(out, dpT[0:NS, PAGES, :], ckvS[:, :], start=False, stop=True).then_inc(dpv_ready, 1)

            def turn_out(b):
                after(pe, "pe", dol_ready, b + 1)
                for c in range(2):
                    mm = pe.transpose(bank[6][:, c * MH:(c + 1) * MH], dol[:, c * P:(c + 1) * P], id16)
                mm.then_inc(dolT_ready, 1)

            id16 = cst[0:MH, C_ID:C_ID + MH]

            def token(b, slot, loads):
                behind = nonzero(b)
                after(pe, "pe", page_in[slot], 16 * PAGES * loads)
                after(pe, "pe", rot_in[slot], 16 * PAGES * loads)
                turn_pages(b, 0, slot)
                if behind:
                    score(b - 1, NQ - 1)
                    score_new(b - 1)
                turn_pages(b, 1, slot)
                after(pe, "pe", qst_ready, b + 1)
                score(b, 0)
                turn_pages(b, 2, slot)
                score(b, 1)
                if behind:
                    turn_probs(b - 1)
                turn_pages(b, 3, slot)
                if behind:
                    weigh_pages(b - 1, (slot + 2) % 3)
                score(b, 2)
                if behind:
                    turn_out(b - 1)

            token(0, 1, 1)
            with pe.Fori(0, (NS - 2) // 3) as i:
                for j in range(3):
                    token(3 * i + (j + 1), (j + 2) % 3, i + (2 if j == 2 else 1))
            token(NS - 1, NS % 3, 3)
            pe.wait_ge(ct_taken, NQ * NS)
            score(NS - 1, NQ - 1)
            score_new(NS - 1)
            turn_probs(NS - 1)
            weigh_pages(NS - 1, NS % 3)
            turn_out(NS - 1)
            pe.wait_ge(dolT_taken, NS)
            for h in range(MH):
                for c in range(2):
                    mm = pe.matmul(bank[h // 8][0:NS, (h % 8) * VD:(h % 8 + 1) * VD], olT[:, c, h, :],
                                   w_ukv[:, c, h * 128 + NOPE:(h + 1) * 128], start=(c == 0), stop=(c == 1))
            mm.then_inc(os_ready, 1)

        qst = sb("qst", [P, 3, MH])
        qst_ready = sem("qst_ready")

        def pool_mla(pool):
            load_pages(pool, kbuf, cache_kpe, rot_in)

        def act_mla(act):
            for t in range(3):
                act_turn(act, 3, t)
            for t, (t0, nt) in enumerate(TILES):
                act.wait_ge(kvq_ready, t + 1)
                act.activation(kvq[0:nt, t, 0:LORA + ROPE], bank[2 * t][0:nt, 0:LORA + ROPE], ACT.Copy)
                act.activation(kvq[0:nt, t, LORA + ROPE:WKVQ], bank[2 * t + 1][0:nt, 0:QLORA], ACT.Copy)
                act.activation(o_all[0:nt, t, 0:LORA], bank[2 * t][0:nt, 0:LORA], ACT.Square,
                               accum_out=std[0:nt, 2 * t:2 * t + 1])
                act.activation(o_all[0:nt, t, LORA:LORA + QLORA], bank[2 * t + 1][0:nt, 0:QLORA], ACT.Square,
                               accum_out=std[0:nt, 2 * t + 1:2 * t + 2])
                act.drain()
                for s, n in enumerate((LORA, QLORA)):
                    act.activation(std[0:nt, 2 * t + s:2 * t + s + 1], std[0:nt, 2 * t + s:2 * t + s + 1], ACT.Sqrt,
                                         scale=1.0 / n, bias=cst[0:nt, C_EPS + 1:C_EPS + 2])
                act.drain()
                act.sem_inc(kvq_taken, 1)
            for t, (t0, nt) in enumerate(TILES):
                act.wait_ge(lt_ready, t + 1)
                act.activation(cqT[:, :, t0:t0 + nt], bank[6][:, 0:3 * P].rearrange("p (k s) -> p k s", k=3)[:, :, 0:nt], ACT.Copy)
                ins = act.activation(ckvT[:, :, t0:t0 + nt], bank[7][:, 0:2 * P].rearrange("p (k s) -> p k s", k=2)[:, :, 0:nt], ACT.Copy)
                if t == 2:
                    ins = act.activation(knT[:, :], bank[7][0:ROPE, 2 * P:2 * P + NS], ACT.Copy)
                ins.then_inc(lt_taken, 1)
            def take_queries(g):
                after(act, "act", q_ready, g + 1)
                for t, (t0, nt) in enumerate(TILES):
                    act.activation(qs[0:nt, t, :, :], bank[(0, 1, 7)[t]][0:nt, 0:HG * QD].rearrange("p (h n) -> p h n", h=HG), ACT.Copy)
                act.drain()
                act.sem_inc(q_taken, 1)

            def group(g, last):
                after(act, "act", kv_ready, g + 1)
                for t in range(2):
                    kv = bank[3 + t][:, :].rearrange("p (h n) -> p h n", h=HG)
                    act.activation(kf[:, t, :, 0:NOPE], kv[:, :, 0:NOPE], ACT.Copy)
                    ins = act.activation(vv[:, t, :, :], kv[:, :, NOPE:128], ACT.Copy)
                act.drain()
                act.sem_inc(kv_taken, 1)
                after(act, "act", qT_ready, g + 1)
                for t, b in ((0, 5), (1, 6)):
                    ins = act.activation(qfT[:, t, :, :], bank[b][0:QD, :].rearrange("p (h s) -> p h s", h=HG), ACT.Copy)
                ins.then_inc(qT_taken, 1)
                act.activation(qsT[:, :, :], bank[1][0:NOPE, 0:HG * NS].rearrange("p (h b) -> p h b", h=HG), ACT.Copy)
                act.activation(qpT[:, :, bass.ts(g, HG)], bank[1][0:ROPE, 64:64 + HG * NS].rearrange("p (h b) -> p b h", h=HG), ACT.Copy)
                after(act, "act", ukT_ready, g + 1)
                for c in range(2):
                    ins = act.activation(ukT[:, c, :, :], bank[2 + c][0:NOPE, :].rearrange("p (h l) -> p h l", h=HG), ACT.Copy)
                ins.then_inc(ukT_taken, 1)
                after(act, "act", qlat_ready, g + 1)
                for c in range(2):
                    ins = act.activation(qlT[:, c, :, bass.ts(g, HG)],
                                         bank[1][:, c * HG * NS:(c + 1) * HG * NS].rearrange("p (h b) -> p b h", h=HG), ACT.Copy)
                ins.then_inc(qlat_taken, 1)
                after(act, "act", sm_ready, g + 1)
                act.activation(pr, pr, ACT.Exp).then_inc(p_ready, 1)
                if not last:
                    take_queries(g + 1)
                after(act, "act", pT_ready, g + 1)
                for a in range(2):
                    ins = act.activation(pT[:, 4 * a:4 * a + 4, :], bank[2 + a][:, :].rearrange("p (a s) -> p a s", a=4), ACT.Copy)
                ins.then_inc(pT_taken, 1)

            take_queries(0)
            with act.Fori(0, NG - 1) as g:
                group(g, False)
            group(NG - 1, True)
            act_turn(act, 4, 0)
            act_turn(act, 4, 1)
            act_ln(act, 2, (0, 1))
            for t in range(2):
                act_turn(act, 5, t)
                act_first(act, 1, t)
            def take_pages(b, q):
                after(act, "act", ct_ready, NQ * b + q + 1)
                for c in range(2):
                    act.activation(cT[:, q % 2, c, :], bank[c][:, :], ACT.Copy)
                act.activation(kpT[:, q % 2, :], bank[2][0:ROPE, :], ACT.Copy).then_inc(ct_taken, 1)

            def exp_scores(b):
                after(act, "act", dm_ready, b + 1)
                act.activation(dp, dsc, ACT.Exp, scale=SCALE, bias=dneg[:, 0:1], accum_out=dsum[:, 0:1])
                act.drain()
                act.sem_inc(dp_ready, 1)

            for q in range(NQ):
                take_pages(0, q)
            with act.Fori(1, NS) as b:
                take_pages(b, 0)
                take_pages(b, 1)
                exp_scores(b - 1)
                take_pages(b, 2)
                take_pages(b, 3)
            exp_scores(NS - 1)
            act.wait_ge(os_ready, 1)
            for c in range(2):
                ins = act.activation(o_all[0:NS, 2, 512 * c:512 * c + 512], bank[c][0:NS, :], ACT.Copy)
            ins.then_inc(x_ready, 1)

        def rotate(dve, v, nt, t, heads):
            cos = bc(cst[0:nt, C_ROPE + 32 * t:C_ROPE + 32 * t + 16], 1, heads)
            sin_ = bc(cst[0:nt, C_ROPE + 32 * t + 16:C_ROPE + 32 * t + 32], 1, heads)
            a, b = v[:, :, 0:16], v[:, :, 16:32]
            r = rt[0:nt]
            for m, (p_, q_) in enumerate(((a, cos), (b, sin_), (b, cos), (a, sin_))):
                dve.tensor_tensor(r[:, m, 0:heads, :], p_, q_, ALU.mult)
            dve.drain()
            dve.tensor_tensor(a, r[:, 0, 0:heads, :], r[:, 1, 0:heads, :], ALU.subtract)
            dve.tensor_tensor(b, r[:, 2, 0:heads, :], r[:, 3, 0:heads, :], ALU.add)
            dve.drain()

        def dve_mla(dve):
            dve.wait_ge(wm_in, 16 * 4)
            for t, (t0, nt) in enumerate(TILES):
                dve.wait_ge(kvq_taken, t + 1)
                dve.reciprocal(rstd[0:nt, 2 * t:2 * t + 2], std[0:nt, 2 * t:2 * t + 2])
                dve.drain()
                for s, (c0, c1, g0) in enumerate(((0, LORA, 0), (LORA + ROPE, WKVQ, LORA))):
                    dve.scalar_tensor_tensor(kvq[0:nt, t, c0:c1], kvq[0:nt, t, c0:c1], rstd[0:nt, 2 * t + s:2 * t + s + 1],
                                             gkq[0:nt, g0:g0 + c1 - c0], ALU.mult, ALU.mult)
                rotate(dve, kvq[0:nt, t, LORA:LORA + ROPE].unsqueeze(1), nt, t, 1)
                if t < 2:
                    dve.tensor_copy(kf[:, t, :, NOPE:QD], bc(kvq[:, t, LORA:LORA + ROPE], 1, HG))
                else:
                    dve.tensor_copy(ckvS[:, :], kvq[0:NS, 2, 0:LORA])
                dve.drain()
                dve.sem_inc(kvq_norm, 1)
            dve.sem_inc(po_taken, 1)
            def own_queries(g):
                dve.tensor_copy(ukst, w_ukv.rearrange("p c (h n) -> p c h n", n=128)[:, :, bass.ts(g, HG), 0:NOPE]).then_inc(ukst_ready, 1)
                after(dve, "dve", q_taken, g + 1)
                for t, (t0, nt) in enumerate(TILES):
                    rotate(dve, qs[0:nt, t, :, NOPE:QD], nt, t, HG)
                dve.sem_inc(qrot_ready, 1)

            def group(g, last):
                after(dve, "dve", kT_ready, g + 1)
                for t, b in ((0, 7), (1, 0)):
                    ins = dve.tensor_copy(kfT[:, t, :, :], bank[b][0:QD, :].rearrange("p (h s) -> p h s", h=HG))
                ins.then_inc(kT_taken, 1)
                after(dve, "dve", s_ready, g + 1)
                own = bc(causal, 1, HG)
                dve.scalar_tensor_tensor(pr[:, 0:HG, :], bank[5][:, :].rearrange("p (h s) -> p h s", h=HG), SCALE, own,
                                         ALU.mult, ALU.add)
                for a in range(2):
                    s4 = bank[6 + a][:, :].rearrange("p (h t s) -> p h t s", h=2, t=2)
                    d4 = pr[:, HG + 4 * a:HG + 4 * a + 4, :].rearrange("p (h t) s -> p h t s", h=2)
                    dve.tensor_scalar(d4[:, :, 0, :], s4[:, :, 0, :], SCALE, None, ALU.mult)
                    dve.scalar_tensor_tensor(d4[:, :, 1, :], s4[:, :, 1, :], SCALE, bc(causal, 1, 2), ALU.mult, ALU.add)
                dve.drain()
                dve.sem_inc(s_taken, 1)
                p1 = pr[:, HG:12, :].rearrange("p (h t) s -> p h (t s)", t=2)
                dve.tensor_reduce(mx[:, 0, :], pr[:, 0:HG, :], AX, ALU.max)
                dve.tensor_reduce(mx[:, 1, :], p1, AX, ALU.max)
                dve.drain()
                dve.tensor_tensor(pr[:, 0:HG, :], pr[:, 0:HG, :], bc(mx[:, 0, :], 2, P), ALU.subtract)
                dve.tensor_tensor(p1, p1, bc(mx[:, 1, :], 2, 2 * P), ALU.subtract)
                dve.drain()
                dve.sem_inc(sm_ready, 1)
                after(dve, "dve", p_ready, g + 1)
                dve.tensor_reduce(sm[:, 0, :], pr[:, 0:HG, :], AX, ALU.add)
                dve.tensor_reduce(sm[:, 1, :], p1, AX, ALU.add)
                dve.drain()
                dve.reciprocal(sm[:, :, :], sm[:, :, :])
                after(dve, "dve", pT_ready, g + 1)
                dve.tensor_copy(pT[:, 8:12, :], bank[4][:, :].rearrange("p (a s) -> p a s", a=4)).then_inc(pT_taken, 1)
                dve.drain()
                if not last:
                    own_queries(g + 1)
                after(dve, "dve", po_ready, g + 1)
                for t in range(2):
                    dve.tensor_tensor(o_all[:, t, bass.ts(g, HG * VD)].rearrange("p (h v) -> p h v", h=HG),
                                      bank[5 + t][:, 0:HG * VD].rearrange("p (h v) -> p h v", h=HG),
                                      bc(sm[:, t, :], 2, VD), ALU.mult)
                dve.drain()
                dve.sem_inc(po_taken, 1)

            own_queries(0)
            with dve.Fori(0, NG - 1) as g:
                group(g, False)
            group(NG - 1, True)
            dve.sem_inc(x_ready, 2)
            def queries(b):
                dve.tensor_copy(qst[:, 0:2, :], qlT[:, :, bass.ds(b, 1), :].rearrange("p c b h -> p c (b h)"))
                dve.tensor_copy(qst[0:ROPE, 2, :], qpT[:, bass.ds(b, 1), :].rearrange("p b h -> p (b h)"))
                dve.drain()
                dve.sem_inc(qst_ready, 1)

            dve.wait_ge(qlat_taken, NG)
            queries(0)
            dve_ln(dve, 2, (0, 1))
            route, dot, weigh, heads = dve_parts(dve, 1)
            for t in range(2):
                route(HH, t, 0, True)

            def take_scores(b, q):
                after(dve, "dve", ds_ready, NQ * b + q + 1)
                s = bank[3 + q % 2][0:MH, :]
                dve.tensor_copy(dsc[:, 512 * q:512 * q + 512], s)
                dve.tensor_reduce(dmx[:, q:q + 1], s, AX, ALU.max).then_inc(ds_taken, 1)

            def maximum(b):
                dve.memset(dsc[:, PAGES * PAGE:NKEY], NEG)
                after(dve, "dve", dn_ready, b + 1)
                dve.drain()
                dve.tensor_copy(dsc[:, bass.ds(b + PAGES * PAGE, 1)], bank[5][0:MH, bass.ds(b, 1)])
                dve.tensor_copy(dmx[:, NQ:NQ + 1], bank[5][0:MH, bass.ds(b, 1)])
                dve.drain()
                dve.tensor_reduce(dneg[:, :], dmx[:, :], AX, ALU.max)
                dve.drain()
                dve.tensor_scalar(dneg[:, :], dneg[:, :], -SCALE, None, ALU.mult)
                dve.drain()
                dve.sem_inc(dm_ready, 1)

            def take_probs(b):
                after(dve, "dve", dpT_ready, b + 1)
                dve.tensor_copy(dpT[:, 0:PAGES, :], bank[6][:, 0:PAGES * MH].rearrange("p (g h) -> p g h", g=PAGES))
                dve.tensor_copy(dpT[0:NS, PAGES, :], bank[6][0:NS, PAGES * MH:(PAGES + 1) * MH])
                dve.reciprocal(drs[:, :], dsum[:, :])
                dve.drain()
                dve.sem_inc(dpT_taken, 1)

            def normalise(b):
                after(dve, "dve", dpv_ready, b + 1)
                dve.tensor_scalar(dol, bank[7][0:MH, 0:LORA], drs[:, 0:1], None, ALU.mult).then_inc(dol_ready, 1)

            def take_out(b):
                after(dve, "dve", dolT_ready, b + 1)
                dve.tensor_copy(olT[:, :, :, bass.ds(b, 1)].rearrange("p c h b -> p c (h b)"),
                                bank[6][:, 0:2 * MH].rearrange("p (c h) -> p c h", c=2))
                dve.drain()
                dve.sem_inc(dolT_taken, 1)

            for q in range(NQ - 1):
                take_scores(0, q)
            with dve.Fori(1, NS) as b:
                take_scores(b - 1, NQ - 1)
                maximum(b - 1)
                queries(b)
                after(dve, "dve", dp_ready, b)
                take_scores(b, 0)
                take_scores(b, 1)
                take_probs(b - 1)
                normalise(b - 1)
                take_scores(b, 2)
                take_out(b - 1)
            take_scores(NS - 1, NQ - 1)
            maximum(NS - 1)
            take_probs(NS - 1)
            normalise(NS - 1)
            take_out(NS - 1)

        block = ctx.enter_context(nc.Block())

        @block.sync
        def _(sp):
            sp_hgrn(sp)
            sp_ln(sp, 0)
            sp_first(sp, 0)
            sp_peer(sp, 0)
            sp_ln(sp, 1)
            sp_mla(sp)
            sp_peer(sp, 1)
            sp_ln(sp, 3)
            for t, (t0, nt) in enumerate(TILES):
                sp.wait_ge(x_ready, 15 + t + 1)
                dst = y_prompt[0, t0:t0 + nt, :] if t < 2 else y_sample.rearrange("b t d -> (b t) d")
                sp.dma_start(dst, x[0:nt, t, :]).then_inc(stored, 16)
            sp.wait_ge(stored, 144)
            for j in range(2):
                sp.wait_ge(st_out[j], 32 * (HH // 2 + 1))

        @block.tensor
        def _(pe):
            pe_hgrn(pe)
            pe_join(pe, 0, 0)
            pe_join(pe, 0, 1)
            pe_first(pe, 0, 0)
            pe_join(pe, 0, 2)
            pe_first(pe, 0, 1)
            pe_first(pe, 0, 2)
            pe_peer(pe, 0)
            pe_mla(pe)
            pe_join(pe, 1, 2)
            pe_first(pe, 1, 2)
            pe_peer(pe, 1)

        @block.scalar
        def _(act):
            act_hgrn(act)
            act_turn(act, 1, 1)
            act_ln(act, 0, (0, 1))
            act_turn(act, 2, 0)
            act_first(act, 0, 0)
            act_turn(act, 1, 2)
            act_ln(act, 0, (2,))
            for t in (1, 2):
                act_turn(act, 2, t)
                act_first(act, 0, t)
            act_peer(act, 0)
            act_ln(act, 1)
            act_mla(act)
            act_turn(act, 4, 2)
            act_ln(act, 2, (2,))
            act_turn(act, 5, 2)
            act_first(act, 1, 2)
            act_peer(act, 1)
            act_ln(act, 3)

        @block.gpsimd
        def _(pool):
            pool.sem_inc(st_out[0], 32)
            pool.sem_inc(st_out[1], 32)
            pool_hgrn(pool)
            pool_peer(pool, 0)
            pool_mla(pool)
            pool_peer(pool, 1)

        @block.vector
        def _(dve):
            dve_hgrn(dve)
            dve_credits(dve)
            dve_ln(dve, 0, (0, 1))
            route, dot, weigh, heads = dve_parts(dve, 0)
            route(0, 0, 0, True)
            dve_ln(dve, 0, (2,))
            dot(0, 0)
            weigh(0, 0)
            route(0, 1, 0, True)
            route(0, 2, 0, True)
            heads()
            dve_ln(dve, 1)
            dve_mla(dve)
            route, dot, weigh, heads = dve_parts(dve, 1)
            dot(HH, 0)
            dve_ln(dve, 2, (2,))
            route(HH, 2, 0, True)
            weigh(HH, 0)
            heads()
            dve_ln(dve, 3)


_INS = ['x_prompt', 'x_sample', 'state_hgrn', 'cache_ckv', 'cache_kpe', 'page_table',
        'hgrn_w_in', 'hgrn_lb_logits', 'hgrn_norm_g', 'hgrn_w_out',
        'mla_w_dkv', 'mla_kv_norm_g', 'mla_w_ukv', 'mla_w_dq', 'mla_q_norm_g', 'mla_w_uq', 'mla_w_o',
        'peer_w_q', 'peer_k1', 'peer_k2', 'peer_u', 'peer_v', 'ln_g', 'ln_b']
_OUTS = [(1, 256, 1024), (8, 1, 1024), (1, 1, 8, 128, 128), (1, 8, 8, 128, 128),
         (1, 256, 256), (1, 256, 32), (8, 1, 256), (8, 1, 32)]


def kernel(**inputs):
    import numpy as _np
    import concourse.bacc as _bacc
    from concourse import mybir as _mybir
    from concourse.bass_utils import run_bass_kernel_spmd as _run

    nc = _bacc.Bacc("TRN2", target_bir_lowering=False, num_devices=1)
    c, lev = shape_constants(_np)
    arrays = {"in_consts": c, "in_levels": lev}
    for name in _INS:
        a = _np.ascontiguousarray(inputs[name])
        if name in ("peer_u", "peer_v"):
            a = a.reshape(-1, a.shape[-1])
        arrays[f"in_{name}"] = a
    args = [nc.dram_tensor(n, a.shape, _mybir.dt.from_np(a.dtype), kind="ExternalInput").ap()
            for n, a in arrays.items()]
    for i, shape in enumerate(_OUTS):
        args.append(nc.dram_tensor(f"out_{i}", shape, _mybir.dt.float32, kind="ExternalOutput").ap())
    trunk_kernel(nc, *args)
    r = _run(nc, [arrays], core_ids=[0])
    return tuple(r.results[0][f"out_{i}"] for i in range(len(_OUTS)))
```
